# Optimizing a Trainium2 kernel written in Bass

```python
import math
import jax, jax.numpy as jnp
from jax import lax
import numpy as np

D_MODEL = 1024
BATCH = 1
SEQ = 256
DEPTH = 2

CHUNK = 64
Q_BLOCK = 128
HEAD_DIM = 64
A_HEADS = 4
B_HEADS = 8
C_HEADS = 8
IDX_HEADS = 4
IDX_DIM = 64
TOPK_MAX = 256
N_BRANCHES = 3
D_FF = 4 * D_MODEL
PLE_DIM = 256
ROPE_THETA = 10000.0
EPS = 1e-6

A_QK = A_HEADS * 2 * HEAD_DIM
A_V = A_HEADS * 2 * HEAD_DIM
A_WIDTH = A_V
B_WIDTH = B_HEADS * HEAD_DIM
C_WIDTH = C_HEADS * HEAD_DIM
IN_SPLITS = (A_QK, A_QK, A_V, B_WIDTH, B_WIDTH, B_WIDTH, C_WIDTH, C_WIDTH, C_WIDTH,
             IDX_HEADS * IDX_DIM, IDX_DIM, IDX_HEADS, N_BRANCHES * D_MODEL)
W_IN_COLS = (2 * A_QK + A_V + 3 * B_WIDTH + 3 * C_WIDTH + IDX_HEADS * IDX_DIM + IDX_DIM
             + IDX_HEADS + N_BRANCHES * D_MODEL)


def rmsnorm(x, g):
    xf = x.astype(jnp.float32)
    y = xf * lax.rsqrt(jnp.mean(xf * xf, axis=-1, keepdims=True) + EPS)
    return (y * g.astype(jnp.float32)).astype(x.dtype)

def rope_tables(positions, dim):
    inv = ROPE_THETA ** (-jnp.arange(0, dim, 2, dtype=jnp.float32) / dim)
    ang = positions.astype(jnp.float32)[..., None] * inv
    return jnp.cos(ang), jnp.sin(ang)

def apply_rope(x, cos, sin):
    c = cos[:, :, None, :]
    s = sin[:, :, None, :]
    xf = x.astype(jnp.float32)
    x1, x2 = jnp.split(xf, 2, axis=-1)
    return jnp.concatenate([x1 * c - x2 * s, x2 * c + x1 * s], axis=-1).astype(x.dtype)

def sweep_query_blocks(fn, *arrays):
    b, s = arrays[0].shape[:2]
    nb = s // Q_BLOCK
    blocks = tuple(jnp.moveaxis(a.reshape((b, nb, Q_BLOCK) + a.shape[2:]), 1, 0) for a in arrays)
    out = lax.map(lambda args: fn(args[0], *args[1:]), (jnp.arange(nb), *blocks))
    return jnp.moveaxis(out, 0, 1).reshape((b, s) + out.shape[3:])

def block_positions(blk, n_keys):
    q_pos = blk * Q_BLOCK + jnp.arange(Q_BLOCK)
    k_pos = jnp.arange(n_keys)
    chunk_ok = (k_pos[None, :] // CHUNK) <= (q_pos[:, None] // CHUNK)
    return q_pos, k_pos, chunk_ok

def diff_attention(q, k, v, lam, lam_init, subln_g):
    n_keys = k.shape[1]
    scale = HEAD_DIM ** -0.5

    def block(blk, qb):
        _, _, chunk_ok = block_positions(blk, n_keys)
        s = jnp.einsum('bqhcd,bkhcd->bhcqk', qb, k).astype(jnp.float32) * scale
        s = jnp.where(chunk_ok, s, -jnp.inf)
        pr = jax.nn.softmax(s, axis=-1)
        attn = (pr[:, :, 0] - lam * pr[:, :, 1]).astype(v.dtype)
        return jnp.einsum('bhqk,bkhe->bqhe', attn, v)

    o = sweep_query_blocks(block, q)
    return rmsnorm(o, subln_g) * (1.0 - lam_init)

def stick_breaking_attention(q, k, v):
    n_keys = k.shape[1]
    scale = HEAD_DIM ** -0.5

    def block(blk, qb):
        q_pos, k_pos, _ = block_positions(blk, n_keys)
        strict = k_pos[None, :] < q_pos[:, None]
        z = jnp.einsum('bqhd,bkhd->bhqk', qb, k).astype(jnp.float32) * scale
        log_beta = jax.nn.log_sigmoid(z)
        log_one_minus = jnp.where(strict, jax.nn.log_sigmoid(-z), 0.0)
        key_axis = log_one_minus.ndim - 1
        later = lax.cumsum(log_one_minus, axis=key_axis, reverse=True) - log_one_minus
        a = jnp.where(strict, jnp.exp(log_beta + later), 0.0).astype(v.dtype)
        return jnp.einsum('bhqk,bkhd->bqhd', a, v)

    return sweep_query_blocks(block, q)

def dsa_attention(q, k, v, qi, ki, wi):
    n_keys = k.shape[1]
    topk = min(TOPK_MAX, n_keys // 4)
    scale = HEAD_DIM ** -0.5

    def block(blk, qb, qib, wib):
        q_pos, _, chunk_ok = block_positions(blk, n_keys)
        idx_s = jnp.einsum('bqhd,bkd->bqhk', qib, ki).astype(jnp.float32) * (IDX_DIM ** -0.5)
        score = jnp.einsum('bqh,bqhk->bqk', wib.astype(jnp.float32) * (IDX_HEADS ** -0.5),
                           jax.nn.relu(idx_s))
        score = jnp.where(chunk_ok, score, -jnp.inf)
        _, sel = lax.top_k(score, topk)
        ok = (sel // CHUNK) <= (q_pos[None, :, None] // CHUNK)
        kg = jax.vmap(lambda kb, ib: kb[ib])(k, sel)
        vg = jax.vmap(lambda vb, ib: vb[ib])(v, sel)
        s = jnp.einsum('bqhd,bqkhd->bhqk', qb, kg).astype(jnp.float32) * scale
        s = jnp.where(ok[:, None], s, -jnp.inf)
        pr = jax.nn.softmax(s, axis=-1).astype(v.dtype)
        return jnp.einsum('bhqk,bqkhd->bqhd', pr, vg)

    return sweep_query_blocks(block, q, qi, wi)

def first_inputs(seed: int = 0) -> dict:
    key = jax.random.key(seed)
    ks = iter(jax.random.split(key, 32))

    def dense(shape, fan_in):
        return jax.random.normal(next(ks), shape, jnp.float32) * (fan_in ** -0.5)

    def gain(shape):
        return 1.0 + 0.05 * jax.random.normal(next(ks), shape, jnp.float32)

    x = jax.random.normal(next(ks), (BATCH, SEQ, D_MODEL), jnp.float32)
    p = jax.random.normal(next(ks), (DEPTH, BATCH, SEQ, PLE_DIM), jnp.float32)
    offset = jax.random.randint(next(ks), (BATCH, 1), 0, 16, dtype=jnp.int32) * CHUNK
    positions = (offset + jnp.arange(SEQ, dtype=jnp.int32)[None, :]).astype(jnp.int32)
    return {
        "x": x,
        "p": p,
        "positions": positions,
        "attn_norm": gain((DEPTH, D_MODEL)),
        "w_in": dense((DEPTH, D_MODEL, W_IN_COLS), D_MODEL),
        "a_q_norm": gain((DEPTH, HEAD_DIM)),
        "a_k_norm": gain((DEPTH, HEAD_DIM)),
        "a_lambda": 0.1 * jax.random.normal(next(ks), (DEPTH, 4, HEAD_DIM), jnp.float32),
        "a_subln": gain((DEPTH, 2 * HEAD_DIM)),
        "c_q_norm": gain((DEPTH, HEAD_DIM)),
        "c_k_norm": gain((DEPTH, HEAD_DIM)),
        "idx_k_norm": gain((DEPTH, IDX_DIM)),
        "w_br_a": dense((DEPTH, A_WIDTH, D_MODEL), A_WIDTH),
        "w_br_b": dense((DEPTH, B_WIDTH, D_MODEL), B_WIDTH),
        "w_br_c": dense((DEPTH, C_WIDTH, D_MODEL), C_WIDTH),
        "w_out": dense((DEPTH, D_MODEL, D_MODEL), D_MODEL),
        "mlp_norm": gain((DEPTH, D_MODEL)),
        "w_up": dense((DEPTH, D_MODEL, D_FF), D_MODEL),
        "w_down": dense((DEPTH, D_FF, D_MODEL), D_FF),
        "ple_norm": gain((DEPTH, D_MODEL)),
        "w_ple_gate": dense((DEPTH, D_MODEL, D_MODEL), D_MODEL),
        "w_ple_proj": dense((DEPTH, PLE_DIM, D_MODEL), PLE_DIM),
    }

def first_block(x, p, positions, attn_norm, w_in, a_q_norm, a_k_norm, a_lambda, a_subln,
              c_q_norm, c_k_norm, idx_k_norm, w_br_a, w_br_b, w_br_c, w_out,
              mlp_norm, w_up, w_down, ple_norm, w_ple_gate, w_ple_proj):
    b, s = x.shape[:2]
    cos, sin = rope_tables(positions, HEAD_DIM)
    offsets = [int(o) for o in np.cumsum(IN_SPLITS)[:-1]]
    for i in range(DEPTH):
        lam_init = 0.8 - 0.6 * math.exp(-0.3 * i)
        h = rmsnorm(x, attn_norm[i])
        proj = h @ w_in[i]
        (aq, ak, av, bq, bk, bv, cq, ck, cv, iq, ik, iw, gl) = jnp.split(proj, offsets, axis=-1)

        aq = apply_rope(rmsnorm(aq.reshape(b, s, 2 * A_HEADS, HEAD_DIM), a_q_norm[i]), cos, sin)
        ak = apply_rope(rmsnorm(ak.reshape(b, s, 2 * A_HEADS, HEAD_DIM), a_k_norm[i]), cos, sin)
        lp = a_lambda[i].astype(jnp.float32)
        lam = jnp.exp(jnp.sum(lp[0] * lp[1])) - jnp.exp(jnp.sum(lp[2] * lp[3])) + lam_init
        y_a = diff_attention(aq.reshape(b, s, A_HEADS, 2, HEAD_DIM),
                             ak.reshape(b, s, A_HEADS, 2, HEAD_DIM),
                             av.reshape(b, s, A_HEADS, 2 * HEAD_DIM),
                             lam, lam_init, a_subln[i]).reshape(b, s, A_WIDTH)

        y_b = stick_breaking_attention(bq.reshape(b, s, B_HEADS, HEAD_DIM),
                                       bk.reshape(b, s, B_HEADS, HEAD_DIM),
                                       bv.reshape(b, s, B_HEADS, HEAD_DIM)).reshape(b, s, B_WIDTH)

        cq = apply_rope(rmsnorm(cq.reshape(b, s, C_HEADS, HEAD_DIM), c_q_norm[i]), cos, sin)
        ck = apply_rope(rmsnorm(ck.reshape(b, s, C_HEADS, HEAD_DIM), c_k_norm[i]), cos, sin)
        iq = apply_rope(iq.reshape(b, s, IDX_HEADS, IDX_DIM), cos, sin)
        ik = apply_rope(rmsnorm(ik, idx_k_norm[i])[:, :, None, :], cos, sin)[:, :, 0]
        y_c = dsa_attention(cq, ck, cv.reshape(b, s, C_HEADS, HEAD_DIM),
                            iq, ik, iw).reshape(b, s, C_WIDTH)

        gates = jax.nn.sigmoid(gl.reshape(b, s, N_BRANCHES, D_MODEL).astype(jnp.float32)).astype(x.dtype)
        merged = (gates[:, :, 0] * (y_a @ w_br_a[i])
                  + gates[:, :, 1] * (y_b @ w_br_b[i])
                  + gates[:, :, 2] * (y_c @ w_br_c[i]))
        x = x + merged @ w_out[i]

        hm = rmsnorm(x, mlp_norm[i])
        x = x + jnp.square(jax.nn.relu(hm @ w_up[i])) @ w_down[i]

        hp = rmsnorm(x, ple_norm[i])
        x = x + jax.nn.sigmoid(hp @ w_ple_gate[i]) * (p[i] @ w_ple_proj[i])
    return x


CTX_LEN = 256
GRID_W = 64
N_MOD = 9
D_FF_2 = 2816
NORM_EPS = 1e-6
RWKV_HEAD = 64
D_RWKV = 3 * D_MODEL // 4
RWKV_HEADS = D_RWKV // RWKV_HEAD
DECAY_RANK = 64
ICLR_RANK = 64
GATE_RANK = 128
DECAY_SCALE = 0.606531
GN_EPS = 64e-5
D_FOURIER = D_MODEL // 4
FOURIER_GROUPS = 4
FOURIER_GROUP = D_FOURIER // FOURIER_GROUPS
D_A_IN = 3 * D_RWKV + DECAY_RANK + ICLR_RANK + GATE_RANK
D_EVEN_IN = D_A_IN + D_FOURIER
D_MIX_EVEN = D_RWKV + D_FOURIER
D_CONV = 3 * D_MODEL // 4
CONV_WIDTH = 31
POOL_WIDTHS = (2, 4, 8, 16)
D_POOL = D_MODEL // 4
POOL_GROUP = D_POOL // len(POOL_WIDTHS)
D_ODD_IN = 2 * D_CONV + D_POOL
D_MIX_ODD = D_CONV + D_POOL


def rmsnorm_2(x, g):
    xf = x.astype(jnp.float32)
    y = xf * lax.rsqrt(jnp.mean(xf * xf, axis=-1, keepdims=True) + NORM_EPS)
    return y.astype(x.dtype) * g

def modulate(h, g, shift, scale):
    return rmsnorm_2(h, g) * (1 + scale) + shift

def swiglu(y, w_gu, w_down):
    gate, up = jnp.split(y @ w_gu, 2, axis=-1)
    return (jax.nn.silu(gate) * up) @ w_down

def half_ffn(h, m, off, g, w_gu, w_down):
    y = modulate(h, g, m[off], m[off + 1])
    return h + 0.5 * m[off + 2] * swiglu(y, w_gu, w_down)

def to_column_major(u):
    b, n = u.shape[0], u.shape[1]
    rows = n // GRID_W
    return u.reshape(b, rows, GRID_W, -1).transpose(0, 2, 1, 3).reshape(b, n, -1)

def from_column_major(u):
    b, n = u.shape[0], u.shape[1]
    rows = n // GRID_W
    return u.reshape(b, GRID_W, rows, -1).transpose(0, 2, 1, 3).reshape(b, n, -1)

def token_shift(z, mu):
    zp = jnp.pad(z, ((0, 0), (1, 1), (0, 0)))
    return z + mu * (0.5 * (zp[:, :-2] + zp[:, 2:]) - z)

def fourier_mix(u):
    b, n, _ = u.shape
    uf = u.astype(jnp.float32).reshape(b, n, FOURIER_GROUPS, FOURIER_GROUP)
    out = jnp.fft.fft2(uf, axes=(1, 3), norm='ortho').real
    return out.reshape(b, n, D_FOURIER).astype(u.dtype)

def rwkv_features(zA, w0, w_up, a0, a_up, g_up, k_k, k_a):
    b, n, _ = zA.shape
    heads = lambda u: u.reshape(b, n, RWKV_HEADS, RWKV_HEAD)
    s = [D_RWKV, 2 * D_RWKV, 3 * D_RWKV, 3 * D_RWKV + DECAY_RANK, 3 * D_RWKV + DECAY_RANK + ICLR_RANK]
    r, k, v, wd, ad, gd = jnp.split(zA, s, axis=-1)
    g = jax.nn.sigmoid(gd) @ g_up
    kk = heads(k * k_k).astype(jnp.float32)
    kk = kk / jnp.maximum(jnp.sqrt(jnp.sum(kk * kk, axis=-1, keepdims=True)), 1e-12)
    dirs = []
    for d in range(2):
        w = jnp.exp(-DECAY_SCALE * jax.nn.sigmoid(w0[d] + jnp.tanh(wd) @ w_up[d]))
        a = jax.nn.sigmoid(a0[d] + ad @ a_up[d])
        kd = k * (1 + (a - 1) * k_a)
        dirs.append((heads(w), heads(kd), kk * heads(a).astype(jnp.float32)))
    return heads(r), heads(v), kk, g, dirs

def wkv_scan(S0, r, w, k, v, kk, bb, reverse):
    tm = lambda u: jnp.moveaxis(u.astype(jnp.float32), 1, 0)
    xs = (tm(r), tm(w), tm(k), tm(v), tm(kk), tm(bb))

    def step(S, inp):
        rt, wt, kt, vt, kkt, bt = inp
        sk = jnp.einsum('bhij,bhj->bhi', S, kkt)
        S = S * wt[:, :, None, :] - sk[..., None] * bt[:, :, None, :] + vt[..., None] * kt[:, :, None, :]
        return S, jnp.einsum('bhij,bhj->bhi', S, rt)

    S, ys = lax.scan(step, S0, xs, reverse=reverse)
    return S, jnp.moveaxis(ys, 0, 1)

def rwkv_output(y, r, kds, v, g, r_k, gn_w, gn_b):
    b, n = y.shape[0], y.shape[1]
    mu = jnp.mean(y, axis=-1, keepdims=True)
    var = jnp.mean(jnp.square(y - mu), axis=-1, keepdims=True)
    yn = ((y - mu) * lax.rsqrt(var + GN_EPS)).reshape(b, n, D_RWKV) * gn_w + gn_b
    rk = r_k.reshape(RWKV_HEADS, RWKV_HEAD)
    coef = jnp.sum(r * kds[0] * rk, axis=-1, keepdims=True) + jnp.sum(r * kds[1] * rk, axis=-1, keepdims=True)
    bonus = (coef * v).reshape(b, n, D_RWKV)
    return (yn.astype(g.dtype) + bonus) * g

def even_mixer(y_ctx, y_lat, col_major, w_in, mu, w0, w_up, a0, a_up, g_up, k_k, k_a, r_k, gn_w, gn_b, w_out):
    z_ctx = y_ctx @ w_in
    z_lat = y_lat @ w_in
    f_ctx = fourier_mix(z_ctx[..., D_A_IN:])
    f_lat = fourier_mix(z_lat[..., D_A_IN:])
    zA_ctx = z_ctx[..., :D_A_IN]
    zA_lat = z_lat[..., :D_A_IN]
    if col_major:
        zA_lat = to_column_major(zA_lat)
    zA_ctx = token_shift(zA_ctx, mu)
    zA_lat = token_shift(zA_lat, mu)
    fargs = (w0, w_up, a0, a_up, g_up, k_k, k_a)
    r_c, v_c, kk_c, g_c, dirs_c = rwkv_features(zA_ctx, *fargs)
    r_l, v_l, kk_l, g_l, dirs_l = rwkv_features(zA_lat, *fargs)
    S0 = jnp.zeros((y_ctx.shape[0], RWKV_HEADS, RWKV_HEAD, RWKV_HEAD), jnp.float32)
    ys_c, ys_l = [], []
    for d in range(2):
        w_c, kd_c, b_c = dirs_c[d]
        w_l, kd_l, b_l = dirs_l[d]
        S_c, yc = wkv_scan(S0, r_c, w_c, kd_c, v_c, kk_c, b_c, reverse=(d == 1))
        _, yl = wkv_scan(S_c, r_l, w_l, kd_l, v_l, kk_l, b_l, reverse=(d == 1))
        ys_c.append(yc)
        ys_l.append(yl)
    o_ctx = rwkv_output(ys_c[0] + ys_c[1], r_c, (dirs_c[0][1], dirs_c[1][1]), v_c, g_c, r_k, gn_w, gn_b)
    o_lat = rwkv_output(ys_l[0] + ys_l[1], r_l, (dirs_l[0][1], dirs_l[1][1]), v_l, g_l, r_k, gn_w, gn_b)
    if col_major:
        o_lat = from_column_major(o_lat)
    out_ctx = jnp.concatenate([o_ctx, f_ctx], axis=-1) @ w_out
    out_lat = jnp.concatenate([o_lat, f_lat], axis=-1) @ w_out
    return out_ctx, out_lat

def centered_pool_minus_self(u, width):
    n = u.shape[1]
    uf = u.astype(jnp.float32)
    cs = jnp.pad(jnp.cumsum(uf, axis=1), ((0, 0), (1, 0), (0, 0)))
    t = jnp.arange(n)
    lo = jnp.maximum(t - width // 2, 0)
    hi = jnp.minimum(t + (width - 1 - width // 2), n - 1)
    total = jnp.take(cs, hi + 1, axis=1) - jnp.take(cs, lo, axis=1)
    mean = total / (hi - lo + 1).astype(jnp.float32)[None, :, None]
    return (mean - uf).astype(u.dtype)

def odd_mixer(y, w_in, conv_w, conv_b, cnorm_g, pool_w, pool_scale, w_out):
    b, n, _ = y.shape
    z = y @ w_in
    ga, gb, q = jnp.split(z, [D_CONV, 2 * D_CONV], axis=-1)
    u = ga * jax.nn.sigmoid(gb)
    u = lax.conv_general_dilated(u, conv_w[:, None, :], window_strides=(1,),
                                 padding=[(CONV_WIDTH // 2, CONV_WIDTH // 2)],
                                 dimension_numbers=('NWC', 'WIO', 'NWC'),
                                 feature_group_count=D_CONV) + conv_b
    u = jax.nn.silu(rmsnorm_2(u, cnorm_g))
    qg = jnp.split(q, len(POOL_WIDTHS), axis=-1)
    p = jnp.stack([centered_pool_minus_self(qi, wd) for qi, wd in zip(qg, POOL_WIDTHS)], axis=2)
    p = jnp.einsum('bngc,gcd->bngd', p, pool_w).reshape(b, n, D_POOL) * pool_scale
    return jnp.concatenate([u, p], axis=-1) @ w_out

def second_inputs(seed: int = 0) -> dict:
    key = jax.random.key(seed)
    ks = iter(jax.random.split(key, 40))
    nrm = lambda shape, scale: scale * jax.random.normal(next(ks), shape, jnp.float32)
    ne, no = (DEPTH + 1) // 2, DEPTH // 2
    D = D_MODEL
    return {
        'x': nrm((BATCH, SEQ, D), 1.0),
        'c': nrm((BATCH, D), 1.0),
        'ctx': nrm((BATCH, CTX_LEN, D), 1.0),
        'c_ctx': nrm((D,), 1.0),
        'ada_w': nrm((DEPTH, D, N_MOD * D), 0.5 * D ** -0.5),
        'ada_b': nrm((DEPTH, N_MOD * D), 0.02),
        'norm_g': 1.0 + nrm((DEPTH, 3, D), 0.05),
        'ffn1_w_gu': nrm((DEPTH, D, 2 * D_FF_2), D ** -0.5),
        'ffn1_w_down': nrm((DEPTH, D_FF_2, D), D_FF_2 ** -0.5),
        'ffn2_w_gu': nrm((DEPTH, D, 2 * D_FF_2), D ** -0.5),
        'ffn2_w_down': nrm((DEPTH, D_FF_2, D), D_FF_2 ** -0.5),
        'e_w_in': nrm((ne, D, D_EVEN_IN), D ** -0.5),
        'e_mu': jax.random.uniform(next(ks), (ne, D_A_IN), jnp.float32),
        'e_w0': -1.0 + nrm((ne, 2, D_RWKV), 0.5),
        'e_w_up': nrm((ne, 2, DECAY_RANK, D_RWKV), DECAY_RANK ** -0.5),
        'e_a0': nrm((ne, 2, D_RWKV), 0.5),
        'e_a_up': nrm((ne, 2, ICLR_RANK, D_RWKV), ICLR_RANK ** -0.5),
        'e_g_up': nrm((ne, GATE_RANK, D_RWKV), GATE_RANK ** -0.5),
        'e_k_k': 1.0 + nrm((ne, D_RWKV), 0.1),
        'e_k_a': 1.0 + nrm((ne, D_RWKV), 0.1),
        'e_r_k': nrm((ne, D_RWKV), 0.1),
        'e_gn_w': 1.0 + nrm((ne, D_RWKV), 0.05),
        'e_gn_b': nrm((ne, D_RWKV), 0.02),
        'e_w_out': nrm((ne, D_MIX_EVEN, D), D_MIX_EVEN ** -0.5),
        'o_w_in': nrm((no, D, D_ODD_IN), D ** -0.5),
        'o_conv_w': nrm((no, CONV_WIDTH, D_CONV), CONV_WIDTH ** -0.5),
        'o_conv_b': nrm((no, D_CONV), 0.02),
        'o_cnorm_g': 1.0 + nrm((no, D_CONV), 0.05),
        'o_pool_w': nrm((no, len(POOL_WIDTHS), POOL_GROUP, POOL_GROUP), POOL_GROUP ** -0.5),
        'o_pool_scale': 1.0 + nrm((no, D_POOL), 0.1),
        'o_w_out': nrm((no, D_MIX_ODD, D), D_MIX_ODD ** -0.5),
        'final_g': 1.0 + nrm((D,), 0.05),
    }

def second_block(x, c, ctx, c_ctx, ada_w, ada_b, norm_g, ffn1_w_gu, ffn1_w_down, ffn2_w_gu, ffn2_w_down,
              e_w_in, e_mu, e_w0, e_w_up, e_a0, e_a_up, e_g_up, e_k_k, e_k_a, e_r_k, e_gn_w, e_gn_b, e_w_out,
              o_w_in, o_conv_w, o_conv_b, o_cnorm_g, o_pool_w, o_pool_scale, o_w_out, final_g):
    h_lat, h_ctx = x, ctx
    for i in range(DEPTH):
        j = i // 2
        with_ctx = not (i == DEPTH - 1 and i % 2 == 1)
        m_lat = jnp.split((jax.nn.silu(c) @ ada_w[i] + ada_b[i])[:, None, :], N_MOD, axis=-1)
        if with_ctx:
            m_ctx = jnp.split((jax.nn.silu(c_ctx) @ ada_w[i] + ada_b[i])[None, None, :], N_MOD, axis=-1)
            h_ctx = half_ffn(h_ctx, m_ctx, 0, norm_g[i, 0], ffn1_w_gu[i], ffn1_w_down[i])
        h_lat = half_ffn(h_lat, m_lat, 0, norm_g[i, 0], ffn1_w_gu[i], ffn1_w_down[i])
        y_lat = modulate(h_lat, norm_g[i, 1], m_lat[3], m_lat[4])
        if i % 2 == 0:
            y_ctx = modulate(h_ctx, norm_g[i, 1], m_ctx[3], m_ctx[4])
            o_ctx, o_lat = even_mixer(y_ctx, y_lat, j % 2 == 1, e_w_in[j], e_mu[j], e_w0[j], e_w_up[j],
                                      e_a0[j], e_a_up[j], e_g_up[j], e_k_k[j], e_k_a[j], e_r_k[j],
                                      e_gn_w[j], e_gn_b[j], e_w_out[j])
            h_ctx = h_ctx + m_ctx[5] * o_ctx
            h_lat = h_lat + m_lat[5] * o_lat
        else:
            odd_args = (o_w_in[j], o_conv_w[j], o_conv_b[j], o_cnorm_g[j], o_pool_w[j], o_pool_scale[j], o_w_out[j])
            h_lat = h_lat + m_lat[5] * odd_mixer(y_lat, *odd_args)
            if with_ctx:
                y_ctx = modulate(h_ctx, norm_g[i, 1], m_ctx[3], m_ctx[4])
                h_ctx = h_ctx + m_ctx[5] * odd_mixer(y_ctx, *odd_args)
        if with_ctx:
            h_ctx = half_ffn(h_ctx, m_ctx, 6, norm_g[i, 2], ffn2_w_gu[i], ffn2_w_down[i])
        h_lat = half_ffn(h_lat, m_lat, 6, norm_g[i, 2], ffn2_w_gu[i], ffn2_w_down[i])
    return rmsnorm_2(h_lat, final_g)


def setup_inputs(seed=0):
    out = dict(first_inputs(seed))
    for name, value in second_inputs(seed + 1).items():
        if name != "x":
            out[name + "_2"] = value
    return out


def reference(
    x, p, positions, attn_norm, w_in, a_q_norm, a_k_norm, a_lambda, a_subln, c_q_norm, c_k_norm,
    idx_k_norm, w_br_a, w_br_b, w_br_c, w_out, mlp_norm, w_up, w_down, ple_norm, w_ple_gate,
    w_ple_proj, c_2, ctx_2, c_ctx_2, ada_w_2, ada_b_2, norm_g_2, ffn1_w_gu_2, ffn1_w_down_2,
    ffn2_w_gu_2, ffn2_w_down_2, e_w_in_2, e_mu_2, e_w0_2, e_w_up_2, e_a0_2, e_a_up_2, e_g_up_2,
    e_k_k_2, e_k_a_2, e_r_k_2, e_gn_w_2, e_gn_b_2, e_w_out_2, o_w_in_2, o_conv_w_2, o_conv_b_2,
    o_cnorm_g_2, o_pool_w_2, o_pool_scale_2, o_w_out_2, final_g_2,
):
    x = first_block(
        x, p, positions, attn_norm, w_in, a_q_norm, a_k_norm, a_lambda, a_subln, c_q_norm,
        c_k_norm, idx_k_norm, w_br_a, w_br_b, w_br_c, w_out, mlp_norm, w_up, w_down, ple_norm,
        w_ple_gate, w_ple_proj,
    )
    return second_block(
        x, c_2, ctx_2, c_ctx_2, ada_w_2, ada_b_2, norm_g_2, ffn1_w_gu_2, ffn1_w_down_2,
        ffn2_w_gu_2, ffn2_w_down_2, e_w_in_2, e_mu_2, e_w0_2, e_w_up_2, e_a0_2, e_a_up_2,
        e_g_up_2, e_k_k_2, e_k_a_2, e_r_k_2, e_gn_w_2, e_gn_b_2, e_w_out_2, o_w_in_2,
        o_conv_w_2, o_conv_b_2, o_cnorm_g_2, o_pool_w_2, o_pool_scale_2, o_w_out_2, final_g_2,
    )


_drawn_inputs = setup_inputs


def setup_inputs(seed=0):
    import zlib

    import numpy as np

    out = dict(_drawn_inputs(seed))
    spreads = {}
    factors = {'c_q_norm': 8.0,
     'c_k_norm': 7.914,
     'idx_k_norm': 2.846,
     'ple_norm': 6.52,
     'ctx_2': 8.0,
     'c_ctx_2': 8.0,
     'ada_b_2': 4.86,
     'norm_g_2': 5.213,
     'e_w0_2': 3.122,
     'e_w_up_2': 4.432,
     'e_a0_2': 4.4,
     'e_k_k_2': 60.04,
     'e_k_a_2': 3.713,
     'e_gn_w_2': 182.437,
     'e_gn_b_2': 200.0,
     'o_conv_b_2': 64.0,
     'o_cnorm_g_2': 181.827,
     'o_pool_scale_2': 21.963}
    for name, (base, spread) in spreads.items():
        noise = np.random.default_rng([zlib.crc32(name.encode()), seed]).standard_normal(out[name].shape)
        drawn = base * np.exp(spread * noise) if base else spread * noise
        out[name] = __import__('jax').numpy.asarray(drawn.astype(out[name].dtype))
    for name, factor in factors.items():
        out[name] = (out[name] * factor).astype(out[name].dtype)
    return out
```

```python
import math
from contextlib import ExitStack

import concourse.bass as bass
from concourse import mybir

F32 = mybir.dt.float32
I32 = mybir.dt.int32
ALU = mybir.AluOpType
ACT = mybir.ActivationFunctionType
AX_X = mybir.AxisListType.X

P = 128
D = 1024
DC = D // P
T = 256
TT = T // P
DEPTH = 2
HD = 64
CHUNK = 64
D_FF = 4 * D
D_FF_2 = 2816
N_MOD = 9
D_RWKV = 768
RC = D_RWKV // P
EPS = 1e-6
GN_EPS = 64e-5
DECAY_SCALE = 0.606531
TOPK = 64
CONV_WIDTH = 31
FAR = -1e30
TAKEN = -3e38
SLOTS = 3
SLOT = 4096
BANKS = 8
BANK = 512
WORK = 27600
LAM_INIT = [0.8 - 0.6 * math.exp(-0.3 * i) for i in range(DEPTH)]
STOP = False


class Counted:

    def __init__(self, handle):
        self.sem = handle
        self.base = 0

    def at(self, n):
        return self.base + n

    def passed(self, n):
        self.base += n


class Chain:

    def __init__(self, eng, counted):
        self.eng, self.counted = eng, counted

    def __call__(self, ins):
        self.counted.base += 1
        ins.then_inc(self.counted.sem, 1)
        self.eng.wait_ge(self.counted.sem, self.counted.base)


class Core:

    def __init__(self, nc, ctx, inputs, consts):
        self.nc, self.ctx, self.inp, self.con = nc, ctx, inputs, consts
        sb = self.sb
        self.x = sb("x", [P, DC, 2 * T])
        self.h = sb("h", [P, DC, 2 * T])
        self.ring = sb("ring", [P, SLOTS, SLOT])
        self.work = sb("work", [P, WORK])
        self.ps = ctx.enter_context(nc.psum_tensor("ps", [P, BANKS, BANK], F32))
        self.ident = sb("ident", [P, P])
        self.ones = sb("ones", [P, P])
        self.head_ones = sb("head_ones", [P, P])
        self.rstd = sb("rstd", [P, 2 * T])
        self.cond = sb("cond", [P, DC, 2])
        self.mod = sb("mod", [P, N_MOD * DC, 2])
        self.gs = sb("gs", [P, 3, DC, 2])
        self.half = sb("half", [P, 2, DC, 2])
        self.w_full = [self.counted(f"weights_arrived_{s}") for s in range(SLOTS)]
        self.w_used = self.counted("weights_used")
        self.tile_done = self.counted("tile_done")
        self.act_done = self.counted("act_done")
        self.dve_done = self.counted("dve_done")
        self.pool_done = self.counted("pool_done")
        self.pe_done = self.counted("pe_done")
        self.loaded = self.counted("loaded")
        self.stored = self.counted("stored")
        self.act_chain = self.counted("act_chain")
        self.dve_chain = self.counted("dve_chain")
        self.pool_chain = self.counted("pool_chain")
        self.slabs, self.slab_count = [], []
        self.issued = self.taken = 0
        self.used = {}

    def sb(self, name, shape, dt=F32):
        return self.ctx.enter_context(self.nc.sbuf_tensor(name, shape, dt))

    def counted(self, name):
        return Counted(self.ctx.enter_context(self.nc.semaphore(name)))

    def block(self):
        return self.nc.Block(no_gpsimd_drain=True)

    def carve(self, at, *shape):
        n = 1
        for s in shape:
            n *= s
        assert at + n <= WORK, (at, shape)
        v = self.work[:, at:at + n]
        if len(shape) == 2:
            v = v.rearrange("p (a b) -> p a b", a=shape[0])
        if len(shape) == 3:
            v = v.rearrange("p (a b c) -> p a b c", a=shape[0], b=shape[1])
        return v, at + n

    def plan(self, parts):
        kt = parts[0].shape[1]
        cols = sum(a.shape[2] for a in parts)
        assert kt * cols <= SLOT
        slot = len(self.slabs) % SLOTS
        before = self.slab_count[-SLOTS] if len(self.slabs) >= SLOTS else 0
        self.slabs.append((parts, kt, cols))
        self.slab_count.append(before + 16 * len(parts))

    def slab_view(self, j):
        _, kt, cols = self.slabs[j]
        return self.ring[:, j % SLOTS, 0:kt * cols].rearrange("p (k c) -> p k c", k=kt)

    def feed(self, sp):
        end = min(self.taken + SLOTS, len(self.slabs))
        while self.issued < end:
            j = self.issued
            if j >= SLOTS:
                sp.wait_ge(*self.used[j - SLOTS])
            c = 0
            for a in self.slabs[j][0]:
                sp.dma_start(self.slab_view(j)[:, :, c:c + a.shape[2]], a).then_inc(
                    self.w_full[j % SLOTS].sem, 16)
                c += a.shape[2]
            self.issued += 1

    def take(self, pe):
        j = self.taken
        pe.wait_ge(self.w_full[j % SLOTS].sem, self.slab_count[j])
        self.taken += 1
        return self.slab_view(j)

    def spent(self, by, count):
        self.used[self.taken - 1] = (by.sem, count)


def gemm(k, groups, rhs, n, act=None, dve=None, first_tile=0):
    tiles = []
    for g in groups:
        tiles.append(g[1] // P)
    last = k.dve_done if dve else k.act_done
    with k.block() as block:
        @block.tensor
        def _(pe):
            m0 = 0
            for (slabs, cols), nt in zip(groups, tiles):
                kt0 = 0
                for s in range(slabs):
                    w = k.take(pe)
                    kts = w.shape[1]
                    for m in range(nt):
                        bank = (m0 + m) % BANKS
                        if s == 0 and m0 + m >= BANKS:
                            pe.wait_ge(last.sem, last.at(m0 + m - BANKS + 1))
                        for kt in range(kts):
                            mm = pe.matmul(k.ps[:, bank, 0:n], w[:, kt, m * P:(m + 1) * P],
                                           rhs(kt0 + kt), start=(s == 0 and kt == 0),
                                           stop=(s == slabs - 1 and kt == kts - 1))
                        if s == slabs - 1:
                            mm.then_inc(k.tile_done.sem, 1)
                    if s == slabs - 1:
                        k.spent(k.tile_done, k.tile_done.at(m0 + nt))
                    else:
                        mm.then_inc(k.w_used.sem, 1)
                        k.w_used.passed(1)
                        k.spent(k.w_used, k.w_used.base)
                    kt0 += kts
                m0 += nt

        if act:
            @block.scalar
            def _(eng):
                chain = Chain(eng, k.act_chain)
                for m in range(sum(tiles)):
                    eng.wait_ge(k.tile_done.sem, k.tile_done.at(m + 1))
                    act(eng, chain, first_tile + m, k.ps[:, m % BANKS, 0:n]).then_inc(k.act_done.sem, 1)

        if dve:
            @block.vector
            def _(eng):
                chain = Chain(eng, k.dve_chain)
                for m in range(sum(tiles)):
                    eng.wait_ge(k.tile_done.sem, k.tile_done.at(m + 1))
                    if act:
                        eng.wait_ge(k.act_done.sem, k.act_done.at(m + 1))
                    dve(eng, chain, first_tile + m, k.ps[:, m % BANKS, 0:n]).then_inc(k.dve_done.sem, 1)

        @block.sync
        def _(sp):
            k.feed(sp)
    k.tile_done.passed(sum(tiles))
    if act:
        k.act_done.passed(sum(tiles))
    if dve:
        k.dve_done.passed(sum(tiles))


def gemm_tokens(k, outs):
    with k.block() as block:
        @block.tensor
        def _(pe):
            for i in range(len(outs)):
                w = k.take(pe)
                cols = w.shape[2]
                for tt in range(TT):
                    u = i * TT + tt
                    if u >= BANKS:
                        pe.wait_ge(k.act_done.sem, k.act_done.at(u - BANKS + 1))
                    for c in range(DC):
                        mm = pe.matmul(k.ps[:, u % BANKS, 0:cols], k.h[:, c, tt * P:(tt + 1) * P],
                                       w[:, c, :], start=(c == 0), stop=(c == DC - 1))
                    mm.then_inc(k.tile_done.sem, 1)
                k.spent(k.tile_done, k.tile_done.at(TT * (i + 1)))

        @block.scalar
        def _(act):
            for i, out in enumerate(outs):
                for tt in range(TT):
                    u = i * TT + tt
                    act.wait_ge(k.tile_done.sem, k.tile_done.at(u + 1))
                    act.activation(out[:, tt, :], k.ps[:, u % BANKS, 0:out.shape[2]], ACT.Copy).then_inc(
                        k.act_done.sem, 1)

        @block.sync
        def _(sp):
            k.feed(sp)
    k.tile_done.passed(TT * len(outs))
    k.act_done.passed(TT * len(outs))


def rmsnorm(k, src, dst, tiles, n, gain, shift=None, width=None, eps=EPS):
    width = width or tiles * P
    with k.block() as block:
        @block.scalar
        def _(act):
            for c in range(tiles):
                act.activation(dst[:, c, 0:n], src[:, c, 0:n], ACT.Square).then_inc(k.act_done.sem, 1)
            act.wait_ge(k.dve_done.sem, k.dve_done.at(1))
            act.activation(k.rstd[:, 0:n], k.rstd[:, 0:n], ACT.Sqrt).then_inc(k.act_done.sem, 1)
            if shift:
                for c in range(tiles):
                    act.wait_ge(k.dve_done.sem, k.dve_done.at(2 + c))
                    for col, (a, b) in shift(c):
                        act.activation(dst[:, c, a:b], dst[:, c, a:b], ACT.Identity, bias=col)

        @block.tensor
        def _(pe):
            for c in range(tiles):
                pe.wait_ge(k.act_done.sem, k.act_done.at(c + 1))
                mm = pe.matmul(k.ps[:, 0, 0:n], k.ones[:, :], dst[:, c, 0:n],
                               start=(c == 0), stop=(c == tiles - 1))
            mm.then_inc(k.pe_done.sem, 1)

        @block.vector
        def _(dve):
            chain = Chain(dve, k.dve_chain)
            dve.wait_ge(k.pe_done.sem, k.pe_done.at(1))
            chain(dve.tensor_scalar(k.rstd[:, 0:n], k.ps[:, 0, 0:n], 1.0 / width, eps, ALU.mult, ALU.add))
            dve.reciprocal(k.rstd[:, 0:n], k.rstd[:, 0:n]).then_inc(k.dve_done.sem, 1)
            dve.wait_ge(k.act_done.sem, k.act_done.at(tiles + 1))
            for c in range(tiles):
                for col, (a, b) in gain(c):
                    ins = dve.scalar_tensor_tensor(out=dst[:, c, a:b], in0=src[:, c, a:b], scalar=col,
                                                   in1=k.rstd[:, a:b], op0=ALU.mult, op1=ALU.mult)
                ins.then_inc(k.dve_done.sem, 1)
    k.act_done.passed(tiles + 1)
    k.pe_done.passed(1)
    k.dve_done.passed(1 + tiles)


def load_params(k):
    i = k.inp
    rows = []
    for name in ("attn_norm", "mlp_norm", "ple_norm", "norm_g_2", "a_subln", "c_2", "c_ctx_2", "ada_b_2",
                 "e_mu_2", "e_w0_2", "e_a0_2", "e_k_k_2", "e_k_a_2", "e_r_k_2", "e_gn_w_2", "e_gn_b_2",
                 "o_conv_b_2", "o_cnorm_g_2", "o_pool_scale_2", "final_g_2"):
        a = i[name]
        while len(a.shape) > 1:
            a = a.rearrange("a b c -> (a b) c") if len(a.shape) == 3 else a.rearrange("a b -> (a b)")
        rows.append((name, a.rearrange("(r c) -> r c", c=P)))
    total = sum(a.shape[0] for _, a in rows)
    nb = (total + P - 1) // P
    k.params = k.sb("params", [P, total])
    stage, end = k.carve(0, nb, P)
    k.col = {}
    at, jobs = 0, []
    for name, a in rows:
        n = a.shape[0]
        k.col[name] = at
        done = 0
        while done < n:
            m = min(n - done, P - (at + done) % P)
            jobs.append((stage[(at + done) % P:(at + done) % P + m, (at + done) // P, :], a[done:done + m, :]))
            done += m
        at += n
    conv, end = k.carve(end, 2 * RC // 2, P)
    k.conv_w = k.sb("conv_w", [P, RC, CONV_WIDTH])
    small = [(k.ident[:, :], k.con["ident"]), (k.ones[:, :], k.con["ones"]),
             (k.head_ones[:, :], k.con["head_ones"])]
    for c in range(RC):
        jobs.append((conv[0:CONV_WIDTH, c, :], i["o_conv_w_2"][0, :, c * P:(c + 1) * P]))
    k.consts1, k.consts2 = {}, {}
    names1 = ("mask_a", "mask_strict", "mask_b", "neg_tri", "neg_ones", "inv_freq")
    for name in names1:
        a = k.con[name]
        k.consts1[name] = k.sb(name, list(a.shape))
        small.append((k.consts1[name][:], a))
    k.posi = k.sb("posi", [P, TT], I32)
    k.hgain = k.sb("hgain", [P, DEPTH, 5, HD])
    for l in range(DEPTH):
        for j, name in enumerate(("a_q_norm", "a_k_norm", "c_q_norm", "c_k_norm", "idx_k_norm")):
            small.append((k.hgain[:, l, j, :], i[name][l, :].partition_broadcast(P)))
    k.lam_in = k.sb("lam_in", [P, DEPTH, 4 * HD])
    for l in range(DEPTH):
        small.append((k.lam_in[:, l, :], i["a_lambda"][l].rearrange("a b -> (a b)").partition_broadcast(P)))
    k.lam = k.sb("lam", [P, DEPTH, 4])
    k.sincos = k.sb("sincos", [P, 2, TT, HD // 2])
    ang, end = k.carve(end, 2 * TT, HD // 2)
    turns, end = k.carve(end, 2 * TT, HD // 2)
    posf, end = k.carve(end, TT)
    prod, end = k.carve(end, 2, HD)
    tok, end = k.carve(end, 2 * TT, D)
    n_load = len(jobs) + len(small) + 3
    ncopy = nb + RC
    with k.block() as block:
        @block.sync
        def _(sp):
            for dst, src in small[0:1] + jobs:
                sp.dma_start(dst, src).then_inc(k.loaded.sem, 16)
            sp.dma_start(tok[:, 0:TT, :], i["x"].rearrange("a (t p) d -> p (a t) d", p=P)).then_inc(k.loaded.sem, 16)
            sp.dma_start(tok[:, TT:2 * TT, :], i["ctx_2"].rearrange("a (t p) d -> p (a t) d", p=P)).then_inc(k.loaded.sem, 16)
            sp.dma_start(k.posi[:, :], i["positions"].rearrange("a (t p) -> p (a t)", p=P),
                         allow_slow_non_contiguous=True).then_inc(k.loaded.sem, 16)
            for dst, src in small[1:]:
                sp.dma_start(dst, src).then_inc(k.loaded.sem, 16)
            k.feed(sp)

        @block.tensor
        def _(pe):
            pe.wait_ge(k.loaded.sem, 16 * n_load)
            n_rows = [min(P, total - b * P) for b in range(nb)]
            for b in range(nb):
                mm = pe.transpose(k.ps[:, b % BANKS, 0:n_rows[b]], stage[0:n_rows[b], b, :],
                                  k.ident[0:n_rows[b], 0:n_rows[b]])
            assert nb < BANKS
            for c in range(RC):
                mm = pe.transpose(k.ps[:, nb, c * 32:c * 32 + CONV_WIDTH], conv[0:CONV_WIDTH, c, :],
                                  k.ident[0:CONV_WIDTH, 0:CONV_WIDTH])
            mm.then_inc(k.pe_done.sem, 1)
            for c in range(DC):
                if c == 0:
                    pe.wait_ge(k.dve_done.sem, k.dve_done.at(1))
                for tt in range(2 * TT):
                    mm = pe.transpose(k.ps[:, c, tt * P:(tt + 1) * P], tok[:, tt, c * P:(c + 1) * P],
                                      k.ident[:, :])
                mm.then_inc(k.pe_done.sem, 1)

        @block.vector
        def _(dve):
            chain = Chain(dve, k.dve_chain)
            dve.wait_ge(k.pe_done.sem, k.pe_done.at(1))
            for b in range(nb):
                w = min(P, total - b * P)
                dve.tensor_copy(k.params[:, b * P:b * P + w], k.ps[:, b, 0:w])
            dve.tensor_copy(k.conv_w[:, :, :], k.ps[:, nb, 0:RC * 32].rearrange("p (c w) -> p c w", c=RC)[:, :, 0:CONV_WIDTH]).then_inc(
                k.dve_done.sem, 1)
            for c in range(DC):
                dve.wait_ge(k.pe_done.sem, k.pe_done.at(c + 2))
                dve.tensor_copy(k.x[:, c, :], k.ps[:, c, :])
            dve.wait_ge(k.loaded.sem, 16 * n_load)
            chain(dve.tensor_copy(posf[:, :], k.posi[:, :]))
            inv = k.consts1["inv_freq"]
            for tt in range(TT):
                dve.tensor_scalar(ang[:, tt, :], inv[:, :], posf[:, tt:tt + 1], None, ALU.mult)
                ins = dve.tensor_scalar(ang[:, TT + tt, :], inv[:, :], posf[:, tt:tt + 1], None, ALU.mult)
            chain(ins)
            a, t = ang[:, :, :], turns[:, :, :]
            big = 1.5 * 2 ** 23
            chain(dve.tensor_scalar(turns[:, 0:TT, :], ang[:, 0:TT, :], 0.15915494309189535, None, ALU.mult))
            chain(dve.tensor_scalar(turns[:, TT:2 * TT, :], ang[:, TT:2 * TT, :], 0.15915494309189535, 0.25, ALU.mult, ALU.add))
            chain(dve.tensor_scalar(t, t, big, None, ALU.add))
            chain(dve.tensor_scalar(t, t, big, None, ALU.subtract))
            for part in (6.28125, 0.0019350051879882812, 3.0199157663446e-07):
                chain(dve.scalar_tensor_tensor(out=a, in0=t, scalar=-part, in1=a, op0=ALU.mult, op1=ALU.add))
            chain(dve.tensor_scalar(ang[:, TT:2 * TT, :], ang[:, TT:2 * TT, :], 1.5707963267948966, None, ALU.add))
            chain(dve.tensor_scalar(a, a, 3.1415925, -3.1415925, ALU.min, ALU.max))
            dve.tensor_copy(a, a).then_inc(k.dve_done.sem, 1)
            for l in range(DEPTH):
                li = k.lam_in[:, l, :].rearrange("p (a b c) -> p a b c", a=2, b=2)
                chain(dve.tensor_tensor(prod[:, :, :], li[:, :, 0, :], li[:, :, 1, :], ALU.mult))
                chain(dve.tensor_reduce(k.lam[:, l, 0:2], prod[:, :, :], AX_X, ALU.add))
            dve.tensor_copy(k.lam[:, :, 2:4], k.lam[:, :, 0:2]).then_inc(k.dve_done.sem, 1)
            dve.wait_ge(k.act_done.sem, k.act_done.at(2))
            for l in range(DEPTH):
                chain(dve.tensor_tensor(k.lam[:, l, 0:1], k.lam[:, l, 3:4], k.lam[:, l, 2:3], ALU.subtract))
                chain(dve.tensor_scalar(k.lam[:, l, 1:2], k.lam[:, l, 0:1], -LAM_INIT[l], None, ALU.add))
            assert k.dve_done.base >= 0

        @block.scalar
        def _(act):
            act.wait_ge(k.dve_done.sem, k.dve_done.at(2))
            act.activation(k.sincos[:, :, :, :].rearrange("p a t f -> p (a t) f"), ang[:, :, :], ACT.Sin).then_inc(k.act_done.sem, 1)
            act.wait_ge(k.dve_done.sem, k.dve_done.at(3))
            act.activation(k.lam[:, :, 2:4], k.lam[:, :, 2:4], ACT.Exp).then_inc(k.act_done.sem, 1)
    k.loaded.passed(16 * n_load)
    k.pe_done.passed(1 + DC)
    k.dve_done.passed(3)
    k.act_done.passed(2)


def head_norm_rope(k, heads, gain, tmp, rs):
    _, tt, nh, _ = heads.shape
    half = HD // 2

    def wide(a, tk):
        return a[:, tk, :].rearrange("p (h o) -> p h o", o=1).broadcast_to([P, nh, HD])

    def angle(s):
        return [k.sincos[:, s, t, :].rearrange("p (o f) -> p o f", o=1).broadcast_to([P, nh, half]) for t in range(TT)]

    with k.block() as block:
        if gain is not None:
            @block.scalar
            def _(act):
                for t in range(TT):
                    act.activation(tmp[:, t], heads[:, t], ACT.Square).then_inc(k.act_done.sem, 1)
                act.wait_ge(k.dve_done.sem, k.dve_done.at(1))
                act.activation(rs, rs, ACT.Sqrt).then_inc(k.act_done.sem, 1)

        @block.vector
        def _(dve):
            chain = Chain(dve, k.dve_chain)
            if gain is not None:
                for t in range(TT):
                    dve.wait_ge(k.act_done.sem, k.act_done.at(t + 1))
                    ins = dve.tensor_reduce(rs[:, t, :], tmp[:, t], AX_X, ALU.add)
                chain(ins)
                chain(dve.tensor_scalar(rs, rs, 1.0 / HD, EPS, ALU.mult, ALU.add))
                dve.reciprocal(rs, rs).then_inc(k.dve_done.sem, 1)
                dve.wait_ge(k.act_done.sem, k.act_done.at(TT + 1))
                for t in range(TT):
                    ins = dve.tensor_tensor(heads[:, t], heads[:, t], wide(rs, t), ALU.mult)
                chain(ins)
                g = gain.rearrange("p (o f) -> p o f", o=1).broadcast_to([P, nh, HD])
                for t in range(TT):
                    ins = dve.tensor_tensor(heads[:, t], heads[:, t], g, ALU.mult)
                chain(ins)
            sin, cos = angle(0), angle(1)
            for t in range(TT):
                x1, x2 = heads[:, t, :, 0:half], heads[:, t, :, half:HD]
                t1, t2 = tmp[:, t, :, 0:half], tmp[:, t, :, half:HD]
                dve.tensor_tensor(t1, x2, sin[t], ALU.mult)
                chain(dve.tensor_tensor(t2, x1, sin[t], ALU.mult))
                dve.tensor_tensor(x1, x1, cos[t], ALU.mult)
                chain(dve.tensor_tensor(x2, x2, cos[t], ALU.mult))
                dve.tensor_tensor(x1, x1, t1, ALU.subtract)
                ins = dve.tensor_tensor(x2, x2, t2, ALU.add)
            chain(ins)
    if gain is not None:
        k.act_done.passed(TT + 1)
        k.dve_done.passed(1)


def turn(k, jobs):
    tiles = []
    for src, out, scale in jobs:
        for f in range(out.shape[1]):
            tiles.append((src, out, scale, f))
    with k.block() as block:
        @block.tensor
        def _(pe):
            for u, (src, out, scale, f) in enumerate(tiles):
                if u >= BANKS:
                    pe.wait_ge(k.act_done.sem, k.act_done.at(u - BANKS + 1))
                for tt in range(TT):
                    mm = pe.transpose(k.ps[:, u % BANKS, tt * P:(tt + 1) * P], src[:, tt, f * P:(f + 1) * P],
                                      k.ident[:, :])
                mm.then_inc(k.tile_done.sem, 1)

        @block.scalar
        def _(act):
            for u, (src, out, scale, f) in enumerate(tiles):
                act.wait_ge(k.tile_done.sem, k.tile_done.at(u + 1))
                act.activation(out[:, f, :], k.ps[:, u % BANKS, 0:T], ACT.Copy, scale=scale).then_inc(k.act_done.sem, 1)
    k.tile_done.passed(len(tiles))
    k.act_done.passed(len(tiles))


def softmax_scores(k, qT, kT, mask, e0, e1, sums, nmax):
    def part(n):
        if n < 8:
            return 0, n, n % 2, (n // 2) * P, P
        m = n - 8
        return 1, m, 2 + 2 * (m // 4) + m % 2, (m % 4 // 2) * T, T

    with k.block() as block:
        @block.tensor
        def _(pe):
            for n in range(16):
                qt, h, bank, off, nk = part(n)
                r = (h % 2) * HD
                mm = pe.matmul(k.ps[:, bank, off:off + nk], qT[r:r + HD, h // 2, qt * P:(qt + 1) * P],
                               kT[r:r + HD, h // 2, 0:nk], start=True, stop=True)
                if off + nk == BANK:
                    mm.then_inc(k.tile_done.sem, 1)

        @block.vector
        def _(dve):
            chain = Chain(dve, k.dve_chain)
            for b in range(6):
                dve.wait_ge(k.tile_done.sem, k.tile_done.at(b + 1))
                if b < 2:
                    e, hs, nh, nk, m = e0, slice(b, 8, 2), 4, P, mask[:, 0, 0:P]
                else:
                    h0 = 4 * ((b - 2) // 2) + b % 2
                    e, hs, nh, nk, m = e1, slice(h0, h0 + 3, 2), 2, T, mask[:, 1, :]
                m = m.rearrange("p (o f) -> p o f", o=1).broadcast_to([P, nh, nk])
                s = k.ps[:, b, :].rearrange("p (h f) -> p h f", h=nh)
                chain(dve.tensor_tensor(e[:, hs, :], s, m, ALU.add))
                qt = 0 if b < 2 else 1
                dve.tensor_reduce(nmax[:, qt, hs], e[:, hs, :], AX_X, ALU.max,
                                  negate=True).then_inc(k.dve_done.sem, 1)
            dve.wait_ge(k.act_done.sem, k.act_done.at(16))
            chain(dve.reciprocal(sums, sums))

        @block.scalar
        def _(act):
            for n in range(16):
                qt, h, bank, _, _ = part(n)
                act.wait_ge(k.dve_done.sem, k.dve_done.at(bank + 1))
                e = e0 if qt == 0 else e1
                act.activation(e[:, h, :], e[:, h, :], ACT.Exp, bias=nmax[:, qt, h:h + 1],
                               accum_out=sums[:, qt, h:h + 1]).then_inc(k.act_done.sem, 1)
    k.tile_done.passed(6)
    k.dve_done.passed(6)
    k.act_done.passed(16)


def turn_probs(k, nh, p0, p1, pT):
    n = nh * 3
    nb = n // 4
    with k.block() as block:
        @block.tensor
        def _(pe):
            for u in range(n):
                h, s = u // 3, u % 3
                src = p0[:, h, :] if s == 0 else p1[:, h, (s - 1) * P:s * P]
                mm = pe.transpose(k.ps[:, u // 4, (u % 4) * P:(u % 4 + 1) * P], src, k.ident[:, :])
                if u % 4 == 3:
                    mm.then_inc(k.tile_done.sem, 1)

        @block.scalar
        def _(act):
            flat = pT.rearrange("p h s q -> p (h s q)")
            for b in range(nb):
                act.wait_ge(k.tile_done.sem, k.tile_done.at(b + 1))
                act.activation(flat[:, b * BANK:(b + 1) * BANK], k.ps[:, b, :], ACT.Copy).then_inc(k.act_done.sem, 1)
            act.wait_ge(k.act_done.sem, k.act_done.at(nb))
    k.tile_done.passed(nb)
    k.act_done.passed(nb)


def values(k, nh, width, v, pT, out):
    per = P // width
    with k.block() as block:
        @block.tensor
        def _(pe):
            for h in range(nh):
                r = (h % per) * width
                bank = h // per
                o = k.ps[r:r + width, bank, 0:T]
                cols = slice(h * width, (h + 1) * width)
                pe.matmul(o, v[:, 0, cols], pT[:, h, 0:2, :].rearrange("p s q -> p (s q)"), start=True, stop=False)
                mm = pe.matmul(k.ps[r:r + width, bank, P:T], v[:, 1, cols], pT[:, h, 2, :], start=False, stop=True)
                if h % per == per - 1:
                    mm.then_inc(k.tile_done.sem, 1)

        @block.scalar
        def _(act):
            for b in range(nh // per):
                act.wait_ge(k.tile_done.sem, k.tile_done.at(b + 1))
                act.activation(out[:, b, :], k.ps[:, b, 0:T], ACT.Copy)
    k.tile_done.passed(nh // per)


def scale_probs(k, nh, p0, p1, rs):
    with k.block() as block:
        @block.vector
        def _(dve):
            for h in range(nh):
                dve.tensor_scalar(p0[:, h, :], p0[:, h, :], rs[:, 0, h:h + 1], None, ALU.mult)
                dve.tensor_scalar(p1[:, h, :], p1[:, h, :], rs[:, 1, h:h + 1], None, ALU.mult)


def differ_probs(k, layer, p0, p1, rs, nrs):
    with k.block() as block:
        @block.vector
        def _(dve):
            chain = Chain(dve, k.dve_chain)
            chain(dve.tensor_scalar(nrs, rs, k.lam[:, layer, 1:2], None, ALU.mult))
            for h in range(4):
                for qt, p in enumerate((p0, p1)):
                    chain(dve.tensor_scalar(p[:, 2 * h, :], p[:, 2 * h, :], rs[:, qt, 2 * h:2 * h + 1], None, ALU.mult))
                    chain(dve.scalar_tensor_tensor(out=p[:, h, :], in0=p[:, 2 * h + 1, :],
                                                   scalar=nrs[:, qt, 2 * h + 1:2 * h + 2],
                                                   in1=p[:, 2 * h, :], op0=ALU.mult, op1=ALU.add))


def subln(k, layer, y, sq):
    g = k.col["a_subln"] + layer
    with k.block() as block:
        @block.scalar
        def _(act):
            for c in range(4):
                act.activation(sq[:, c, :], y[:, c, :], ACT.Square).then_inc(k.act_done.sem, 1)
            for c in range(4):
                act.wait_ge(k.dve_done.sem, k.dve_done.at(c + 1))
                act.activation(sq[:, c, :], sq[:, c, :], ACT.Sqrt).then_inc(k.act_done.sem, 1)

        @block.tensor
        def _(pe):
            for c in range(4):
                pe.wait_ge(k.act_done.sem, k.act_done.at(c + 1))
                pe.matmul(k.ps[:, c, 0:T], k.ones[:, :], sq[:, c, :], start=True, stop=True).then_inc(k.pe_done.sem, 1)

        @block.vector
        def _(dve):
            chain = Chain(dve, k.dve_chain)
            for c in range(4):
                dve.wait_ge(k.pe_done.sem, k.pe_done.at(c + 1))
                chain(dve.tensor_scalar(sq[:, c, :], k.ps[:, c, 0:T], 1.0 / P, EPS, ALU.mult, ALU.add))
                dve.reciprocal(sq[:, c, :], sq[:, c, :]).then_inc(k.dve_done.sem, 1)
            for c in range(4):
                dve.wait_ge(k.act_done.sem, k.act_done.at(5 + c))
                chain(dve.scalar_tensor_tensor(out=y[:, c, :], in0=y[:, c, :], scalar=k.params[:, g:g + 1],
                                               in1=sq[:, c, :], op0=ALU.mult, op1=ALU.mult))
                dve.tensor_scalar(y[:, c, :], y[:, c, :], 1.0 - LAM_INIT[layer], None, ALU.mult)
    k.act_done.passed(8)
    k.pe_done.passed(4)
    k.dve_done.passed(4)


def stick_breaking(k, qT, kT, v, y, sp, at, tmp):
    NZ = T + P
    with k.block() as block:
        @block.tensor
        def _(pe):
            for h in range(8):
                r = (h % 2) * HD
                pe.matmul(k.ps[:, h, 0:T], kT[r:r + HD, h // 2, 0:P], qT[r:r + HD, h // 2, :], start=True, stop=True)
                pe.matmul(k.ps[:, h, T:NZ], kT[r:r + HD, h // 2, P:T], qT[r:r + HD, h // 2, P:T],
                          start=False, stop=True, skip_group_check=True).then_inc(k.tile_done.sem, 1)
            for h in range(8):
                pe.wait_ge(k.dve_done.sem, k.dve_done.at(h + 1))
                pe.matmul(k.ps[:, h, 0:T], k.consts1["neg_tri"][:, :], sp[:, h, 0:T], start=False, stop=True, skip_group_check=True)
                pe.matmul(k.ps[:, h, P:T], k.consts1["neg_ones"][:, :], sp[:, h, T:NZ], start=False, stop=True, skip_group_check=True)
                pe.matmul(k.ps[:, h, T:NZ], k.consts1["neg_tri"][:, :], sp[:, h, T:NZ], start=False, stop=True,
                          skip_group_check=True).then_inc(k.tile_done.sem, 1)

        @block.scalar
        def _(act):
            chain = Chain(act, k.act_chain)
            for h in range(8):
                act.wait_ge(k.tile_done.sem, k.tile_done.at(h + 1))
                if h >= 3:
                    act.wait_ge(k.dve_done.sem, k.dve_done.at(h - 2))
                chain(act.activation(tmp[:, h % 3, :], k.ps[:, h, 0:NZ], ACT.Abs))
                chain(act.activation(tmp[:, h % 3, :], tmp[:, h % 3, :], ACT.Exp, scale=-1.0))
                act.activation(tmp[:, h % 3, :], tmp[:, h % 3, :], ACT.Ln, bias=1.0).then_inc(k.act_done.sem, 1)
            for h in range(8):
                act.wait_ge(k.dve_done.sem, k.dve_done.at(9 + h))
                act.activation(at[:, h, :], at[:, h, :], ACT.Exp).then_inc(k.act_done.sem, 1)

        @block.vector
        def _(dve):
            chain = Chain(dve, k.dve_chain)
            strict = k.consts1["mask_strict"][:, :].rearrange("p (o f) -> p o f", o=1).broadcast_to([P, 2, P])
            for h in range(8):
                dve.wait_ge(k.act_done.sem, k.act_done.at(h + 1))
                chain(dve.scalar_tensor_tensor(out=sp[:, h, :], in0=k.ps[:, h, 0:NZ], scalar=0.0, in1=tmp[:, h % 3, :],
                                               op0=ALU.max, op1=ALU.add))
                diag = sp[:, h, :].rearrange("p (a f) -> p a f", a=3)[:, 0:3:2, :]
                dve.tensor_tensor(diag, diag, strict, ALU.mult).then_inc(k.dve_done.sem, 1)
            for h in range(8):
                dve.wait_ge(k.tile_done.sem, k.tile_done.at(9 + h))
                dve.tensor_tensor(at[:, h, :], k.ps[:, h, 0:NZ], k.consts1["mask_b"][:, :], ALU.add).then_inc(k.dve_done.sem, 1)
    k.tile_done.passed(16)
    k.act_done.passed(16)
    k.dve_done.passed(16)
    with k.block() as block:
        @block.tensor
        def _(pe):
            for h in range(8):
                r = (h % 2) * HD
                o = k.ps[r:r + HD, h // 2, :]
                pe.matmul(o[:, 0:T], v[:, 0, h * HD:(h + 1) * HD], at[:, h, 0:T], start=True, stop=False)
                mm = pe.matmul(o[:, P:T], v[:, 1, h * HD:(h + 1) * HD], at[:, h, T:NZ], start=False, stop=True)
                if h % 2:
                    mm.then_inc(k.tile_done.sem, 1)

        @block.scalar
        def _(act):
            for b in range(4):
                act.wait_ge(k.tile_done.sem, k.tile_done.at(b + 1))
                act.activation(y[:, b, :], k.ps[:, b, 0:T], ACT.Copy)
    k.tile_done.passed(4)


def pick_keys(k, iqT, ikT, iw, score, picked, relu, best):
    with k.block() as block:
        @block.tensor
        def _(pe):
            for n in range(8):
                qt, h = n // 4, n % 4
                r = (h % 2) * HD
                nk = P if qt == 0 else T
                bank = 2 * qt + h % 2
                off = h // 2 * nk
                mm = pe.matmul(k.ps[:, bank, off:off + nk], iqT[r:r + HD, h // 2, qt * P:(qt + 1) * P],
                               ikT[r:r + HD, 0, 0:nk], start=True, stop=True)
                if h >= 2:
                    mm.then_inc(k.tile_done.sem, 1)

        @block.scalar
        def _(act):
            for b in range(4):
                act.wait_ge(k.tile_done.sem, k.tile_done.at(b + 1))
                w = T if b < 2 else 2 * T
                act.activation(relu[:, b, 0:w], k.ps[:, b, 0:w], ACT.Relu).then_inc(k.act_done.sem, 1)

        @block.vector
        def _(dve):
            chain = Chain(dve, k.dve_chain)
            chain(dve.tensor_scalar(iw, iw, 0.5, None, ALU.mult))
            for qt, nk in ((0, P), (1, T)):
                s = score[:, qt, 0:nk]
                dve.wait_ge(k.act_done.sem, k.act_done.at(2 if qt == 0 else 4))
                for h in range(4):
                    r = relu[:, 2 * qt + h % 2, h // 2 * nk:(h // 2 + 1) * nk]
                    w = iw[:, qt, h:h + 1]
                    if h == 0:
                        chain(dve.tensor_scalar(s, r, w, None, ALU.mult))
                    else:
                        chain(dve.scalar_tensor_tensor(out=s, in0=r, scalar=w, in1=s, op0=ALU.mult, op1=ALU.add))
                chain(dve.tensor_tensor(s, s, k.consts1["mask_a"][:, qt, 0:nk], ALU.add))
                for _ in range(TOPK // 8):
                    chain(dve.max(best, s))
                    chain(dve.match_replace(s, best, s, TAKEN))
                m = picked[:, qt, 0:nk]
                chain(dve.tensor_scalar(m, s, TAKEN, 1.0, ALU.is_equal, ALU.subtract))
                dve.tensor_scalar(m, m, -FAR, None, ALU.mult)
    k.tile_done.passed(4)
    k.act_done.passed(4)


def wslab(a, r0, r1, c0, c1):
    return a[r0:r1, c0:c1].rearrange("(k p) c -> p k c", p=P)


A_Q, A_K, A_VC, B_Q, B_K, B_VC, C_Q, C_K, C_VC = (512 * j for j in range(9))
IDX_C = 9 * 512
IDX_W = 256 + HD + 4
GATE_C = IDX_C + IDX_W


def plan_first(k, l):
    w = k.inp["w_in"][l]
    for c0 in (A_Q, A_K, A_VC, B_Q, B_K, B_VC, C_Q, C_K, C_VC):
        k.plan([wslab(w, 0, D, c0, c0 + 512)])
        if c0 == C_VC:
            k.plan([wslab(w, 0, D, IDX_C, GATE_C)])
    for j in range(6):
        k.plan([wslab(w, 0, D, GATE_C + 512 * j, GATE_C + 512 * (j + 1))])
    for name in ("w_br_a", "w_br_b", "w_br_c"):
        k.plan([wslab(k.inp[name][l], 0, 512, 0, D)])
    for j in range(2):
        k.plan([wslab(k.inp["w_out"][l], 0, D, 512 * j, 512 * (j + 1))])
    for j in range(D_FF // 512):
        k.plan([wslab(k.inp["w_up"][l], 0, D, 512 * j, 512 * (j + 1))])
    for j in range(2):
        for r in range(D_FF // D):
            k.plan([wslab(k.inp["w_down"][l], D * r, D * (r + 1), 512 * j, 512 * (j + 1))])
    for j in range(2):
        k.plan([wslab(k.inp["w_ple_gate"][l], 0, D, 512 * j, 512 * (j + 1))])
    k.plan([wslab(k.inp["w_ple_proj"][l], 0, T, 0, D)])


def column(k, name, at):
    c = k.col[name] + at
    return k.params[:, c:c + 1]


def add_to_x(k, n=T, scale=None):
    def dve(eng, chain, m, ps):
        if scale is None:
            return eng.tensor_tensor(k.x[:, m, 0:n], k.x[:, m, 0:n], ps, ALU.add)
        for col, (a, b) in scale(m):
            ins = eng.scalar_tensor_tensor(out=k.x[:, m, a:b], in0=ps[:, a:b], scalar=col, in1=k.x[:, m, a:b],
                                           op0=ALU.mult, op1=ALU.add)
        return ins
    return dve


def first_layer(k, l):
    gates, end = k.carve(0, 24, T)
    y, end = k.carve(end, 12, T)
    v0 = end
    tm, end = k.carve(end, 3 * TT, 512)
    qT, end = k.carve(end, 4, T)
    kT, end = k.carve(end, 4, T)
    free = end

    rmsnorm(k, k.x, k.h, DC, T, lambda c: [(column(k, "attn_norm", l * DC + c), (0, T))])

    def heads(j, nh=8):
        return tm[:, j * TT:(j + 1) * TT, 0:nh * HD].rearrange("p t (h f) -> p t h f", h=nh)

    def part(j):
        return tm[:, j * TT:(j + 1) * TT, :]

    for branch in range(3):
        ybr = y[:, 4 * branch:4 * branch + 4, :]
        gemm_tokens(k, [part(0), part(1), part(2)])
        tmp, _ = k.carve(free, TT, 512)
        tmp = tmp.rearrange("p t (h f) -> p t h f", h=8)
        rs, _ = k.carve(free + TT * 512, TT, 8)
        if branch != 1:
            g = 0 if branch == 0 else 2
            head_norm_rope(k, heads(0), k.hgain[:, l, g, :], tmp, rs)
            head_norm_rope(k, heads(1), k.hgain[:, l, g + 1, :], tmp, rs)
        turn(k, [(part(0), qT, HD ** -0.5), (part(1), kT, 1.0)])
        e0, end = k.carve(free, 8, P)
        e1, end = k.carve(end, 8, T)
        pT, end = k.carve(end, 8 * 3, P)
        pT = pT.rearrange("p (h s) q -> p h s q", s=3)
        sums, end = k.carve(end, 2, 8)
        nmax, end = k.carve(end, 2, 8)
        if branch == 0:
            softmax_scores(k, qT, kT, k.consts1["mask_a"], e0, e1, sums, nmax)
            differ_probs(k, l, e0, e1, sums, nmax)
            turn_probs(k, 4, e0, e1, pT[:, 0:4])
            values(k, 4, 2 * HD, part(2), pT, ybr)
            sq, _ = k.carve(free, 4, T)
            subln(k, l, ybr, sq)
        elif branch == 1:
            sp, end = k.carve(free, 8, T + P)
            at, end = k.carve(end, 8, T + P)
            tmp3, end = k.carve(end, 3, T + P)
            stick_breaking(k, qT, kT, part(2), ybr, sp, at, tmp3)
        else:
            idx = tm[:, 0:TT, 0:IDX_W]
            gemm_tokens(k, [idx])
            iq = tm[:, 0:TT, 0:256].rearrange("p t (h f) -> p t h f", h=4)
            ik = tm[:, 0:TT, 256:256 + HD].rearrange("p t (h f) -> p t h f", h=1)
            iw = tm[:, 0:TT, 256 + HD:IDX_W]
            itmp, end2 = k.carve(free, TT, 256)
            irs, end2 = k.carve(end2, TT, 1)
            head_norm_rope(k, iq, None, itmp.rearrange("p t (h f) -> p t h f", h=4), None)
            head_norm_rope(k, ik, k.hgain[:, l, 4, :], itmp[:, :, 0:HD].rearrange("p t (h f) -> p t h f", h=1), irs)
            iqT, end2 = k.carve(end2, 2, T)
            ikT, end2 = k.carve(end2, 1, T)
            pair, end2 = k.carve(end2, TT, P)
            with k.block() as block:
                @block.vector
                def _(dve):
                    dve.tensor_copy(pair[:, :, 0:HD], tm[:, 0:TT, 256:256 + HD])
                    dve.tensor_copy(pair[:, :, HD:P], tm[:, 0:TT, 256:256 + HD])
            turn(k, [(tm[:, 0:TT, 0:256], iqT, HD ** -0.5), (pair, ikT, 1.0)])
            picked = tm[:, TT:2 * TT, 0:T]
            score = tm[:, TT:2 * TT, T:2 * T]
            relu, end2 = k.carve(end2, 4, BANK)
            best, end2 = k.carve(end2, 8)
            pick_keys(k, iqT, ikT, iw, score, picked, relu, best)
            softmax_scores(k, qT, kT, picked, e0, e1, sums, nmax)
            scale_probs(k, 8, e0, e1, sums)
            turn_probs(k, 8, e0, e1, pT)
            values(k, 8, HD, part(2), pT, ybr)

    def to_gates(eng, chain, m, ps):
        return eng.activation(gates[:, m, :], ps, ACT.Sigmoid)
    gemm(k, [(1, 512)] * 6, lambda kt: k.h[:, kt, 0:T], T, act=to_gates)
    for branch in range(3):
        def merge(eng, chain, m, ps, branch=branch):
            g = gates[:, branch * DC + m, :]
            if branch == 0:
                return eng.tensor_tensor(k.h[:, m, 0:T], ps, g, ALU.mult)
            chain(eng.tensor_tensor(g, ps, g, ALU.mult))
            return eng.tensor_tensor(k.h[:, m, 0:T], k.h[:, m, 0:T], g, ALU.add)
        gemm(k, [(1, D)], lambda kt, branch=branch: y[:, 4 * branch + kt, :], T, dve=merge)
    gemm(k, [(1, 512)] * 2, lambda kt: k.h[:, kt, 0:T], T, dve=add_to_x(k))

    up, _ = k.carve(0, D_FF // P, T)
    rmsnorm(k, k.x, k.h, DC, T, lambda c: [(column(k, "mlp_norm", l * DC + c), (0, T))])
    gemm(k, [(1, 512)] * (D_FF // 512), lambda kt: k.h[:, kt, 0:T], T,
         act=lambda eng, chain, m, ps: eng.activation(up[:, m, :], ps, ACT.Relu),
         dve=lambda eng, chain, m, ps: eng.tensor_tensor(up[:, m, :], up[:, m, :], up[:, m, :], ALU.mult))
    gemm(k, [(D_FF // D, 512)] * 2, lambda kt: up[:, kt, :], T, dve=add_to_x(k))

    gate, end = k.carve(0, DC, T)
    ptok, end = k.carve(end, TT, T)
    pT, end = k.carve(end, TT, T)
    rmsnorm(k, k.x, k.h, DC, T, lambda c: [(column(k, "ple_norm", l * DC + c), (0, T))])
    with k.block() as block:
        @block.sync
        def _(sp):
            sp.dma_start(ptok, k.inp["p"][l, 0].rearrange("(t p) d -> p t d", p=P)).then_inc(k.loaded.sem, 16)
            sp.wait_ge(k.loaded.sem, k.loaded.at(16))
    k.loaded.passed(16)
    turn(k, [(ptok, pT, 1.0)])
    gemm(k, [(1, 512)] * 2, lambda kt: k.h[:, kt, 0:T], T,
         act=lambda eng, chain, m, ps: eng.activation(gate[:, m, :], ps, ACT.Sigmoid))

    def gated(eng, chain, m, ps):
        chain(eng.tensor_tensor(gate[:, m, :], ps, gate[:, m, :], ALU.mult))
        return eng.tensor_tensor(k.x[:, m, 0:T], k.x[:, m, 0:T], gate[:, m, :], ALU.add)
    gemm(k, [(1, D)], lambda kt: pT[:, kt, :], T, dve=gated)


NF2 = D_FF_2 // P
FF_COLS = 256
R0, K0, V0, WA, GD, FO = 0, RC, 2 * RC, 3 * RC, 3 * RC + 1, 3 * RC + 2
MIX_E = FO + 2
LEVELS = 6
NB = 2 * TT
NC2 = 2 * NB


def plan_ffn(k, gu, down, i):
    g, d = k.inp[gu][i], k.inp[down][i]
    for j in range(D_FF_2 // FF_COLS):
        c = FF_COLS * j
        k.plan([wslab(g, 0, D, c, c + FF_COLS), wslab(g, 0, D, D_FF_2 + c, D_FF_2 + c + FF_COLS)])
    for j in range(2):
        for r in range(0, D_FF_2, D):
            k.plan([wslab(d, r, min(r + D, D_FF_2), 512 * j, 512 * (j + 1))])


def plan_cols(k, w, cols):
    for c in range(0, cols, 512):
        k.plan([wslab(w, 0, D, c, min(c + 512, cols))])


def plan_second(k, i):
    plan_cols(k, k.inp["ada_w_2"][i], N_MOD * D)
    plan_ffn(k, "ffn1_w_gu_2", "ffn1_w_down_2", i)
    if i == 0:
        plan_cols(k, k.inp["e_w_in_2"][0], MIX_E * P)
        plan_cols(k, k.inp["e_w_out_2"][0], D)
    else:
        plan_cols(k, k.inp["o_w_in_2"][0], 14 * P)
        plan_cols(k, k.inp["o_w_out_2"][0], D)
    plan_ffn(k, "ffn2_w_gu_2", "ffn2_w_down_2", i)


def column_groups(cols):
    return [(1, min(512, cols - c)) for c in range(0, cols, 512)]


def modulation(k, i, both):
    n_streams = 2 if both else 1
    if i == 0:
        with k.block() as block:
            @block.scalar
            def _(act):
                c, cc = k.col["c_2"], k.col["c_ctx_2"]
                chain = Chain(act, k.act_chain)
                act.activation(k.cond[:, :, 0], k.params[:, c:c + DC], ACT.Sigmoid)
                act.activation(k.cond[:, :, 1], k.params[:, cc:cc + DC], ACT.Sigmoid).then_inc(k.act_done.sem, 1)

            @block.vector
            def _(dve):
                c, cc = k.col["c_2"], k.col["c_ctx_2"]
                dve.wait_ge(k.act_done.sem, k.act_done.at(1))
                dve.tensor_tensor(k.cond[:, :, 0], k.cond[:, :, 0], k.params[:, c:c + DC], ALU.mult)
                dve.tensor_tensor(k.cond[:, :, 1], k.cond[:, :, 1], k.params[:, cc:cc + DC], ALU.mult)
        k.act_done.passed(1)
    nt = N_MOD * DC
    per = 4
    n_slabs = nt // per
    with k.block() as block:
        @block.tensor
        def _(pe):
            for s in range(n_slabs):
                w = k.take(pe)
                for m in range(per):
                    t = s * per + m
                    for kt in range(DC):
                        mm = pe.matmul(k.ps[:, 0, 2 * t:2 * t + n_streams], w[:, kt, m * P:(m + 1) * P],
                                       k.cond[:, kt, 0:n_streams], start=(kt == 0), stop=(kt == DC - 1))
                mm.then_inc(k.tile_done.sem, 1)
                k.spent(k.tile_done, k.tile_done.at(s + 1))

        @block.sync
        def _(sp):
            k.feed(sp)

        @block.vector
        def _(dve):
            chain = Chain(dve, k.dve_chain)
            dve.wait_ge(k.tile_done.sem, k.tile_done.at(n_slabs))
            b = k.col["ada_b_2"] + i * nt
            for s in range(n_streams):
                ins = dve.tensor_tensor(k.mod[:, :, s], k.ps[:, 0, s:2 * nt:2], k.params[:, b:b + nt], ALU.add)
            chain(ins)
            for j in range(3):
                g = k.col["norm_g_2"] + (3 * i + j) * DC
                for s in range(n_streams):
                    sc = k.mod[:, (3 * j + 1) * DC:(3 * j + 2) * DC, s]
                    dve.scalar_tensor_tensor(out=k.gs[:, j, :, s], in0=sc, scalar=1.0, in1=k.params[:, g:g + DC],
                                             op0=ALU.add, op1=ALU.mult)
                    if j != 1:
                        dve.tensor_scalar(k.half[:, j // 2, :, s], k.mod[:, (3 * j + 2) * DC:(3 * j + 3) * DC, s],
                                          0.5, None, ALU.mult)
    k.tile_done.passed(n_slabs)


def streams(n):
    return [(0, (0, T))] + ([(1, (T, 2 * T))] if n > T else [])


def modulate(k, j, n):
    rmsnorm(k, k.x, k.h, DC, n,
            lambda c: [(k.gs[:, j, c, s:s + 1], r) for s, r in streams(n)],
            shift=lambda c: [(k.mod[:, 3 * j * DC + c, s:s + 1], r) for s, r in streams(n)])


def half_ffn(k, j, n):
    modulate(k, j, n)
    u, end = k.carve(0, NF2, n)
    s, end = k.carve(end, 4, n)
    pairs = FF_COLS // P
    glu(k, D_FF_2 // FF_COLS, pairs, n, u, s)
    jj = j // 2
    gemm(k, [(3, 512)] * 2, lambda kt: u[:, kt, :], n,
         dve=add_to_x(k, n, lambda m: [(k.half[:, jj, m, st:st + 1], r) for st, r in streams(n)]))


def glu(k, n_slabs, pairs, n, u, s):
    per = 2 * pairs
    with k.block() as block:
        @block.tensor
        def _(pe):
            for j in range(n_slabs):
                w = k.take(pe)
                for m in range(per):
                    t = j * per + m
                    if t >= BANKS:
                        pe.wait_ge(k.dve_done.sem, k.dve_done.at(t - BANKS + 1))
                    for kt in range(DC):
                        mm = pe.matmul(k.ps[:, t % BANKS, 0:n], w[:, kt, m * P:(m + 1) * P], k.h[:, kt, 0:n],
                                       start=(kt == 0), stop=(kt == DC - 1))
                    mm.then_inc(k.tile_done.sem, 1)
                k.spent(k.tile_done, k.tile_done.at(per * (j + 1)))

        @block.sync
        def _(sp):
            k.feed(sp)

        @block.scalar
        def _(act):
            for j in range(n_slabs):
                for m in range(pairs):
                    f = j * pairs + m
                    act.wait_ge(k.tile_done.sem, k.tile_done.at(j * per + m + 1))
                    if f >= 4:
                        act.wait_ge(k.dve_done.sem, k.dve_done.at((f - 4) // pairs * per + (f - 4) % pairs + 1))
                    act.activation(s[:, f % 4, :], k.ps[:, (j * per + m) % BANKS, 0:n], ACT.Sigmoid).then_inc(
                        k.act_done.sem, 1)

        @block.vector
        def _(dve):
            for j in range(n_slabs):
                for m in range(per):
                    t = j * per + m
                    f = j * pairs + m % pairs
                    if m < pairs:
                        dve.wait_ge(k.act_done.sem, k.act_done.at(f + 1))
                        ins = dve.tensor_tensor(u[:, f, :], k.ps[:, t % BANKS, 0:n], s[:, f % 4, :], ALU.mult)
                    else:
                        dve.wait_ge(k.tile_done.sem, k.tile_done.at(t + 1))
                        dve.wait_ge(k.dve_done.sem, k.dve_done.at(t - pairs + 1))
                        ins = dve.tensor_tensor(u[:, f, :], k.ps[:, t % BANKS, 0:n], u[:, f, :], ALU.mult)
                    ins.then_inc(k.dve_done.sem, 1)
    k.tile_done.passed(n_slabs * per)
    k.act_done.passed(n_slabs * pairs)
    k.dve_done.passed(n_slabs * per)


def load_constants(k, jobs):
    with k.block() as block:
        @block.sync
        def _(sp):
            for dst, src in jobs:
                sp.dma_start(dst, src).then_inc(k.loaded.sem, 16)
            sp.wait_ge(k.loaded.sem, k.loaded.at(16 * len(jobs)))
    k.loaded.passed(16 * len(jobs))


def fourier(k, u, out, at):
    cs, end = k.carve(at, 2 * P)
    cn, end = k.carve(end, 2 * TT, T)
    mid, end = k.carve(end, 2 * TT, 2 * P)
    load_constants(k, [(cs, k.con["dft_channels"]), (cn, k.con["dft_tokens"].rearrange("(a p) t -> p a t", p=P))])
    with k.block() as block:
        @block.tensor
        def _(pe):
            for f in range(2):
                for tt in range(TT):
                    pe.matmul(k.ps[:, f * TT + tt, 0:2 * P], u[:, f, tt * P:(tt + 1) * P], cs,
                              start=True, stop=True).then_inc(k.tile_done.sem, 1)
            for f in range(2):
                pe.wait_ge(k.act_done.sem, k.act_done.at((f + 1) * TT))
                for q in range(2 * TT):
                    part, tt = q // TT, q % TT
                    mm = pe.matmul(k.ps[:, 4 + f, 0:T], mid[:, f * TT + tt, part * P:(part + 1) * P],
                                   cn[:, q, :], start=(q == 0), stop=(q == 2 * TT - 1))
                mm.then_inc(k.tile_done.sem, 1)

        @block.scalar
        def _(act):
            for q in range(4):
                act.wait_ge(k.tile_done.sem, k.tile_done.at(q + 1))
                act.activation(mid[:, q, :], k.ps[:, q, 0:2 * P], ACT.Copy).then_inc(k.act_done.sem, 1)
            for f in range(2):
                act.wait_ge(k.tile_done.sem, k.tile_done.at(5 + f))
                act.activation(out[:, f, :], k.ps[:, 4 + f, 0:T], ACT.Copy)
    k.tile_done.passed(6)
    k.act_done.passed(4)


def token_shift(k, z, tiles, mu, tmp):
    with k.block() as block:
        @block.vector
        def _(dve):
            chain = Chain(dve, k.dve_chain)
            for c in range(tiles):
                t = tmp[:, c % 2, :].rearrange("p (s t) -> p s t", s=2)
                v = z[:, c, :].rearrange("p (s t) -> p s t", s=2)
                dve.tensor_copy(t[:, :, T - 1:T], v[:, :, T - 2:T - 1])
                dve.tensor_copy(t[:, :, 0:1], v[:, :, 1:2])
                chain(dve.tensor_tensor(t[:, :, 1:T - 1], v[:, :, 0:T - 2], v[:, :, 2:T], ALU.add))
                chain(dve.scalar_tensor_tensor(out=t, in0=t, scalar=0.5, in1=v, op0=ALU.mult, op1=ALU.subtract))
                dve.scalar_tensor_tensor(out=v, in0=t, scalar=column(k, "e_mu_2", mu + c), in1=v, op0=ALU.mult, op1=ALU.add)
            ins = dve.tensor_copy(tmp[:, 0, 0:1], tmp[:, 0, 0:1])
            chain(ins)


def scan_tile(k, p, z, y, at):
    n = 2 * T
    r, kz, v = z[:, R0 + p, :], z[:, K0 + p, :], z[:, V0 + p, :]
    kk, end = k.carve(at, n)
    vt, end = k.carve(end, NB, P)
    coef, end = k.carve(end, T)
    after_common = end
    t1, _ = k.carve(end, n)
    t2, _ = k.carve(end + n, n)
    col = lambda name, a=0: column(k, name, a + p)
    wa = z[:, WA, :]
    with k.block() as block:
        @block.vector
        def _(dve):
            chain = Chain(dve, k.dve_chain)
            chain(dve.tensor_scalar(kk, kz, col("e_k_k_2"), None, ALU.mult))
            dve.tensor_tensor(t1, kk, kk, ALU.mult).then_inc(k.dve_done.sem, 1)
            dve.wait_ge(k.act_done.sem, k.act_done.at(1))
            chain(dve.tensor_scalar(t2, t2, 1e-12, None, ALU.max))
            chain(dve.reciprocal(t2, t2))
            dve.tensor_tensor(kk, kk, t2, ALU.mult)

        @block.tensor
        def _(pe):
            for b in range(NB):
                mm = pe.transpose(k.ps[:, 1, b * P:(b + 1) * P], v[:, b * P:(b + 1) * P], k.ident[:, :])
            mm.then_inc(k.pe_done.sem, 1)
            pe.wait_ge(k.dve_done.sem, k.dve_done.at(1))
            pe.matmul(k.ps[:, 0, 0:n], k.head_ones[:, :], t1, start=True, stop=True).then_inc(k.pe_done.sem, 1)

        @block.scalar
        def _(act):
            act.wait_ge(k.pe_done.sem, k.pe_done.at(2))
            act.activation(t2, k.ps[:, 0, 0:n], ACT.Sqrt).then_inc(k.act_done.sem, 1)
            act.activation(vt, k.ps[:, 1, :].rearrange("p (b f) -> p b f", b=NB), ACT.Copy)
    k.dve_done.passed(1)
    k.act_done.passed(1)
    k.pe_done.passed(2)

    for d in range(2):
        end = after_common
        A, end = k.carve(end, n)
        BK, end = k.carve(end, 2, n)
        R, end = k.carve(end, T)
        gend, end = k.carve(end, NC2)
        tot, end = k.carve(end, NC2)
        At, end = k.carve(end, NB, P)
        Bt, end = k.carve(end, NB, P)
        Kt, end = k.carve(end, NB, P)
        after_prep = end
        lw, end = k.carve(end, n)
        cum, end = k.carve(end, n)
        a, end = k.carve(end, n)
        kd, end = k.carve(end, n)
        g, end = k.carve(end, n)
        m = k.masks[d]

        with k.block() as block:
            @block.tensor
            def _(pe):
                up = k.up_w[d * RC + p]
                pe.matmul(k.ps[:, 0, 0:n], up[0:HD, :], wa[0:HD, :], start=True, stop=True).then_inc(k.pe_done.sem, 1)
                pe.matmul(k.ps[:, 1, 0:n], up[HD:P, :], wa[HD:P, :], start=True, stop=True).then_inc(k.pe_done.sem, 1)

            @block.scalar
            def _(act):
                act.wait_ge(k.pe_done.sem, k.pe_done.at(1))
                act.activation(lw, k.ps[:, 0, 0:n], ACT.Sigmoid, bias=col("e_w0_2", d * RC)).then_inc(k.act_done.sem, 1)
                act.wait_ge(k.pe_done.sem, k.pe_done.at(2))
                act.activation(a, k.ps[:, 1, 0:n], ACT.Sigmoid, bias=col("e_a0_2", d * RC)).then_inc(k.act_done.sem, 1)
                act.wait_ge(k.dve_done.sem, k.dve_done.at(1))
                act.activation(g, cum, ACT.Exp).then_inc(k.act_done.sem, 1)
                act.activation(gend, tot, ACT.Exp).then_inc(k.act_done.sem, 1)
                act.activation(BK[:, 0, :], cum, ACT.Exp, scale=-1.0).then_inc(k.act_done.sem, 1)
                act.activation(A, lw, ACT.Exp).then_inc(k.act_done.sem, 1)

            @block.vector
            def _(dve):
                chain = Chain(dve, k.dve_chain)
                dve.wait_ge(k.act_done.sem, k.act_done.at(1))
                chain(dve.tensor_scalar(lw, lw, -DECAY_SCALE, None, ALU.mult))
                chain(dve.tensor_tensor_scan(cum, k.chunk_start, lw, 0.0, ALU.mult, ALU.add))
                c3 = cum.rearrange("p (c t) -> p c t", c=NC2)
                l3 = lw.rearrange("p (c t) -> p c t", c=NC2)
                chain(dve.tensor_copy(tot, c3[:, :, CHUNK - 1]))
                if d == 1:
                    chain(dve.tensor_tensor(cum, lw, cum, ALU.subtract))
                    chain(dve.tensor_tensor(c3, c3, tot.rearrange("p (c o) -> p c o", o=1).broadcast_to([P, NC2, CHUNK]), ALU.add))
                dve.tensor_tensor(lw, cum, lw, ALU.subtract).then_inc(k.dve_done.sem, 1)
                dve.wait_ge(k.act_done.sem, k.act_done.at(2))
                chain(dve.tensor_scalar(kd, a, 1.0, col("e_k_a_2"), ALU.subtract, ALU.mult))
                chain(dve.scalar_tensor_tensor(out=kd, in0=kd, scalar=1.0, in1=kz, op0=ALU.add, op1=ALU.mult))
                chain(dve.tensor_tensor(a, a, kk, ALU.mult))
                dve.wait_ge(k.act_done.sem, k.act_done.at(6))
                dve.tensor_tensor(BK[:, 1, :], BK[:, 0, :], kd, ALU.mult)
                dve.tensor_tensor(A, A, kk, ALU.mult)
                chain(dve.tensor_tensor(R, g[:, 0:T], r[:, 0:T], ALU.mult))
                chain(dve.scalar_tensor_tensor(out=kd[:, 0:T], in0=kd[:, 0:T], scalar=col("e_r_k_2"), in1=r[:, 0:T],
                                               op0=ALU.mult, op1=ALU.mult))
                chain(dve.tensor_tensor(BK[:, 0, :], BK[:, 0, :], a, ALU.mult))
                if d == 0:
                    chain(dve.tensor_copy(coef, kd[:, 0:T]))
                else:
                    chain(dve.tensor_tensor(coef, coef, kd[:, 0:T], ALU.add))
        k.pe_done.passed(2)
        k.act_done.passed(6)
        k.dve_done.passed(1)

        end = after_prep
        per = {}
        for h in range(2):
            per[h], end = {}, end
            for name, shape in (("MT", (NB, P)), ("N", (NB, P)), ("T", (NB, P)), ("TT", (NB, P)), ("Q", (NB, P)),
                                ("off", (NB, P)), ("E", (NB, HD)), ("Z", (TT, P)), ("RK", (TT, P)), ("RB", (TT, P)),
                                ("K2", (NB, HD))):
                per[h][name], end = k.carve(end, *shape)
        r2, end = k.carve(end, T)
        step, end = k.carve(end, NC2, HD)
        inp, end = k.carve(end, NC2, HD)
        state, end = k.carve(end, 9, HD)

        def rows(h):
            return slice(h * HD, (h + 1) * HD)

        def bl(b):
            return slice(b * P, (b + 1) * P)

        def bank(i, nb=NB, w=P):
            return k.ps[:, i, 0:nb * w].rearrange("p (b f) -> p b f", b=nb)

        def wide(mask, nb):
            return mask.rearrange("p (o f) -> p o f", o=1).broadcast_to([P, nb, P])

        with k.block() as block:
            @block.tensor
            def _(pe):
                for i, s in enumerate((A, BK[:, 0, :], BK[:, 1, :])):
                    for b in range(NB):
                        mm = pe.transpose(k.ps[:, i, bl(b)], s[:, bl(b)], k.ident[:, :])
                    mm.then_inc(k.tile_done.sem, 1)
                for h in range(2):
                    for b in range(NB):
                        mm = pe.matmul(k.ps[:, 3 + h, bl(b)], BK[rows(h), 0, bl(b)], A[rows(h), bl(b)], start=True, stop=True)
                    mm.then_inc(k.tile_done.sem, 1)
                for i, (h, j) in enumerate(((0, 1), (0, 0), (1, 1), (1, 0))):
                    if i == 3:
                        pe.wait_ge(k.act_done.sem, k.act_done.at(1))
                    for b in range(NB):
                        mm = pe.matmul(k.ps[:, (5 + i) % BANKS, bl(b)], A[rows(h), bl(b)], BK[rows(h), j, bl(b)],
                                       start=True, stop=True)
                    mm.then_inc(k.tile_done.sem, 1)
                pe.wait_ge(k.act_done.sem, k.act_done.at(3))
                for h in range(2):
                    for j in range(2):
                        for b in range(TT):
                            c0 = (j * TT + b) * P
                            mm = pe.matmul(k.ps[:, 1 + h, c0:c0 + P], BK[rows(h), j, bl(b)], R[rows(h), bl(b)],
                                           start=True, stop=True)
                    mm.then_inc(k.tile_done.sem, 1)

            @block.scalar
            def _(act):
                for i, dst in enumerate((At, Bt, Kt)):
                    act.wait_ge(k.tile_done.sem, k.tile_done.at(i + 1))
                    act.activation(dst, bank(i), ACT.Copy).then_inc(k.act_done.sem, 1)
                for h in range(2):
                    act.wait_ge(k.tile_done.sem, k.tile_done.at(4 + h))
                    act.activation(per[h]["MT"], bank(3 + h), ACT.Copy).then_inc(k.act_done.sem, 1)

            @block.vector
            def _(dve):
                chain = Chain(dve, k.dve_chain)
                for i, (h, j) in enumerate(((0, 1), (0, 0), (1, 1), (1, 0))):
                    dve.wait_ge(k.tile_done.sem, k.tile_done.at(6 + i))
                    bk = bank((5 + i) % BANKS)
                    if j == 1:
                        dve.tensor_tensor(per[h]["N"], bk, wide(m["strict"], NB), ALU.mult)
                    else:
                        chain(dve.tensor_tensor(per[h]["T"], bk, wide(m["level0"], NB), ALU.mult))
                        dve.tensor_tensor(per[h]["T"], wide(k.ident[:, :], NB), per[h]["T"], ALU.subtract)
                for h in range(2):
                    dve.wait_ge(k.act_done.sem, k.act_done.at(4 + h))
                    chain(dve.tensor_tensor(per[h]["TT"], per[h]["MT"], wide(m["level0_T"], NB), ALU.mult))
                    dve.tensor_tensor(per[h]["TT"], wide(k.ident[:, :], NB), per[h]["TT"], ALU.subtract)
                for h in range(2):
                    dve.wait_ge(k.tile_done.sem, k.tile_done.at(10 + h))
                    dve.tensor_tensor(per[h]["RB"], bank(1 + h)[:, 0:TT, :], wide(m["incl_T"], TT), ALU.mult)
                    dve.tensor_tensor(per[h]["RK"], bank(1 + h)[:, TT:NB, :], wide(m["incl_T"], TT), ALU.mult)
        k.tile_done.passed(11)
        k.act_done.passed(5)

        with k.block() as block:
            @block.gpsimd
            def _(pool):
                for l in range(1, LEVELS):
                    for h in range(2):
                        if l > 1:
                            pool.wait_ge(k.tile_done.sem, k.tile_done.at(6 * (l - 2) + 3 * h + 1))
                        pool.tensor_tensor(per[h]["off"], per[h]["MT"], wide(m[f"level{l}_T"], NB), ALU.mult).then_inc(
                            k.pool_done.sem, 1)

            @block.tensor
            def _(pe):
                for l in range(1, LEVELS):
                    for h in range(2):
                        pe.wait_ge(k.pool_done.sem, k.pool_done.at(2 * (l - 1) + h + 1))
                        if l > 1:
                            pe.wait_ge(k.dve_done.sem, k.dve_done.at(4 * (l - 2) + 2 * h + 1))
                        for b in range(NB):
                            mm = pe.matmul(k.ps[:, 3 * h, bl(b)], per[h]["off"][:, b, :], per[h]["T"][:, b, :],
                                           start=True, stop=True)
                        mm.then_inc(k.tile_done.sem, 1)
                        pe.wait_ge(k.act_done.sem, k.act_done.at(2 * (l - 1) + h + 1))
                        if l > 1:
                            pe.wait_ge(k.dve_done.sem, k.dve_done.at(4 * (l - 2) + 2 * h + 2))
                        for b in range(NB):
                            mm = pe.matmul(k.ps[:, 3 * h + 1, bl(b)], per[h]["TT"][:, b, :], per[h]["Q"][:, b, :],
                                           start=True, stop=True)
                        mm.then_inc(k.tile_done.sem, 1)
                        for b in range(NB):
                            mm = pe.matmul(k.ps[:, 3 * h + 2, bl(b)], per[h]["Q"][:, b, :], per[h]["TT"][:, b, :],
                                           start=True, stop=True)
                        mm.then_inc(k.tile_done.sem, 1)

            @block.scalar
            def _(act):
                for l in range(1, LEVELS):
                    for h in range(2):
                        act.wait_ge(k.tile_done.sem, k.tile_done.at(6 * (l - 1) + 3 * h + 1))
                        act.activation(per[h]["Q"], bank(3 * h), ACT.Copy).then_inc(k.act_done.sem, 1)

            @block.vector
            def _(dve):
                for l in range(1, LEVELS):
                    for h in range(2):
                        for j, name in enumerate(("T", "TT")):
                            dve.wait_ge(k.tile_done.sem, k.tile_done.at(6 * (l - 1) + 3 * h + 3))
                            dve.tensor_tensor(per[h][name], per[h][name], bank(3 * h + 1 + j), ALU.subtract).then_inc(
                                k.dve_done.sem, 1)
        k.pool_done.passed(2 * (LEVELS - 1))
        k.tile_done.passed(6 * (LEVELS - 1))
        k.act_done.passed(2 * (LEVELS - 1))
        k.dve_done.passed(4 * (LEVELS - 1))

        with k.block() as block:
            @block.tensor
            def _(pe):
                for h in range(2):
                    for b in range(NB):
                        pe.matmul(k.ps[:, 2 * h, b * HD:(b + 1) * HD], per[h]["T"][:, b, :], Bt[:, b, rows(h)],
                                  start=True, stop=True)
                    for b in range(TT):
                        mm = pe.matmul(k.ps[:, 2 * h + 1, bl(b)], per[h]["T"][:, b, :], per[h]["RB"][:, b, :],
                                       start=True, stop=True)
                    mm.then_inc(k.tile_done.sem, 1)
                    pe.wait_ge(k.act_done.sem, k.act_done.at(2 * h + 2))
                    for b in range(NB):
                        pe.matmul(k.ps[:, 4 + h, b * HD:(b + 1) * HD], per[h]["N"][:, b, :], per[h]["E"][:, b, :],
                                  start=True, stop=True)
                    for b in range(TT):
                        mm = pe.matmul(k.ps[:, 6 + h, bl(b)], per[h]["N"][:, b, :], per[h]["Z"][:, b, :],
                                       start=True, stop=True)
                    mm.then_inc(k.tile_done.sem, 1)

            @block.scalar
            def _(act):
                for h in range(2):
                    act.wait_ge(k.tile_done.sem, k.tile_done.at(2 * h + 1))
                    act.activation(per[h]["E"], bank(2 * h, NB, HD), ACT.Copy).then_inc(k.act_done.sem, 1)
                    act.activation(per[h]["Z"], bank(2 * h + 1, TT), ACT.Copy).then_inc(k.act_done.sem, 1)

            @block.vector
            def _(dve):
                for h in range(2):
                    dve.wait_ge(k.tile_done.sem, k.tile_done.at(2 * h + 2))
                    dve.tensor_tensor(per[h]["K2"], Kt[:, :, rows(h)], bank(4 + h, NB, HD), ALU.subtract)
                    dve.tensor_tensor(per[h]["RK"], per[h]["RK"], bank(6 + h, TT), ALU.subtract)
        k.tile_done.passed(4)
        k.act_done.passed(4)

        with k.block() as block:
            @block.tensor
            def _(pe):
                for h in range(2):
                    for b in range(TT):
                        mm = pe.matmul(k.ps[rows(h), 0, bl(b)], At[:, b, rows(h)], per[h]["Z"][:, b, :], start=True, stop=True)
                mm.then_inc(k.tile_done.sem, 1)
                for c in range(NC2):
                    b, q = c // 2, c % 2
                    for h in range(2):
                        o = slice(b * HD, (b + 1) * HD)
                        pe.matmul(k.ps[rows(h), 1 + q, o], At[rows(q), b, rows(h)], per[h]["E"][rows(q), b, :],
                                  start=True, stop=True)
                        mm = pe.matmul(k.ps[rows(h), 3 + q, o], per[h]["K2"][rows(q), b, :], vt[rows(q), b, rows(h)],
                                       start=True, stop=True)
                mm.then_inc(k.tile_done.sem, 1)

            @block.vector
            def _(dve):
                chain = Chain(dve, k.dve_chain)
                dve.wait_ge(k.tile_done.sem, k.tile_done.at(1))
                dve.tensor_tensor(r2, R, k.ps[:, 0, 0:T], ALU.subtract)
                chain(dve.memset(state[:, 0, :], 0.0))
                dve.wait_ge(k.tile_done.sem, k.tile_done.at(2))
                for q in range(2):
                    dve.tensor_tensor(step[:, q:NC2:2, :], k.ident2[:, :].rearrange("p (o f) -> p o f", o=1).broadcast_to([P, NB, HD]),
                                      bank(1 + q, NB, HD), ALU.subtract)
                    dve.tensor_tensor(inp[:, q:NC2:2, :], bank(3 + q, NB, HD),
                                      gend[:, q:NC2:2].rearrange("p (c o) -> p c o", o=1).broadcast_to([P, NB, HD]), ALU.mult)
        k.tile_done.passed(2)

        order = [4, 5, 6, 7, 0, 1, 2, 3] if d == 0 else [7, 6, 5, 4, 3, 2, 1, 0]
        with k.block() as block:
            @block.tensor
            def _(pe):
                for i, c in enumerate(order):
                    if i:
                        pe.wait_ge(k.dve_done.sem, k.dve_done.at(i))
                    for h in range(2):
                        mm = pe.matmul(k.ps[rows(h), 2 * (i % 2) + h, 0:HD], step[rows(h), c, :], state[rows(h), i, :],
                                       start=True, stop=True)
                    mm.then_inc(k.tile_done.sem, 1)

            @block.vector
            def _(dve):
                for i, c in enumerate(order):
                    dve.wait_ge(k.tile_done.sem, k.tile_done.at(i + 1))
                    for h in range(2):
                        ins = dve.scalar_tensor_tensor(out=state[rows(h), i + 1, :], in0=k.ps[rows(h), 2 * (i % 2) + h, 0:HD],
                                                       scalar=gend[rows(h), c:c + 1], in1=inp[rows(h), c, :],
                                                       op0=ALU.mult, op1=ALU.add)
                    ins.then_inc(k.dve_done.sem, 1)
        k.tile_done.passed(8)
        k.dve_done.passed(8)

        with k.block() as block:
            @block.tensor
            def _(pe):
                for h in range(2):
                    for i, c in enumerate(order):
                        if c < NC2 // 2:
                            o = slice(c * CHUNK, (c + 1) * CHUNK)
                            pe.matmul(k.ps[rows(h), h, o], state[rows(h), i, :], r2[rows(h), o], start=True, stop=True)
                for h in range(2):
                    for b in range(TT):
                        mm = pe.matmul(k.ps[rows(h), 2, bl(b)], vt[:, b, rows(h)], per[h]["RK"][:, b, :], start=True, stop=True)
                mm.then_inc(k.tile_done.sem, 1)

            @block.vector
            def _(dve):
                chain = Chain(dve, k.dve_chain)
                dve.wait_ge(k.tile_done.sem, k.tile_done.at(1))
                for h in range(2):
                    if d == 0:
                        ins = dve.tensor_copy(y[rows(h), :], k.ps[rows(h), h, 0:T])
                    else:
                        ins = dve.tensor_tensor(y[rows(h), :], y[rows(h), :], k.ps[rows(h), h, 0:T], ALU.add)
                chain(ins)
                dve.tensor_tensor(y, y, k.ps[:, 2, 0:T], ALU.add)
        k.tile_done.passed(1)

    t1, end = k.carve(after_common, 2, T)
    t2, end = k.carve(end, 2, T)
    with k.block() as block:
        @block.tensor
        def _(pe):
            pe.matmul(k.ps[:, 0, 0:T], k.head_ones[:, :], y, start=True, stop=True).then_inc(k.tile_done.sem, 1)
            pe.matmul(k.ps[:, 1, 0:T], k.head_ones[:, :], coef, start=True, stop=True).then_inc(k.tile_done.sem, 1)
            pe.wait_ge(k.dve_done.sem, k.dve_done.at(1))
            pe.matmul(k.ps[:, 2, 0:T], k.head_ones[:, :], t1[:, 0, :], start=True, stop=True).then_inc(k.tile_done.sem, 1)

        @block.vector
        def _(dve):
            chain = Chain(dve, k.dve_chain)
            dve.wait_ge(k.tile_done.sem, k.tile_done.at(1))
            chain(dve.scalar_tensor_tensor(out=y, in0=k.ps[:, 0, 0:T], scalar=-1.0 / HD, in1=y, op0=ALU.mult, op1=ALU.add))
            dve.tensor_tensor(t1[:, 0, :], y, y, ALU.mult).then_inc(k.dve_done.sem, 1)
            dve.wait_ge(k.tile_done.sem, k.tile_done.at(2))
            dve.tensor_tensor(t2[:, 0, :], k.ps[:, 1, 0:T], v[:, 0:T], ALU.mult)
            dve.wait_ge(k.tile_done.sem, k.tile_done.at(3))
            chain(dve.tensor_scalar(t1[:, 1, :], k.ps[:, 2, 0:T], 1.0 / HD, GN_EPS, ALU.mult, ALU.add))
            dve.reciprocal(t1[:, 1, :], t1[:, 1, :]).then_inc(k.dve_done.sem, 1)
            dve.wait_ge(k.act_done.sem, k.act_done.at(1))
            chain(dve.tensor_tensor(y, y, t1[:, 1, :], ALU.mult))
            chain(dve.tensor_scalar(y, y, col("e_gn_w_2"), col("e_gn_b_2"), ALU.mult, ALU.add))
            chain(dve.tensor_tensor(y, y, t2[:, 0, :], ALU.add))
            dve.tensor_tensor(y, y, k.gate[:, p, :], ALU.mult)

        @block.scalar
        def _(act):
            act.wait_ge(k.dve_done.sem, k.dve_done.at(2))
            act.activation(t1[:, 1, :], t1[:, 1, :], ACT.Sqrt).then_inc(k.act_done.sem, 1)
    k.tile_done.passed(3)
    k.dve_done.passed(2)
    k.act_done.passed(1)


def even_mixer(k):
    n = 2 * T
    z, end = k.carve(0, MIX_E, n)
    gemm(k, column_groups(MIX_E * P), lambda kt: k.h[:, kt, :], n,
         act=lambda eng, chain, m, ps: eng.activation(z[:, m, :], ps, ACT.Copy))
    y = k.h[:, :, 0:T]
    fourier(k, z[:, FO:FO + 2, 0:T], y[:, RC:RC + 2, :], end)
    tmp, _ = k.carve(end, 2, n)
    token_shift(k, z, FO, 0, tmp)
    k.gate, end = k.carve(FO * n, RC, T)
    spare = [k.x[:, b // 2, T + b % 2 * P:T + (b % 2 + 1) * P] for b in range(2 * DC)]
    masks = spare[0:2 * (LEVELS + 2)]
    k.ident2, end = k.carve(end, HD)
    k.chunk_start, end = k.carve(end, n)
    k.up_w = [k.h[:, b // 2, T + b % 2 * P:T + (b % 2 + 1) * P] for b in range(2 * RC)]
    g_up, _ = k.carve(end, D_RWKV)
    i = k.inp
    jobs = [(m, k.con["scan_masks"][P * j:P * (j + 1), :]) for j, m in enumerate(masks)] + [(k.ident2, k.con["ident2"]),
            (k.chunk_start, k.con["chunk_start"]), (g_up, i["e_g_up_2"][0])]
    for d in range(2):
        for p in range(RC):
            jobs.append((k.up_w[d * RC + p][0:HD, :], i["e_w_up_2"][0, d, :, p * P:(p + 1) * P]))
            jobs.append((k.up_w[d * RC + p][HD:P, :], i["e_a_up_2"][0, d, :, p * P:(p + 1) * P]))
    load_constants(k, jobs)
    fwd, bwd = {}, {}
    fwd["strict"], bwd["strict"] = masks[0], masks[1]
    fwd["incl_T"], bwd["incl_T"] = masks[2], masks[3]
    for l in range(LEVELS):
        a, b = masks[4 + 2 * l], masks[5 + 2 * l]
        fwd[f"level{l}"], fwd[f"level{l}_T"] = a, b
        bwd[f"level{l}"], bwd[f"level{l}_T"] = b, a
    k.masks = [fwd, bwd]
    with k.block() as block:
        @block.scalar
        def _(act):
            act.activation(z[0:HD, WA, :], z[0:HD, WA, :], ACT.Tanh)
            act.activation(z[:, GD, 0:T], z[:, GD, 0:T], ACT.Sigmoid).then_inc(k.act_done.sem, 1)
            for c in range(RC):
                act.wait_ge(k.tile_done.sem, k.tile_done.at(c + 1))
                act.activation(k.gate[:, c, :], k.ps[:, c, 0:T], ACT.Copy)

        @block.tensor
        def _(pe):
            pe.wait_ge(k.act_done.sem, k.act_done.at(1))
            for c in range(RC):
                pe.matmul(k.ps[:, c, 0:T], g_up[:, c * P:(c + 1) * P], z[:, GD, 0:T], start=True, stop=True).then_inc(
                    k.tile_done.sem, 1)
    k.act_done.passed(1)
    k.tile_done.passed(RC)
    for p in range(RC):
        scan_tile(k, p, z, y[:, p, :], end)
    gemm(k, column_groups(D), lambda kt: y[:, kt, :], T,
         dve=add_to_x(k, T, lambda m: [(k.mod[:, 5 * DC + m, 0:1], (0, T))]))


def odd_mixer(k):
    z, end = k.carve(0, 14, T)
    gemm(k, column_groups(14 * P), lambda kt: k.h[:, kt, 0:T], T,
         act=lambda eng, chain, m, ps: eng.activation(z[:, m, :], ps, ACT.Copy if m < RC or m >= 2 * RC else ACT.Sigmoid))
    pad = CONV_WIDTH // 2
    u, end = k.carve(end, RC, T + 2 * pad)
    c, end = k.carve(end, RC, T)
    cn, end = k.carve(end, RC, T)
    pool, end = k.carve(end, 4 * TT, T)
    pw, end = k.carve(end, 2, P)
    mid, end = k.carve(end, 2 * TT, P)
    y = k.h[:, :, 0:T]
    load_constants(k, [(pool, k.con["pool"].rearrange("(a p) t -> p a t", p=P))])
    with k.block() as block:
        @block.vector
        def _(dve):
            chain = Chain(dve, k.dve_chain)
            dve.memset(pw, 0.0).then_inc(k.dve_done.sem, 1)
            chain(dve.memset(u, 0.0))
            for f in range(RC):
                ins = dve.tensor_tensor(u[:, f, pad:pad + T], z[:, f, :], z[:, RC + f, :], ALU.mult)
            chain(ins)
            for w in range(CONV_WIDTH):
                for f in range(RC):
                    src, tap = u[:, f, w:w + T], k.conv_w[:, f, w:w + 1]
                    if w == 0:
                        ins = dve.tensor_scalar(c[:, f, :], src, tap, column(k, "o_conv_b_2", f), ALU.mult, ALU.add)
                    else:
                        ins = dve.scalar_tensor_tensor(out=c[:, f, :], in0=src, scalar=tap, in1=c[:, f, :],
                                                       op0=ALU.mult, op1=ALU.add)
                chain(ins)

        @block.sync
        def _(sp):
            sp.wait_ge(k.dve_done.sem, k.dve_done.at(1))
            for g in range(4):
                r = (g % 2) * HD
                sp.dma_start(pw[r:r + HD, g // 2, r:r + HD], k.inp["o_pool_w_2"][0, g]).then_inc(k.loaded.sem, 16)

        @block.tensor
        def _(pe):
            pe.wait_ge(k.loaded.sem, k.loaded.at(64))
            for f in range(2):
                for tt in range(TT):
                    pe.matmul(k.ps[:, 2 * f + tt, 0:P], z[:, 2 * RC + f, tt * P:(tt + 1) * P], pw[:, f, :],
                              start=True, stop=True).then_inc(k.tile_done.sem, 1)
            pe.wait_ge(k.act_done.sem, k.act_done.at(4))
            for g in range(4):
                r = (g % 2) * HD
                for tt in range(TT):
                    mm = pe.matmul(k.ps[r:r + HD, 4 + g // 2, 0:T], mid[:, g // 2 * TT + tt, r:r + HD],
                                   pool[:, g * TT + tt, :], start=(tt == 0), stop=(tt == TT - 1))
            mm.then_inc(k.tile_done.sem, 1)

        @block.scalar
        def _(act):
            for q in range(4):
                act.wait_ge(k.tile_done.sem, k.tile_done.at(q + 1))
                act.activation(mid[:, q, :], k.ps[:, q, 0:P], ACT.Copy).then_inc(k.act_done.sem, 1)
            act.wait_ge(k.tile_done.sem, k.tile_done.at(5))
            for f in range(2):
                act.activation(y[:, RC + f, :], k.ps[:, 4 + f, 0:T], ACT.Copy, scale=column(k, "o_pool_scale_2", f))
    k.dve_done.passed(1)
    k.loaded.passed(64)
    k.tile_done.passed(5)
    k.act_done.passed(4)
    rmsnorm(k, c, cn, RC, T, lambda f: [(column(k, "o_cnorm_g_2", f), (0, T))])
    with k.block() as block:
        @block.scalar
        def _(act):
            for f in range(RC):
                act.activation(c[:, f, :], cn[:, f, :], ACT.Sigmoid).then_inc(k.act_done.sem, 1)

        @block.vector
        def _(dve):
            for f in range(RC):
                dve.wait_ge(k.act_done.sem, k.act_done.at(f + 1))
                dve.tensor_tensor(y[:, f, :], c[:, f, :], cn[:, f, :], ALU.mult)
    k.act_done.passed(RC)
    gemm(k, column_groups(D), lambda kt: y[:, kt, :], T,
         dve=add_to_x(k, T, lambda m: [(k.mod[:, 5 * DC + m, 0:1], (0, T))]))


def second_block(k):
    for i in range(DEPTH):
        both = i == 0
        modulation(k, i, both)
        half_ffn(k, 0, 2 * T if both else T)
        modulate(k, 1, 2 * T if both else T)
        if i == 0:
            even_mixer(k)
        else:
            odd_mixer(k)
        half_ffn(k, 2, T)
    rmsnorm(k, k.x, k.h, DC, T, lambda c: [(column(k, "final_g_2", c), (0, T))])


def more_constants(c):
    import numpy as np
    i = np.arange(P)
    ch, t = np.arange(HD), np.arange(T)
    ang = 2 * np.pi * np.outer(ch, ch) / HD
    both = np.eye(2)
    c["dft_channels"] = np.concatenate([np.kron(both, np.cos(ang)), np.kron(both, -np.sin(ang))], axis=1)
    ang = 2 * np.pi * (np.outer(t, t) % T) / T
    norm = 1.0 / np.sqrt(T * HD)
    c["dft_tokens"] = np.concatenate([np.cos(ang), np.sin(ang)], axis=0) * norm
    same = (i[:, None] // CHUNK) == (i[None, :] // CHUNK)
    lower = (i[:, None] > i[None, :]) & same
    masks = [lower, lower.T, (lower | np.eye(P, dtype=bool)).T, lower | np.eye(P, dtype=bool)]
    for l in range(LEVELS):
        w = 1 << l
        level = ((i[:, None] // (2 * w)) == (i[None, :] // (2 * w))) & ((i[:, None] // w) % 2 == 1) & ((i[None, :] // w) % 2 == 0)
        masks += [level, level.T]
    c["scan_masks"] = np.concatenate(masks, axis=0)
    c["ident2"] = np.concatenate([np.eye(HD), np.eye(HD)], axis=0)
    c["chunk_start"] = np.broadcast_to((np.arange(2 * T) % CHUNK != 0)[None, :], (P, 2 * T))
    pools = []
    for w in (2, 4, 8, 16):
        lo = np.maximum(t - w // 2, 0)
        hi = np.minimum(t + (w - 1 - w // 2), T - 1)
        inside = (t[:, None] >= lo[None, :]) & (t[:, None] <= hi[None, :])
        pools.append(inside / (hi - lo + 1)[None, :] - np.eye(T))
    c["pool"] = np.concatenate(pools, axis=0)


def store_output(k, src):
    tok, _ = k.carve(WORK - TT * D, TT, D)
    with k.block() as block:
        @block.tensor
        def _(pe):
            for c in range(DC):
                for tt in range(TT):
                    mm = pe.transpose(k.ps[:, c, tt * P:(tt + 1) * P], src[:, c, tt * P:(tt + 1) * P], k.ident[:, :])
                mm.then_inc(k.tile_done.sem, 1)

        @block.vector
        def _(dve):
            for c in range(DC):
                dve.wait_ge(k.tile_done.sem, k.tile_done.at(c + 1))
                ins = dve.tensor_copy(tok[:, :, c * P:(c + 1) * P], k.ps[:, c, 0:T].rearrange("p (t f) -> p t f", t=TT))
            ins.then_inc(k.dve_done.sem, 1)

        @block.sync
        def _(sp):
            sp.wait_ge(k.dve_done.sem, k.dve_done.at(1))
            sp.dma_start(k.out[0].rearrange("(t p) d -> p t d", p=P), tok).then_inc(k.stored.sem, 16)
            sp.wait_ge(k.stored.sem, 16)


def program(nc, inputs, consts, out):
    with ExitStack() as ctx:
        k = Core(nc, ctx, inputs, consts)
        k.out = out
        for l in range(DEPTH):
            plan_first(k, l)
        if not STOP:
            for i in range(DEPTH):
                plan_second(k, i)
        load_params(k)
        for l in range(DEPTH):
            first_layer(k, l)
        if not STOP:
            second_block(k)
            final = k.h
        else:
            final = k.x
        store_output(k, final)


def constants():
    import numpy as np
    f = np.float32
    i = np.arange(P)
    same = (i[:, None] // HD) == (i[None, :] // HD)
    c = {"ident": np.eye(P), "ones": np.ones((P, P)), "head_ones": same}
    q = np.arange(T).reshape(TT, P).T[:, :, None]
    key = np.arange(T)[None, None, :]
    c["mask_a"] = np.where(key // CHUNK <= q // CHUNK, 0.0, FAR)
    strict = i[:, None] < i[None, :]
    c["mask_strict"] = strict
    diag = np.where(strict, 0.0, FAR)
    c["mask_b"] = np.concatenate([diag, np.zeros((P, P)), diag], axis=1)
    c["neg_tri"] = -(i[:, None] >= i[None, :]).astype(f)
    c["neg_ones"] = -np.ones((P, P))
    half = HD // 2
    inv = (f(10000.0) ** (-np.arange(0, HD, 2, dtype=f) / f(HD))).astype(f)
    c["inv_freq"] = np.broadcast_to(inv[None, :], (P, half))
    if not STOP:
        more_constants(c)
    return {n: np.ascontiguousarray(a, dtype=f) for n, a in c.items()}


NAMES = (
    "x p positions attn_norm w_in a_q_norm a_k_norm a_lambda a_subln c_q_norm c_k_norm idx_k_norm w_br_a w_br_b "
    "w_br_c w_out mlp_norm w_up w_down ple_norm w_ple_gate w_ple_proj c_2 ctx_2 c_ctx_2 ada_w_2 ada_b_2 norm_g_2 "
    "ffn1_w_gu_2 ffn1_w_down_2 ffn2_w_gu_2 ffn2_w_down_2 e_w_in_2 e_mu_2 e_w0_2 e_w_up_2 e_a0_2 e_a_up_2 e_g_up_2 "
    "e_k_k_2 e_k_a_2 e_r_k_2 e_gn_w_2 e_gn_b_2 e_w_out_2 o_w_in_2 o_conv_w_2 o_conv_b_2 o_cnorm_g_2 o_pool_w_2 "
    "o_pool_scale_2 o_w_out_2 final_g_2").split()


def kernel(**inputs):
    import numpy as np
    import concourse.bacc as bacc
    from concourse.bass_utils import run_bass_kernel_spmd

    nc = bacc.Bacc("TRN2", target_bir_lowering=False, num_devices=1)
    arrays, aps, consts = {}, {}, {}
    for name in NAMES:
        a = np.ascontiguousarray(inputs[name])
        arrays["in_" + name] = a
        aps[name] = nc.dram_tensor("in_" + name, a.shape, mybir.dt.from_np(a.dtype), kind="ExternalInput").ap()
    for name, a in constants().items():
        arrays["const_" + name] = a
        consts[name] = nc.dram_tensor("const_" + name, a.shape, F32, kind="ExternalInput").ap()
    out = nc.dram_tensor("out_0", (1, T, D), F32, kind="ExternalOutput").ap()
    program(nc, aps, consts, out)
    return run_bass_kernel_spmd(nc, [arrays], core_ids=[0]).results[0]["out_0"]
```

```python
import math
from contextlib import ExitStack

import concourse.bass as bass
from concourse import mybir

F32 = mybir.dt.float32
I32 = mybir.dt.int32
F32R = mybir.dt.float32r
ALU = mybir.AluOpType
ACT = mybir.ActivationFunctionType
AX_X = mybir.AxisListType.X

P = 128
D = 1024
DC = D // P
T = 256
TT = T // P
DEPTH = 2
HD = 64
CHUNK = 64
D_FF = 4 * D
D_FF_2 = 2816
N_MOD = 9
D_RWKV = 768
RC = D_RWKV // P
EPS = 1e-6
GN_EPS = 64e-5
DECAY_SCALE = 0.606531
TOPK = 64
SIDE = N_MOD * D // 512
CONV_WIDTH = 31
FAR = -1e30
TAKEN = -3e38
SLOTS = 3
SLOT = 4096
BANKS = 8
BANK = 512
WORK = 28650
LAM_INIT = [0.8 - 0.6 * math.exp(-0.3 * i) for i in range(DEPTH)]
STOP = False


class Counted:

    def __init__(self, handle):
        self.sem = handle
        self.base = 0

    def at(self, n):
        return self.base + n

    def passed(self, n):
        self.base += n


class Chain:

    def __init__(self, eng, counted):
        self.eng, self.counted = eng, counted

    def __call__(self, ins):
        self.counted.base += 1
        ins.then_inc(self.counted.sem, 1)
        self.eng.wait_ge(self.counted.sem, self.counted.base)


class Core:

    def __init__(self, nc, ctx, inputs, consts):
        self.nc, self.ctx, self.inp, self.con = nc, ctx, inputs, consts
        sb = self.sb
        self.x = sb("x", [P, DC, 2 * T])
        self.h = sb("h", [P, DC, 2 * T])
        self.ring = sb("ring", [P, SLOTS, SLOT])
        self.ps = ctx.enter_context(nc.psum_tensor("ps", [P, BANKS, BANK], F32))
        self.ident = sb("ident", [P, P])
        self.ones = sb("ones", [P, P])
        self.head_ones = sb("head_ones", [P, P])
        self.rstd = sb("rstd", [P, 2 * T])
        self.cond = sb("cond", [P, DC, 2])
        self.mods = sb("mods", [P, DEPTH, N_MOD * DC, 2])
        self.gs = sb("gs", [P, 3, DC, 2])
        self.half = sb("half", [P, 2, DC, 2])
        self.works = 0
        self.hi_made = self.counted("hi_made")
        self.lo_made = self.counted("lo_made")
        self.w_full = [self.counted(f"weights_arrived_{s}") for s in range(SLOTS)]
        self.w_used = self.counted("weights_used")
        self.tile_done = self.counted("tile_done")
        self.act_done = self.counted("act_done")
        self.dve_done = self.counted("dve_done")
        self.side_sum = self.counted("side_sum")
        self.side_read = self.counted("side_read")
        self.fill_done = self.counted("fill_done")
        self.fill_out = self.counted("fill_out")
        self.pool_done = self.counted("pool_done")
        self.pe_done = self.counted("pe_done")
        self.loaded = self.counted("loaded")
        self.stored = self.counted("stored")
        self.act_chain = self.counted("act_chain")
        self.dve_chain = self.counted("dve_chain")
        self.pool_chain = self.counted("pool_chain")
        self.slabs, self.slab_count = [], []
        self.issued = self.taken = 0
        self.used = {}

    def sb(self, name, shape, dt=F32):
        return self.ctx.enter_context(self.nc.sbuf_tensor(name, shape, dt))

    def open_work(self):
        self.works += 1
        self.work_ctx = ExitStack()
        self.work = self.work_ctx.enter_context(self.nc.sbuf_tensor(f"work_{self.works}", [P, WORK], F32))

    def counted(self, name):
        return Counted(self.ctx.enter_context(self.nc.semaphore(name)))

    def block(self):
        return self.nc.Block(no_gpsimd_drain=True)

    def carve(self, at, *shape):
        n = 1
        for s in shape:
            n *= s
        assert at + n <= WORK, (at, shape)
        v = self.work[:, at:at + n]
        if len(shape) == 2:
            v = v.rearrange("p (a b) -> p a b", a=shape[0])
        if len(shape) == 3:
            v = v.rearrange("p (a b c) -> p a b c", a=shape[0], b=shape[1])
        return v, at + n

    def plan(self, parts):
        kt = parts[0].shape[1]
        cols = sum(a.shape[2] for a in parts)
        assert kt * cols <= SLOT
        slot = len(self.slabs) % SLOTS
        before = self.slab_count[-SLOTS] if len(self.slabs) >= SLOTS else 0
        self.slabs.append((parts, kt, cols))
        self.slab_count.append(before + 16 * len(parts))

    def slab_view(self, j):
        _, kt, cols = self.slabs[j]
        return self.ring[:, j % SLOTS, 0:kt * cols].rearrange("p (k c) -> p k c", k=kt)

    def feed(self, sp):
        end = min(self.taken + SLOTS, len(self.slabs))
        while self.issued < end:
            j = self.issued
            if j >= SLOTS:
                sp.wait_ge(*self.used[j - SLOTS])
            c = 0
            for a in self.slabs[j][0]:
                sp.dma_start(self.slab_view(j)[:, :, c:c + a.shape[2]], a).then_inc(
                    self.w_full[j % SLOTS].sem, 16)
                c += a.shape[2]
            self.issued += 1

    def take(self, pe):
        j = self.taken
        pe.wait_ge(self.w_full[j % SLOTS].sem, self.slab_count[j])
        self.taken += 1
        return self.slab_view(j)

    def take_aside(self):
        j = self.taken
        self.taken += 1
        return self.slab_view(j), (self.w_full[j % SLOTS].sem, self.slab_count[j])

    def spent(self, by, count):
        self.used[self.taken - 1] = (by.sem, count)


class Side:

    def __init__(self, k, layer, at):
        self.k, self.layer = k, layer
        self.streams = 2 if layer == 0 else 1
        self.sums, _ = k.carve(at, 2 * 2, BANK)
        self.added = self.read = 0

    def add(self, dve, chain, view):
        k, j = self.k, self.added
        if j >= 2:
            dve.wait_ge(k.side_read.sem, k.side_read.at(j - 1))
        for kt in range(DC):
            for s in range(self.streams):
                out = self.sums[:, 2 * (j % 2) + s, :]
                c = k.cond[:, kt, s:s + 1]
                if kt == 0:
                    ins = dve.tensor_scalar(out, view[:, kt, :], c, None, ALU.mult)
                else:
                    ins = dve.scalar_tensor_tensor(out=out, in0=view[:, kt, :], scalar=c, in1=out,
                                                   op0=ALU.mult, op1=ALU.add)
            if kt < DC - 1:
                chain(ins)
        ins.then_inc(k.side_sum.sem, 1)
        self.added += 1

    def sum_rows(self, pe):
        k, j = self.k, self.read
        pe.wait_ge(k.side_sum.sem, k.side_sum.at(j + 1))
        for s in range(self.streams):
            row = s * SIDE + j
            mm = pe.matmul(k.ps[0:2 * SIDE, 7, :], k.onehot[:, 2 * SIDE - row:4 * SIDE - row],
                           self.sums[:, 2 * (j % 2) + s, :], start=(j == 0 and s == 0),
                           stop=(j == SIDE - 1 and s == self.streams - 1), skip_group_check=True)
        mm.then_inc(k.side_read.sem, 1)
        self.read += 1

    def finish(self):
        k, n = self.k, self.streams * SIDE
        rows = self.sums[0:2 * SIDE, 0, :]
        with k.block() as block:
            @block.scalar
            def _(act):
                act.activation(rows, k.ps[0:2 * SIDE, 7, :], ACT.Copy).then_inc(k.act_done.sem, 1)

            @block.tensor
            def _(pe):
                pe.wait_ge(k.act_done.sem, k.act_done.at(1))
                for m in range(4):
                    mm = pe.transpose(k.ps[:, 6, m * 2 * SIDE:(m + 1) * 2 * SIDE], rows[:, m * P:(m + 1) * P],
                                      k.ident[0:2 * SIDE, 0:2 * SIDE])
                mm.then_inc(k.pe_done.sem, 1)

            @block.vector
            def _(dve):
                dve.wait_ge(k.pe_done.sem, k.pe_done.at(1))
                b = k.col["ada_b_2"] + self.layer * N_MOD * DC
                bias = k.params[:, b:b + N_MOD * DC].rearrange("p (j m) -> p j m", m=4)
                for s in range(self.streams):
                    src = k.ps[:, 6, 0:4 * 2 * SIDE].rearrange("p (m s j) -> p s j m", m=4, s=2)[:, s]
                    dve.tensor_tensor(k.mods[:, self.layer, :, s].rearrange("p (j m) -> p j m", m=4), src, bias, ALU.add)
        k.act_done.passed(1)
        k.pe_done.passed(1)
        k.side_sum.passed(SIDE)
        k.side_read.passed(SIDE)


def gemm(k, groups, rhs, n, act=None, dve=None, side=None, aside=None, loads=(), late=(), width=None):
    width = width or (lambda m: n)
    tiles = [cols // P for _, cols in groups]
    banks = BANKS - 1 if side else BANKS
    last = k.dve_done if dve else k.act_done
    views = []
    with k.block() as block:
        @block.tensor
        def _(pe):
            m0, i = 0, 0
            for (slabs, cols), nt in zip(groups, tiles):
                kt0 = 0
                for s in range(slabs):
                    w = k.take(pe)
                    kts = w.shape[1]
                    for m in range(nt):
                        bank = (m0 + m) % banks
                        if s == 0 and m0 + m >= banks:
                            pe.wait_ge(last.sem, last.at(m0 + m - banks + 1))
                        for kt in range(kts):
                            nm = width(m0 + m)
                            mm = pe.matmul(k.ps[:, bank, 0:nm], w[:, kt, m * P:(m + 1) * P],
                                           rhs(kt0 + kt)[:, 0:nm], start=(s == 0 and kt == 0),
                                           stop=(s == slabs - 1 and kt == kts - 1))
                        if s == slabs - 1:
                            mm.then_inc(k.tile_done.sem, 1)
                    if s == slabs - 1:
                        k.spent(k.tile_done, k.tile_done.at(m0 + nt))
                    else:
                        mm.then_inc(k.w_used.sem, 1)
                        k.w_used.passed(1)
                        k.spent(k.w_used, k.w_used.base)
                    kt0 += kts
                    if side:
                        while side[0].read < side[0].added + len(views):
                            side[0].sum_rows(pe)
                        for _ in range(side[1][i]):
                            views.append((i, k.take_aside()))
                            k.spent(k.side_sum, k.side_sum.at(side[0].added + len(views)))
                    i += 1
                m0 += nt
            if side:
                while side[0].read < side[0].added + len(views):
                    side[0].sum_rows(pe)

        if act:
            @block.scalar
            def _(eng):
                chain = Chain(eng, k.act_chain)
                for m in range(sum(tiles)):
                    eng.wait_ge(k.tile_done.sem, k.tile_done.at(m + 1))
                    act(eng, chain, m, k.ps[:, m % banks, 0:width(m)]).then_inc(k.act_done.sem, 1)

        if aside:
            @block.vector
            def _(eng):
                chain = Chain(eng, k.dve_chain)
                for m in sorted(aside):
                    if m >= 0:
                        eng.wait_ge(k.act_done.sem, k.act_done.at(m + 1))
                    aside[m](eng, chain)

        if dve or side:
            @block.vector
            def _(eng):
                chain = Chain(eng, k.dve_chain)
                m, i = 0, 0
                for (slabs, cols), nt in zip(groups, tiles):
                    for s in range(slabs):
                        while views and views[0][0] < i:
                            view, arrived = views.pop(0)[1]
                            eng.wait_ge(*arrived)
                            side[0].add(eng, chain, view)
                        i += 1
                    for m in range(m, m + nt):
                        eng.wait_ge(k.tile_done.sem, k.tile_done.at(m + 1))
                        if act:
                            eng.wait_ge(k.act_done.sem, k.act_done.at(m + 1))
                        dve(eng, chain, m, k.ps[:, m % banks, 0:n]).then_inc(k.dve_done.sem, 1)
                    m += 1
                while views:
                    view, arrived = views.pop(0)[1]
                    eng.wait_ge(*arrived)
                    side[0].add(eng, chain, view)

        @block.sync
        def _(sp):
            for dst, src in loads:
                sp.dma_start(dst, src).then_inc(k.loaded.sem, 16)
            if late:
                sp.wait_ge(k.dve_done.sem, k.dve_done.at(1))
            for dst, src in late:
                sp.dma_start(dst, src).then_inc(k.loaded.sem, 16)
            k.feed(sp)
            if loads or late:
                sp.wait_ge(k.loaded.sem, k.loaded.at(16 * (len(loads) + len(late))))
    k.loaded.passed(16 * (len(loads) + len(late)))
    k.tile_done.passed(sum(tiles))
    if act:
        k.act_done.passed(sum(tiles))
    if dve:
        k.dve_done.passed(sum(tiles))


def gemm_tokens(k, outs):
    with k.block() as block:
        @block.tensor
        def _(pe):
            for i in range(len(outs)):
                w = k.take(pe)
                cols = w.shape[2]
                for tt in range(TT):
                    u = i * TT + tt
                    if u >= BANKS:
                        pe.wait_ge(k.act_done.sem, k.act_done.at(u - BANKS + 1))
                    for c in range(DC):
                        mm = pe.matmul(k.ps[:, u % BANKS, 0:cols], k.h[:, c, tt * P:(tt + 1) * P],
                                       w[:, c, :], start=(c == 0), stop=(c == DC - 1))
                    mm.then_inc(k.tile_done.sem, 1)
                k.spent(k.tile_done, k.tile_done.at(TT * (i + 1)))

        @block.scalar
        def _(act):
            for i, out in enumerate(outs):
                for tt in range(TT):
                    u = i * TT + tt
                    act.wait_ge(k.tile_done.sem, k.tile_done.at(u + 1))
                    act.activation(out[:, tt, :], k.ps[:, u % BANKS, 0:out.shape[2]], ACT.Copy).then_inc(
                        k.act_done.sem, 1)

        @block.sync
        def _(sp):
            k.feed(sp)
    k.tile_done.passed(TT * len(outs))
    k.act_done.passed(TT * len(outs))


def rmsnorm(k, src, dst, tiles, n, gain, shift=None, width=None, eps=EPS):
    width = width or tiles * P
    with k.block() as block:
        @block.scalar
        def _(act):
            for c in range(tiles):
                act.activation(dst[:, c, 0:n], src[:, c, 0:n], ACT.Square).then_inc(k.act_done.sem, 1)
            act.wait_ge(k.dve_done.sem, k.dve_done.at(1))
            act.activation(k.rstd[:, 0:n], k.rstd[:, 0:n], ACT.Sqrt).then_inc(k.act_done.sem, 1)
            if shift:
                for c in range(tiles):
                    act.wait_ge(k.dve_done.sem, k.dve_done.at(2 + c))
                    for col, (a, b) in shift(c):
                        act.activation(dst[:, c, a:b], dst[:, c, a:b], ACT.Identity, bias=col)

        @block.tensor
        def _(pe):
            for c in range(tiles):
                pe.wait_ge(k.act_done.sem, k.act_done.at(c + 1))
                mm = pe.matmul(k.ps[:, 0, 0:n], k.ones[:, :], dst[:, c, 0:n],
                               start=(c == 0), stop=(c == tiles - 1))
            mm.then_inc(k.pe_done.sem, 1)

        @block.vector
        def _(dve):
            chain = Chain(dve, k.dve_chain)
            dve.wait_ge(k.pe_done.sem, k.pe_done.at(1))
            chain(dve.tensor_scalar(k.rstd[:, 0:n], k.ps[:, 0, 0:n], 1.0 / width, eps, ALU.mult, ALU.add))
            dve.reciprocal(k.rstd[:, 0:n], k.rstd[:, 0:n]).then_inc(k.dve_done.sem, 1)
            dve.wait_ge(k.act_done.sem, k.act_done.at(tiles + 1))
            for c in range(tiles):
                for col, (a, b) in gain(c):
                    ins = dve.scalar_tensor_tensor(out=dst[:, c, a:b], in0=src[:, c, a:b], scalar=col,
                                                   in1=k.rstd[:, a:b], op0=ALU.mult, op1=ALU.mult)
                ins.then_inc(k.dve_done.sem, 1)
    k.act_done.passed(tiles + 1)
    k.pe_done.passed(1)
    k.dve_done.passed(1 + tiles)


def load_params(k):
    i = k.inp
    rows = []
    for name in ("attn_norm", "mlp_norm", "ple_norm", "norm_g_2", "a_subln", "c_2", "c_ctx_2", "ada_b_2",
                 "e_mu_2", "e_w0_2", "e_a0_2", "e_k_k_2", "e_k_a_2", "e_r_k_2", "e_gn_w_2", "e_gn_b_2",
                 "o_conv_b_2", "o_cnorm_g_2", "o_pool_scale_2", "final_g_2"):
        a = i[name]
        while len(a.shape) > 1:
            a = a.rearrange("a b c -> (a b) c") if len(a.shape) == 3 else a.rearrange("a b -> (a b)")
        rows.append((name, a.rearrange("(r c) -> r c", c=P)))
    total = sum(a.shape[0] for _, a in rows)
    nb = (total + P - 1) // P
    k.params = k.sb("params", [P, total])
    k.conv_w = k.sb("conv_w", [P, RC, CONV_WIDTH])
    k.onehot = k.sb("onehot", [P, 4 * SIDE])
    k.posi = k.sb("posi", [P, TT], I32)
    k.hgain = k.sb("hgain", [P, DEPTH, 5, HD])
    k.lam = k.sb("lam", [P, DEPTH, 4])
    k.sincos = k.sb("sincos", [P, 2, TT, HD // 2])
    names1 = ("mask_a", "mask_strict", "mask_b", "neg_tri", "neg_ones", "inv_freq")
    k.consts1 = {name: k.sb(name, list(k.con[name].shape)) for name in names1}
    k.open_work()
    stage, end = k.carve(0, nb, P)
    k.col = {}
    at, jobs = 0, []
    for name, a in rows:
        n = a.shape[0]
        k.col[name] = at
        done = 0
        while done < n:
            m = min(n - done, P - (at + done) % P)
            jobs.append((stage[(at + done) % P:(at + done) % P + m, (at + done) // P, :], a[done:done + m, :]))
            done += m
        at += n
    conv, end = k.carve(end, 2 * RC // 2, P)
    small = [(k.ident[:, :], k.con["ident"]), (k.ones[:, :], k.con["ones"]),
             (k.head_ones[:, :], k.con["head_ones"])]
    for c in range(RC):
        jobs.append((conv[0:CONV_WIDTH, c, :], i["o_conv_w_2"][0, :, c * P:(c + 1) * P]))
    small.append((k.onehot[:, :], k.con["onehot"]))
    for name in names1:
        a = k.con[name]
        small.append((k.consts1[name][:], a))
    for l in range(DEPTH):
        for j, name in enumerate(("a_q_norm", "a_k_norm", "c_q_norm", "c_k_norm", "idx_k_norm")):
            small.append((k.hgain[:, l, j, :], i[name][l, :].partition_broadcast(P)))
    k.lam_in, end = k.carve(end, DEPTH, 4 * HD)
    for l in range(DEPTH):
        small.append((k.lam_in[:, l, :], i["a_lambda"][l].rearrange("a b -> (a b)").partition_broadcast(P)))
    ang, end = k.carve(end, 2 * TT, HD // 2)
    turns, end = k.carve(end, 2 * TT, HD // 2)
    posf, end = k.carve(end, TT)
    prod, end = k.carve(end, 2, HD)
    tok, end = k.carve(end, 2 * TT, D)
    n_load = len(jobs) + len(small) + 3
    ncopy = nb + RC
    with k.block() as block:
        @block.sync
        def _(sp):
            for dst, src in small[0:1] + jobs:
                sp.dma_start(dst, src).then_inc(k.loaded.sem, 16)
            sp.dma_start(tok[:, 0:TT, :], i["x"].rearrange("a (t p) d -> p (a t) d", p=P)).then_inc(k.loaded.sem, 16)
            sp.dma_start(tok[:, TT:2 * TT, :], i["ctx_2"].rearrange("a (t p) d -> p (a t) d", p=P)).then_inc(k.loaded.sem, 16)
            sp.dma_start(k.posi[:, :], i["positions"].rearrange("a (t p) -> p (a t)", p=P),
                         allow_slow_non_contiguous=True).then_inc(k.loaded.sem, 16)
            for dst, src in small[1:]:
                sp.dma_start(dst, src).then_inc(k.loaded.sem, 16)
            k.feed(sp)

        @block.tensor
        def _(pe):
            pe.wait_ge(k.loaded.sem, 16 * n_load)
            n_rows = [min(P, total - b * P) for b in range(nb)]
            for b in range(nb):
                mm = pe.transpose(k.ps[:, b % BANKS, 0:n_rows[b]], stage[0:n_rows[b], b, :],
                                  k.ident[0:n_rows[b], 0:n_rows[b]])
            assert nb < BANKS
            for c in range(RC):
                mm = pe.transpose(k.ps[:, nb, c * 32:c * 32 + CONV_WIDTH], conv[0:CONV_WIDTH, c, :],
                                  k.ident[0:CONV_WIDTH, 0:CONV_WIDTH])
            mm.then_inc(k.pe_done.sem, 1)
            for c in range(DC):
                if c == 0:
                    pe.wait_ge(k.dve_done.sem, k.dve_done.at(1))
                for tt in range(2 * TT):
                    mm = pe.transpose(k.ps[:, c, tt * P:(tt + 1) * P], tok[:, tt, c * P:(c + 1) * P],
                                      k.ident[:, :])
                mm.then_inc(k.pe_done.sem, 1)

        @block.vector
        def _(dve):
            chain = Chain(dve, k.dve_chain)
            dve.wait_ge(k.pe_done.sem, k.pe_done.at(1))
            for b in range(nb):
                w = min(P, total - b * P)
                dve.tensor_copy(k.params[:, b * P:b * P + w], k.ps[:, b, 0:w])
            dve.tensor_copy(k.conv_w[:, :, :], k.ps[:, nb, 0:RC * 32].rearrange("p (c w) -> p c w", c=RC)[:, :, 0:CONV_WIDTH]).then_inc(
                k.dve_done.sem, 1)
            for c in range(DC):
                dve.wait_ge(k.pe_done.sem, k.pe_done.at(c + 2))
                dve.tensor_copy(k.x[:, c, :], k.ps[:, c, :])
            dve.wait_ge(k.loaded.sem, 16 * n_load)
            chain(dve.tensor_copy(posf[:, :], k.posi[:, :]))
            inv = k.consts1["inv_freq"]
            for tt in range(TT):
                dve.tensor_scalar(ang[:, tt, :], inv[:, :], posf[:, tt:tt + 1], None, ALU.mult)
                ins = dve.tensor_scalar(ang[:, TT + tt, :], inv[:, :], posf[:, tt:tt + 1], None, ALU.mult)
            chain(ins)
            a, t = ang[:, :, :], turns[:, :, :]
            big = 1.5 * 2 ** 23
            chain(dve.tensor_scalar(turns[:, 0:TT, :], ang[:, 0:TT, :], 0.15915494309189535, None, ALU.mult))
            chain(dve.tensor_scalar(turns[:, TT:2 * TT, :], ang[:, TT:2 * TT, :], 0.15915494309189535, 0.25, ALU.mult, ALU.add))
            chain(dve.tensor_scalar(t, t, big, None, ALU.add))
            chain(dve.tensor_scalar(t, t, big, None, ALU.subtract))
            for part in (6.28125, 0.0019350051879882812, 3.0199157663446e-07):
                chain(dve.scalar_tensor_tensor(out=a, in0=t, scalar=-part, in1=a, op0=ALU.mult, op1=ALU.add))
            chain(dve.tensor_scalar(ang[:, TT:2 * TT, :], ang[:, TT:2 * TT, :], 1.5707963267948966, None, ALU.add))
            chain(dve.tensor_scalar(a, a, 3.1415925, -3.1415925, ALU.min, ALU.max))
            dve.tensor_copy(a, a).then_inc(k.dve_done.sem, 1)
            for l in range(DEPTH):
                li = k.lam_in[:, l, :].rearrange("p (a b c) -> p a b c", a=2, b=2)
                chain(dve.tensor_tensor(prod[:, :, :], li[:, :, 0, :], li[:, :, 1, :], ALU.mult))
                chain(dve.tensor_reduce(k.lam[:, l, 0:2], prod[:, :, :], AX_X, ALU.add))
            dve.tensor_copy(k.lam[:, :, 2:4], k.lam[:, :, 0:2]).then_inc(k.dve_done.sem, 1)
            dve.wait_ge(k.act_done.sem, k.act_done.at(3))
            c, cc = k.col["c_2"], k.col["c_ctx_2"]
            dve.tensor_tensor(k.cond[:, :, 0], k.cond[:, :, 0], k.params[:, c:c + DC], ALU.mult)
            dve.tensor_tensor(k.cond[:, :, 1], k.cond[:, :, 1], k.params[:, cc:cc + DC], ALU.mult)
            for l in range(DEPTH):
                chain(dve.tensor_tensor(k.lam[:, l, 0:1], k.lam[:, l, 3:4], k.lam[:, l, 2:3], ALU.subtract))
                chain(dve.tensor_scalar(k.lam[:, l, 1:2], k.lam[:, l, 0:1], -LAM_INIT[l], None, ALU.add))

        @block.scalar
        def _(act):
            c, cc = k.col["c_2"], k.col["c_ctx_2"]
            act.wait_ge(k.dve_done.sem, k.dve_done.at(1))
            act.activation(k.cond[:, :, 0], k.params[:, c:c + DC], ACT.Sigmoid)
            act.activation(k.cond[:, :, 1], k.params[:, cc:cc + DC], ACT.Sigmoid).then_inc(k.act_done.sem, 1)
            act.wait_ge(k.dve_done.sem, k.dve_done.at(2))
            act.activation(k.sincos[:, :, :, :].rearrange("p a t f -> p (a t) f"), ang[:, :, :], ACT.Sin).then_inc(k.act_done.sem, 1)
            act.wait_ge(k.dve_done.sem, k.dve_done.at(3))
            act.activation(k.lam[:, :, 2:4], k.lam[:, :, 2:4], ACT.Exp).then_inc(k.act_done.sem, 1)
    k.loaded.passed(16 * n_load)
    k.pe_done.passed(1 + DC)
    k.dve_done.passed(3)
    k.act_done.passed(3)


def gate_fill(k, gates, slabs):
    def pe_part(pe):
        for i, g in enumerate(slabs):
            w = k.take(pe)
            for m in range(4):
                if i:
                    pe.wait_ge(k.fill_out.sem, k.fill_out.at(4 * (i - 1) + m + 1))
                for kt in range(DC):
                    mm = pe.matmul(k.ps[:, 4 + m, 0:T], w[:, kt, m * P:(m + 1) * P], k.h[:, kt, 0:T],
                                   start=(kt == 0), stop=(kt == DC - 1))
                mm.then_inc(k.fill_done.sem, 1)
            k.spent(k.fill_done, k.fill_done.at(4 * (i + 1)))

    def act_part(act):
        for i, g in enumerate(slabs):
            for m in range(4):
                act.wait_ge(k.fill_done.sem, k.fill_done.at(4 * i + m + 1))
                act.activation(gates[:, 4 * g + m, :], k.ps[:, 4 + m, 0:T], ACT.Sigmoid).then_inc(k.fill_out.sem, 1)
        k.fill_done.passed(4 * len(slabs))
        k.fill_out.passed(4 * len(slabs))
    return pe_part, act_part


def head_norm_rope(k, heads, gain, tmp, rs, fill=None):
    _, tt, nh, _ = heads.shape
    half = HD // 2

    def wide(a, tk):
        return a[:, tk, :].rearrange("p (h o) -> p h o", o=1).broadcast_to([P, nh, HD])

    def angle(s):
        return [k.sincos[:, s, t, :].rearrange("p (o f) -> p o f", o=1).broadcast_to([P, nh, half]) for t in range(TT)]

    with k.block() as block:
        if fill:
            @block.tensor
            def _(pe):
                fill[0](pe)

            @block.sync
            def _(sp):
                k.feed(sp)

        if gain is not None:
            @block.scalar
            def _(act):
                for t in range(TT):
                    act.activation(tmp[:, t], heads[:, t], ACT.Square).then_inc(k.act_done.sem, 1)
                act.wait_ge(k.dve_done.sem, k.dve_done.at(1))
                act.activation(rs, rs, ACT.Sqrt).then_inc(k.act_done.sem, 1)
                if fill:
                    fill[1](act)

        @block.vector
        def _(dve):
            chain = Chain(dve, k.dve_chain)
            if gain is not None:
                for t in range(TT):
                    dve.wait_ge(k.act_done.sem, k.act_done.at(t + 1))
                    ins = dve.tensor_reduce(rs[:, t, :], tmp[:, t], AX_X, ALU.add)
                chain(ins)
                chain(dve.tensor_scalar(rs, rs, 1.0 / HD, EPS, ALU.mult, ALU.add))
                dve.reciprocal(rs, rs).then_inc(k.dve_done.sem, 1)
                dve.wait_ge(k.act_done.sem, k.act_done.at(TT + 1))
                for t in range(TT):
                    ins = dve.tensor_tensor(heads[:, t], heads[:, t], wide(rs, t), ALU.mult)
                chain(ins)
                g = gain.rearrange("p (o f) -> p o f", o=1).broadcast_to([P, nh, HD])
                for t in range(TT):
                    ins = dve.tensor_tensor(heads[:, t], heads[:, t], g, ALU.mult)
                chain(ins)
            sin, cos = angle(0), angle(1)
            for t in range(TT):
                x1, x2 = heads[:, t, :, 0:half], heads[:, t, :, half:HD]
                t1, t2 = tmp[:, t, :, 0:half], tmp[:, t, :, half:HD]
                dve.tensor_tensor(t1, x2, sin[t], ALU.mult)
                chain(dve.tensor_tensor(t2, x1, sin[t], ALU.mult))
                dve.tensor_tensor(x1, x1, cos[t], ALU.mult)
                chain(dve.tensor_tensor(x2, x2, cos[t], ALU.mult))
                dve.tensor_tensor(x1, x1, t1, ALU.subtract)
                ins = dve.tensor_tensor(x2, x2, t2, ALU.add)
            chain(ins)
    if gain is not None:
        k.act_done.passed(TT + 1)
        k.dve_done.passed(1)


def turn(k, jobs):
    tiles = []
    for src, out, scale in jobs:
        for f in range(out.shape[1]):
            tiles.append((src, out, scale, f))
    with k.block() as block:
        @block.tensor
        def _(pe):
            for u, (src, out, scale, f) in enumerate(tiles):
                if u >= BANKS:
                    pe.wait_ge(k.act_done.sem, k.act_done.at(u - BANKS + 1))
                for tt in range(TT):
                    mm = pe.transpose(k.ps[:, u % BANKS, tt * P:(tt + 1) * P], src[:, tt, f * P:(f + 1) * P],
                                      k.ident[:, :])
                mm.then_inc(k.tile_done.sem, 1)

        @block.scalar
        def _(act):
            for u, (src, out, scale, f) in enumerate(tiles):
                act.wait_ge(k.tile_done.sem, k.tile_done.at(u + 1))
                act.activation(out[:, f, :], k.ps[:, u % BANKS, 0:T], ACT.Copy, scale=scale).then_inc(k.act_done.sem, 1)
    k.tile_done.passed(len(tiles))
    k.act_done.passed(len(tiles))


def softmax_scores(k, qT, kT, mask, e0, e1, sums, nmax):
    def part(n):
        if n < 8:
            return 0, n, n % 2, (n // 2) * P, P
        m = n - 8
        return 1, m, 2 + 2 * (m // 4) + m % 2, (m % 4 // 2) * T, T

    with k.block() as block:
        @block.tensor
        def _(pe):
            for n in range(16):
                qt, h, bank, off, nk = part(n)
                r = (h % 2) * HD
                mm = pe.matmul(k.ps[:, bank, off:off + nk], qT[r:r + HD, h // 2, qt * P:(qt + 1) * P],
                               kT[r:r + HD, h // 2, 0:nk], start=True, stop=True)
                if off + nk == BANK:
                    mm.then_inc(k.tile_done.sem, 1)

        @block.vector
        def _(dve):
            chain = Chain(dve, k.dve_chain)
            for b in range(6):
                dve.wait_ge(k.tile_done.sem, k.tile_done.at(b + 1))
                if b < 2:
                    e, hs, nh, nk, m = e0, slice(b, 8, 2), 4, P, mask[:, 0, 0:P]
                else:
                    h0 = 4 * ((b - 2) // 2) + b % 2
                    e, hs, nh, nk, m = e1, slice(h0, h0 + 3, 2), 2, T, mask[:, 1, :]
                m = m.rearrange("p (o f) -> p o f", o=1).broadcast_to([P, nh, nk])
                s = k.ps[:, b, :].rearrange("p (h f) -> p h f", h=nh)
                chain(dve.tensor_tensor(e[:, hs, :], s, m, ALU.add))
                qt = 0 if b < 2 else 1
                dve.tensor_reduce(nmax[:, qt, hs], e[:, hs, :], AX_X, ALU.max,
                                  negate=True).then_inc(k.dve_done.sem, 1)
            dve.wait_ge(k.act_done.sem, k.act_done.at(16))
            chain(dve.reciprocal(sums, sums))

        @block.scalar
        def _(act):
            for n in range(16):
                qt, h, bank, _, _ = part(n)
                act.wait_ge(k.dve_done.sem, k.dve_done.at(bank + 1))
                e = e0 if qt == 0 else e1
                act.activation(e[:, h, :], e[:, h, :], ACT.Exp, bias=nmax[:, qt, h:h + 1],
                               accum_out=sums[:, qt, h:h + 1]).then_inc(k.act_done.sem, 1)
    k.tile_done.passed(6)
    k.dve_done.passed(6)
    k.act_done.passed(16)


def turn_probs(k, nh, p0, p1, pT):
    n = nh * 3
    nb = n // 4
    with k.block() as block:
        @block.tensor
        def _(pe):
            for u in range(n):
                h, s = u // 3, u % 3
                src = p0[:, h, :] if s == 0 else p1[:, h, (s - 1) * P:s * P]
                mm = pe.transpose(k.ps[:, u // 4, (u % 4) * P:(u % 4 + 1) * P], src, k.ident[:, :])
                if u % 4 == 3:
                    mm.then_inc(k.tile_done.sem, 1)

        @block.scalar
        def _(act):
            flat = pT.rearrange("p h s q -> p (h s q)")
            for b in range(nb):
                act.wait_ge(k.tile_done.sem, k.tile_done.at(b + 1))
                act.activation(flat[:, b * BANK:(b + 1) * BANK], k.ps[:, b, :], ACT.Copy).then_inc(k.act_done.sem, 1)
            act.wait_ge(k.act_done.sem, k.act_done.at(nb))
    k.tile_done.passed(nb)
    k.act_done.passed(nb)


def values(k, nh, width, v, pT, out):
    per = P // width
    with k.block() as block:
        @block.tensor
        def _(pe):
            for h in range(nh):
                r = (h % per) * width
                bank = h // per
                o = k.ps[r:r + width, bank, 0:T]
                cols = slice(h * width, (h + 1) * width)
                pe.matmul(o, v[:, 0, cols], pT[:, h, 0:2, :].rearrange("p s q -> p (s q)"), start=True, stop=False)
                mm = pe.matmul(k.ps[r:r + width, bank, P:T], v[:, 1, cols], pT[:, h, 2, :], start=False, stop=True)
                if h % per == per - 1:
                    mm.then_inc(k.tile_done.sem, 1)

        @block.scalar
        def _(act):
            for b in range(nh // per):
                act.wait_ge(k.tile_done.sem, k.tile_done.at(b + 1))
                act.activation(out[:, b, :], k.ps[:, b, 0:T], ACT.Copy)
    k.tile_done.passed(nh // per)


def scale_probs(k, nh, p0, p1, rs):
    with k.block() as block:
        @block.vector
        def _(dve):
            for h in range(nh):
                dve.tensor_scalar(p0[:, h, :], p0[:, h, :], rs[:, 0, h:h + 1], None, ALU.mult)
                dve.tensor_scalar(p1[:, h, :], p1[:, h, :], rs[:, 1, h:h + 1], None, ALU.mult)


def differ_probs(k, layer, p0, p1, rs, nrs):
    with k.block() as block:
        @block.vector
        def _(dve):
            chain = Chain(dve, k.dve_chain)
            chain(dve.tensor_scalar(nrs, rs, k.lam[:, layer, 1:2], None, ALU.mult))
            for h in range(4):
                for qt, p in enumerate((p0, p1)):
                    chain(dve.tensor_scalar(p[:, 2 * h, :], p[:, 2 * h, :], rs[:, qt, 2 * h:2 * h + 1], None, ALU.mult))
                    chain(dve.scalar_tensor_tensor(out=p[:, h, :], in0=p[:, 2 * h + 1, :],
                                                   scalar=nrs[:, qt, 2 * h + 1:2 * h + 2],
                                                   in1=p[:, 2 * h, :], op0=ALU.mult, op1=ALU.add))


def subln(k, layer, y, sq):
    g = k.col["a_subln"] + layer
    with k.block() as block:
        @block.scalar
        def _(act):
            for c in range(4):
                act.activation(sq[:, c, :], y[:, c, :], ACT.Square).then_inc(k.act_done.sem, 1)
            for c in range(4):
                act.wait_ge(k.dve_done.sem, k.dve_done.at(c + 1))
                act.activation(sq[:, c, :], sq[:, c, :], ACT.Sqrt).then_inc(k.act_done.sem, 1)

        @block.tensor
        def _(pe):
            for c in range(4):
                pe.wait_ge(k.act_done.sem, k.act_done.at(c + 1))
                pe.matmul(k.ps[:, c, 0:T], k.ones[:, :], sq[:, c, :], start=True, stop=True).then_inc(k.pe_done.sem, 1)

        @block.vector
        def _(dve):
            chain = Chain(dve, k.dve_chain)
            for c in range(4):
                dve.wait_ge(k.pe_done.sem, k.pe_done.at(c + 1))
                chain(dve.tensor_scalar(sq[:, c, :], k.ps[:, c, 0:T], 1.0 / P, EPS, ALU.mult, ALU.add))
                dve.reciprocal(sq[:, c, :], sq[:, c, :]).then_inc(k.dve_done.sem, 1)
            for c in range(4):
                dve.wait_ge(k.act_done.sem, k.act_done.at(5 + c))
                chain(dve.scalar_tensor_tensor(out=y[:, c, :], in0=y[:, c, :], scalar=k.params[:, g:g + 1],
                                               in1=sq[:, c, :], op0=ALU.mult, op1=ALU.mult))
                dve.tensor_scalar(y[:, c, :], y[:, c, :], 1.0 - LAM_INIT[layer], None, ALU.mult)
    k.act_done.passed(8)
    k.pe_done.passed(4)
    k.dve_done.passed(4)


def stick_breaking(k, qT, kT, v, y, sp, at, tmp):
    NZ = T + P
    with k.block() as block:
        @block.tensor
        def _(pe):
            for h in range(8):
                r = (h % 2) * HD
                pe.matmul(k.ps[:, h, 0:T], kT[r:r + HD, h // 2, 0:P], qT[r:r + HD, h // 2, :], start=True, stop=True)
                pe.matmul(k.ps[:, h, T:NZ], kT[r:r + HD, h // 2, P:T], qT[r:r + HD, h // 2, P:T],
                          start=False, stop=True, skip_group_check=True).then_inc(k.tile_done.sem, 1)
            for h in range(8):
                pe.wait_ge(k.dve_done.sem, k.dve_done.at(h + 1))
                pe.matmul(k.ps[:, h, 0:T], k.consts1["neg_tri"][:, :], sp[:, h, 0:T], start=False, stop=True, skip_group_check=True)
                pe.matmul(k.ps[:, h, P:T], k.consts1["neg_ones"][:, :], sp[:, h, T:NZ], start=False, stop=True, skip_group_check=True)
                pe.matmul(k.ps[:, h, T:NZ], k.consts1["neg_tri"][:, :], sp[:, h, T:NZ], start=False, stop=True,
                          skip_group_check=True).then_inc(k.tile_done.sem, 1)

        @block.scalar
        def _(act):
            chain = Chain(act, k.act_chain)
            for h in range(8):
                act.wait_ge(k.tile_done.sem, k.tile_done.at(h + 1))
                if h >= 3:
                    act.wait_ge(k.dve_done.sem, k.dve_done.at(h - 2))
                chain(act.activation(tmp[:, h % 3, :], k.ps[:, h, 0:NZ], ACT.Abs))
                chain(act.activation(tmp[:, h % 3, :], tmp[:, h % 3, :], ACT.Exp, scale=-1.0))
                act.activation(tmp[:, h % 3, :], tmp[:, h % 3, :], ACT.Ln, bias=1.0).then_inc(k.act_done.sem, 1)
            for h in range(8):
                act.wait_ge(k.dve_done.sem, k.dve_done.at(9 + h))
                act.activation(at[:, h, :], at[:, h, :], ACT.Exp).then_inc(k.act_done.sem, 1)

        @block.vector
        def _(dve):
            chain = Chain(dve, k.dve_chain)
            strict = k.consts1["mask_strict"][:, :].rearrange("p (o f) -> p o f", o=1).broadcast_to([P, 2, P])
            for h in range(8):
                dve.wait_ge(k.act_done.sem, k.act_done.at(h + 1))
                chain(dve.scalar_tensor_tensor(out=sp[:, h, :], in0=k.ps[:, h, 0:NZ], scalar=0.0, in1=tmp[:, h % 3, :],
                                               op0=ALU.max, op1=ALU.add))
                diag = sp[:, h, :].rearrange("p (a f) -> p a f", a=3)[:, 0:3:2, :]
                dve.tensor_tensor(diag, diag, strict, ALU.mult).then_inc(k.dve_done.sem, 1)
            for h in range(8):
                dve.wait_ge(k.tile_done.sem, k.tile_done.at(9 + h))
                dve.tensor_tensor(at[:, h, :], k.ps[:, h, 0:NZ], k.consts1["mask_b"][:, :], ALU.add).then_inc(k.dve_done.sem, 1)
    k.tile_done.passed(16)
    k.act_done.passed(16)
    k.dve_done.passed(16)
    with k.block() as block:
        @block.tensor
        def _(pe):
            for h in range(8):
                r = (h % 2) * HD
                o = k.ps[r:r + HD, h // 2, :]
                pe.matmul(o[:, 0:T], v[:, 0, h * HD:(h + 1) * HD], at[:, h, 0:T], start=True, stop=False)
                mm = pe.matmul(o[:, P:T], v[:, 1, h * HD:(h + 1) * HD], at[:, h, T:NZ], start=False, stop=True)
                if h % 2:
                    mm.then_inc(k.tile_done.sem, 1)

        @block.scalar
        def _(act):
            for b in range(4):
                act.wait_ge(k.tile_done.sem, k.tile_done.at(b + 1))
                act.activation(y[:, b, :], k.ps[:, b, 0:T], ACT.Copy)
    k.tile_done.passed(4)


def pick_keys(k, iqT, ikT, iw, score, picked, relu, best, fill):
    with k.block() as block:
        @block.tensor
        def _(pe):
            for n in range(8):
                qt, h = n // 4, n % 4
                r = (h % 2) * HD
                nk = P if qt == 0 else T
                bank = 2 * qt + h % 2
                off = h // 2 * nk
                mm = pe.matmul(k.ps[:, bank, off:off + nk], iqT[r:r + HD, h // 2, qt * P:(qt + 1) * P],
                               ikT[r:r + HD, 0, 0:nk], start=True, stop=True)
                if h >= 2:
                    mm.then_inc(k.tile_done.sem, 1)
            fill[0](pe)

        @block.sync
        def _(sp):
            k.feed(sp)

        @block.scalar
        def _(act):
            for b in range(4):
                act.wait_ge(k.tile_done.sem, k.tile_done.at(b + 1))
                w = T if b < 2 else 2 * T
                act.activation(relu[:, b, 0:w], k.ps[:, b, 0:w], ACT.Relu).then_inc(k.act_done.sem, 1)
            fill[1](act)

        @block.vector
        def _(dve):
            chain = Chain(dve, k.dve_chain)
            chain(dve.tensor_scalar(iw, iw, 0.5, None, ALU.mult))
            for qt, nk in ((0, P), (1, T)):
                s = score[:, qt, 0:nk]
                dve.wait_ge(k.act_done.sem, k.act_done.at(2 if qt == 0 else 4))
                for h in range(4):
                    r = relu[:, 2 * qt + h % 2, h // 2 * nk:(h // 2 + 1) * nk]
                    w = iw[:, qt, h:h + 1]
                    if h == 0:
                        chain(dve.tensor_scalar(s, r, w, None, ALU.mult))
                    else:
                        chain(dve.scalar_tensor_tensor(out=s, in0=r, scalar=w, in1=s, op0=ALU.mult, op1=ALU.add))
                chain(dve.tensor_tensor(s, s, k.consts1["mask_a"][:, qt, 0:nk], ALU.add))
                for _ in range(TOPK // 8):
                    chain(dve.max(best, s))
                    chain(dve.match_replace(s, best, s, TAKEN))
                m = picked[:, qt, 0:nk]
                chain(dve.tensor_scalar(m, s, TAKEN, 1.0, ALU.is_equal, ALU.subtract))
                dve.tensor_scalar(m, m, -FAR, None, ALU.mult)
    k.tile_done.passed(4)
    k.act_done.passed(4)


def wslab(a, r0, r1, c0, c1):
    return a[r0:r1, c0:c1].rearrange("(k p) c -> p k c", p=P)


A_Q, A_K, A_VC, B_Q, B_K, B_VC, C_Q, C_K, C_VC = (512 * j for j in range(9))
IDX_C = 9 * 512
IDX_W = 256 + HD + 4
GATE_C = IDX_C + IDX_W


SIDE_PLAN = [2, 1, 1, 1, 1, 1, 1, 1]


def plan_first(k, l):
    w = k.inp["w_in"][l]
    def cols(c0, c1):
        k.plan([wslab(w, 0, D, c0, c1)])

    def gate(j):
        cols(GATE_C + 512 * j, GATE_C + 512 * (j + 1))
    for c0 in (A_Q, A_K, A_VC):
        cols(c0, c0 + 512)
    gate(0), gate(1)
    for c0 in (B_Q, B_K, B_VC, C_Q, C_K, C_VC):
        cols(c0, c0 + 512)
    gate(2), gate(3)
    cols(IDX_C, GATE_C)
    gate(4), gate(5)
    for name in ("w_br_a", "w_br_b", "w_br_c"):
        k.plan([wslab(k.inp[name][l], 0, 512, 0, D)])
    for j in range(2):
        k.plan([wslab(k.inp["w_out"][l], 0, D, 512 * j, 512 * (j + 1))])
    side = 0
    for j in range(D_FF // 512):
        k.plan([wslab(k.inp["w_up"][l], 0, D, 512 * j, 512 * (j + 1))])
        for _ in range(SIDE_PLAN[j]):
            k.plan([wslab(k.inp["ada_w_2"][l], 0, D, 512 * side, 512 * (side + 1))])
            side += 1
    for j in range(2):
        for r in range(D_FF // D):
            k.plan([wslab(k.inp["w_down"][l], D * r, D * (r + 1), 512 * j, 512 * (j + 1))])
            for _ in range(SIDE_PLAN[j * (D_FF // D) + r]):
                k.plan([wslab(k.inp["ada_w_2"][l], 0, D, 512 * side, 512 * (side + 1))])
                side += 1
    assert side == SIDE
    for j in range(2):
        k.plan([wslab(k.inp["w_ple_gate"][l], 0, D, 512 * j, 512 * (j + 1))])
    k.plan([wslab(k.inp["w_ple_proj"][l], 0, T, 0, D)])


def column(k, name, at):
    c = k.col[name] + at
    return k.params[:, c:c + 1]


def add_to_x(k, n=T, scale=None):
    def dve(eng, chain, m, ps):
        if scale is None:
            return eng.tensor_tensor(k.x[:, m, 0:n], k.x[:, m, 0:n], ps, ALU.add)
        for col, (a, b) in scale(m):
            ins = eng.scalar_tensor_tensor(out=k.x[:, m, a:b], in0=ps[:, a:b], scalar=col, in1=k.x[:, m, a:b],
                                           op0=ALU.mult, op1=ALU.add)
        return ins
    return dve


def first_layer(k, l):
    gates, end = k.carve(0, 24, T)
    y, end = k.carve(end, 12, T)
    v0 = end
    tm, end = k.carve(end, 3 * TT, 512)
    qT, end = k.carve(end, 4, T)
    kT, end = k.carve(end, 4, T)
    free = end

    rmsnorm(k, k.x, k.h, DC, T, lambda c: [(column(k, "attn_norm", l * DC + c), (0, T))])

    def heads(j, nh=8):
        return tm[:, j * TT:(j + 1) * TT, 0:nh * HD].rearrange("p t (h f) -> p t h f", h=nh)

    def part(j):
        return tm[:, j * TT:(j + 1) * TT, :]

    for branch in range(3):
        ybr = y[:, 4 * branch:4 * branch + 4, :]
        gemm_tokens(k, [part(0), part(1), part(2)])
        tmp, _ = k.carve(free, TT, 512)
        tmp = tmp.rearrange("p t (h f) -> p t h f", h=8)
        rs, _ = k.carve(free + TT * 512, TT, 8)
        if branch != 1:
            g = 0 if branch == 0 else 2
            head_norm_rope(k, heads(0), k.hgain[:, l, g, :], tmp, rs, gate_fill(k, gates, [g]))
            head_norm_rope(k, heads(1), k.hgain[:, l, g + 1, :], tmp, rs, gate_fill(k, gates, [g + 1]))
        turn(k, [(part(0), qT, HD ** -0.5), (part(1), kT, 1.0)])
        e0, end = k.carve(free, 8, P)
        e1, end = k.carve(end, 8, T)
        pT, end = k.carve(end, 8 * 3, P)
        pT = pT.rearrange("p (h s) q -> p h s q", s=3)
        sums, end = k.carve(end, 2, 8)
        nmax, end = k.carve(end, 2, 8)
        if branch == 0:
            softmax_scores(k, qT, kT, k.consts1["mask_a"], e0, e1, sums, nmax)
            differ_probs(k, l, e0, e1, sums, nmax)
            turn_probs(k, 4, e0, e1, pT[:, 0:4])
            values(k, 4, 2 * HD, part(2), pT, ybr)
            sq, _ = k.carve(free, 4, T)
            subln(k, l, ybr, sq)
        elif branch == 1:
            sp, end = k.carve(free, 8, T + P)
            at, end = k.carve(end, 8, T + P)
            tmp3, end = k.carve(end, 3, T + P)
            stick_breaking(k, qT, kT, part(2), ybr, sp, at, tmp3)
        else:
            idx = tm[:, 0:TT, 0:IDX_W]
            gemm_tokens(k, [idx])
            iq = tm[:, 0:TT, 0:256].rearrange("p t (h f) -> p t h f", h=4)
            ik = tm[:, 0:TT, 256:256 + HD].rearrange("p t (h f) -> p t h f", h=1)
            iw = tm[:, 0:TT, 256 + HD:IDX_W]
            itmp, end2 = k.carve(free, TT, 256)
            irs, end2 = k.carve(end2, TT, 1)
            head_norm_rope(k, iq, None, itmp.rearrange("p t (h f) -> p t h f", h=4), None)
            head_norm_rope(k, ik, k.hgain[:, l, 4, :], itmp[:, :, 0:HD].rearrange("p t (h f) -> p t h f", h=1), irs)
            iqT, end2 = k.carve(end2, 2, T)
            ikT, end2 = k.carve(end2, 1, T)
            pair, end2 = k.carve(end2, TT, P)
            with k.block() as block:
                @block.vector
                def _(dve):
                    dve.tensor_copy(pair[:, :, 0:HD], tm[:, 0:TT, 256:256 + HD])
                    dve.tensor_copy(pair[:, :, HD:P], tm[:, 0:TT, 256:256 + HD])
            turn(k, [(tm[:, 0:TT, 0:256], iqT, HD ** -0.5), (pair, ikT, 1.0)])
            picked = tm[:, TT:2 * TT, 0:T]
            score = tm[:, TT:2 * TT, T:2 * T]
            relu, end2 = k.carve(end2, 4, BANK)
            best, end2 = k.carve(end2, 8)
            pick_keys(k, iqT, ikT, iw, score, picked, relu, best, gate_fill(k, gates, [4, 5]))
            softmax_scores(k, qT, kT, picked, e0, e1, sums, nmax)
            scale_probs(k, 8, e0, e1, sums)
            turn_probs(k, 8, e0, e1, pT)
            values(k, 8, HD, part(2), pT, ybr)

    for branch in range(3):
        def merge(eng, chain, m, ps, branch=branch):
            g = gates[:, branch * DC + m, :]
            if branch == 0:
                return eng.tensor_tensor(k.h[:, m, 0:T], ps, g, ALU.mult)
            chain(eng.tensor_tensor(g, ps, g, ALU.mult))
            return eng.tensor_tensor(k.h[:, m, 0:T], k.h[:, m, 0:T], g, ALU.add)
        gemm(k, [(1, D)], lambda kt, branch=branch: y[:, 4 * branch + kt, :], T, dve=merge)
    gemm(k, [(1, 512)] * 2, lambda kt: k.h[:, kt, 0:T], T, dve=add_to_x(k))

    up, end = k.carve(0, D_FF // P, T)
    side = Side(k, l, end)
    rmsnorm(k, k.x, k.h, DC, T, lambda c: [(column(k, "mlp_norm", l * DC + c), (0, T))])
    gemm(k, [(1, 512)] * (D_FF // 512), lambda kt: k.h[:, kt, 0:T], T,
         act=lambda eng, chain, m, ps: eng.activation(up[:, m, :], ps, ACT.Relu),
         dve=lambda eng, chain, m, ps: eng.tensor_tensor(up[:, m, :], up[:, m, :], up[:, m, :], ALU.mult),
         side=(side, SIDE_PLAN))
    gemm(k, [(D_FF // D, 512)] * 2, lambda kt: up[:, kt, :], T, dve=add_to_x(k), side=(side, SIDE_PLAN))
    side.finish()

    gate, end = k.carve(0, DC, T)
    ptok, end = k.carve(end, TT, T)
    pT, end = k.carve(end, TT, T)
    rmsnorm(k, k.x, k.h, DC, T, lambda c: [(column(k, "ple_norm", l * DC + c), (0, T))])
    with k.block() as block:
        @block.sync
        def _(sp):
            sp.dma_start(ptok, k.inp["p"][l, 0].rearrange("(t p) d -> p t d", p=P)).then_inc(k.loaded.sem, 16)
            sp.wait_ge(k.loaded.sem, k.loaded.at(16))
    k.loaded.passed(16)
    turn(k, [(ptok, pT, 1.0)])
    gemm(k, [(1, 512)] * 2, lambda kt: k.h[:, kt, 0:T], T,
         act=lambda eng, chain, m, ps: eng.activation(gate[:, m, :], ps, ACT.Sigmoid))

    def gated(eng, chain, m, ps):
        chain(eng.tensor_tensor(gate[:, m, :], ps, gate[:, m, :], ALU.mult))
        return eng.tensor_tensor(k.x[:, m, 0:T], k.x[:, m, 0:T], gate[:, m, :], ALU.add)
    gemm(k, [(1, D)], lambda kt: pT[:, kt, :], T, dve=gated)


NF2 = D_FF_2 // P
FF_COLS = 256
R0, K0, V0, WA, GD, FO = 0, RC, 2 * RC, 3 * RC, 3 * RC + 1, 3 * RC + 2
MIX_E = FO + 2
LEVELS = 6
NB = 2 * TT
NC2 = 2 * NB


def plan_ffn(k, gu, down, i):
    g, d = k.inp[gu][i], k.inp[down][i]
    for j in range(D_FF_2 // FF_COLS):
        c = FF_COLS * j
        k.plan([wslab(g, 0, D, c, c + FF_COLS), wslab(g, 0, D, D_FF_2 + c, D_FF_2 + c + FF_COLS)])
    for j in range(2):
        for r in range(0, D_FF_2, D):
            k.plan([wslab(d, r, min(r + D, D_FF_2), 512 * j, 512 * (j + 1))])


def plan_cols(k, w, cols):
    for c in range(0, cols, 512):
        k.plan([wslab(w, 0, D, c, min(c + 512, cols))])


def plan_second(k, i):
    for _ in range(2 if i == 0 else 1):
        plan_ffn(k, "ffn1_w_gu_2", "ffn1_w_down_2", i)
    if i == 0:
        plan_cols(k, k.inp["e_w_in_2"][0], MIX_E * P)
        plan_cols(k, k.inp["e_w_out_2"][0], D)
    else:
        w = k.inp["o_w_in_2"][0]
        for c in range(0, D_RWKV, 2 * P):
            k.plan([wslab(w, 0, D, c, c + 2 * P), wslab(w, 0, D, D_RWKV + c, D_RWKV + c + 2 * P)])
        k.plan([wslab(w, 0, D, 2 * D_RWKV, 14 * P)])
        plan_cols(k, k.inp["o_w_out_2"][0], D)
    plan_ffn(k, "ffn2_w_gu_2", "ffn2_w_down_2", i)


def column_groups(cols):
    return [(1, min(512, cols - c)) for c in range(0, cols, 512)]


def modulation(k, i, both):
    k.mod = k.mods[:, i]
    with k.block() as block:
        @block.vector
        def _(dve):
            for j in range(3):
                g = k.col["norm_g_2"] + (3 * i + j) * DC
                for s in range(2 if both else 1):
                    sc = k.mod[:, (3 * j + 1) * DC:(3 * j + 2) * DC, s]
                    dve.scalar_tensor_tensor(out=k.gs[:, j, :, s], in0=sc, scalar=1.0, in1=k.params[:, g:g + DC],
                                             op0=ALU.add, op1=ALU.mult)
                    if j != 1:
                        dve.tensor_scalar(k.half[:, j // 2, :, s], k.mod[:, (3 * j + 2) * DC:(3 * j + 3) * DC, s],
                                          0.5, None, ALU.mult)


def streams(n):
    return [(0, (0, T))] + ([(1, (T, 2 * T))] if n > T else [])


def modulate(k, j, n):
    rmsnorm(k, k.x, k.h, DC, n,
            lambda c: [(k.gs[:, j, c, s:s + 1], r) for s, r in streams(n)],
            shift=lambda c: [(k.mod[:, 3 * j * DC + c, s:s + 1], r) for s, r in streams(n)])


def half_ffn(k, j, s):
    here = slice(s * T, (s + 1) * T)
    rmsnorm(k, k.x[:, :, here], k.h[:, :, here], DC, T,
            lambda c: [(k.gs[:, j, c, s:s + 1], (0, T))],
            shift=lambda c: [(k.mod[:, 3 * j * DC + c, s:s + 1], (0, T))])
    k.work_ctx.close()
    with ExitStack() as ctx:
        split_ffn(k, j, s, ctx)
    k.open_work()


def split_ffn(k, j, stream, ctx):
    HALF, UNITS, COLS = 4, 3, 512
    n_up, per = D_FF_2 // FF_COLS, COLS // P
    works = k.works

    def pair(name, shape):
        return [ctx.enter_context(k.nc.sbuf_tensor(f"{name}_{part}_{works}", shape, F32R)) for part in ("hi", "lo")]

    w_hi, w_lo = pair("w", [P, UNITS, HALF, COLS])
    h_hi, h_lo = pair("h", [P, DC, T])
    u_hi, u_lo = pair("u", [P, NF2, T])
    here = slice(stream * T, (stream + 1) * T)
    h = k.h[:, :, here]
    other = k.h[:, :, slice((1 - stream) * T, (2 - stream) * T)]
    s = [other[:, 2 * g:2 * g + 2, :] for g in range(2)]
    t = [other[:, 4 + 2 * g:6 + 2 * g, :] for g in range(2)]

    units, groups = [], []
    for slabs in [1] * n_up + [3] * (D // COLS):
        mine, kt0 = [], 0
        for _ in range(slabs):
            view, arrived = k.take_aside()
            kts = view.shape[1]
            cut = (kts + 1) // 2
            for a, b in ((0, cut), (cut, kts)):
                mine.append(len(units))
                units.append((view[:, a:b, :], arrived, kt0 + a))
            kt0 += kts
            k.spent(k.lo_made, k.lo_made.at(len(units) + 1))
        groups.append(mine)

    ahead = [range(mine[0] + (2 if g else 0), min(mine[-1] + 3, len(units))) for g, mine in enumerate(groups)]

    def hi(i):
        return w_hi[:, i % UNITS, 0:units[i][0].shape[1], :]

    def lo(i):
        return w_lo[:, i % UNITS, 0:units[i][0].shape[1], :]

    def banks(g, a, b):
        return k.ps[:, per * (g % 2) + a:per * (g % 2) + b, 0:T]

    with k.block() as block:
        @block.sync
        def _(sp):
            k.feed(sp)

        @block.tensor
        def _(pe):
            for g, mine in enumerate(groups):
                if g >= n_up:
                    pe.wait_ge(k.dve_done.sem, k.dve_done.at(2 * n_up))
                elif g >= 2:
                    pe.wait_ge(k.dve_done.sem, k.dve_done.at(2 * (g - 2) + 1))
                x_hi, x_lo = (h_hi, h_lo) if g < n_up else (u_hi, u_lo)
                for i in mine:
                    pe.wait_ge(k.lo_made.sem, k.lo_made.at(i + 2))
                    w, _, kt0 = units[i]
                    kts = w.shape[1]
                    for m in range(per):
                        o = k.ps[:, per * (g % 2) + m, 0:T]
                        cols = slice(m * P, (m + 1) * P)
                        for kt in range(kts):
                            first, final = kt0 + kt == 0, i == mine[-1] and kt == kts - 1
                            pe.matmul(o, hi(i)[:, kt, cols], x_hi[:, kt0 + kt, :], start=first, stop=False)
                            pe.matmul(o, hi(i)[:, kt, cols], x_lo[:, kt0 + kt, :], start=False, stop=False)
                            mm = pe.matmul(o, lo(i)[:, kt, cols], x_hi[:, kt0 + kt, :], start=False, stop=final)
                    mm.then_inc(k.tile_done.sem, 1)

        @block.scalar
        def _(act):
            def split(mine):
                for i in mine:
                    act.wait_ge(*units[i][1])
                    if i >= UNITS:
                        act.wait_ge(k.tile_done.sem, k.tile_done.at(i - UNITS + 1))
                    act.activation(hi(i), units[i][0], ACT.Copy).then_inc(k.hi_made.sem, 1)

            act.activation(h_hi[:, :, :], h, ACT.Copy).then_inc(k.hi_made.sem, 1)
            for g, mine in enumerate(groups):
                split(ahead[g])
                if g < n_up:
                    act.wait_ge(k.tile_done.sem, k.tile_done.at(mine[-1] + 1))
                    if g >= 2:
                        act.wait_ge(k.dve_done.sem, k.dve_done.at(2 * (g - 2) + 1))
                    act.activation(s[g % 2], banks(g, 0, 2), ACT.Sigmoid).then_inc(k.act_done.sem, 1)
                    act.wait_ge(k.dve_done.sem, k.dve_done.at(2 * g + 1))
                    act.activation(u_hi[:, 2 * g:2 * g + 2, :], t[g % 2], ACT.Copy).then_inc(k.act_done.sem, 1)

        @block.vector
        def _(dve):
            chain = Chain(dve, k.dve_chain)

            def split(mine):
                for i in mine:
                    dve.wait_ge(k.hi_made.sem, k.hi_made.at(i + 2))
                    dve.tensor_tensor(lo(i), units[i][0], hi(i), ALU.subtract).then_inc(k.lo_made.sem, 1)

            dve.wait_ge(k.hi_made.sem, k.hi_made.at(1))
            dve.tensor_tensor(h_lo[:, :, :], h, h_hi[:, :, :], ALU.subtract).then_inc(k.lo_made.sem, 1)
            for g, mine in enumerate(groups):
                split(ahead[g])
                if g < n_up:
                    dve.wait_ge(k.act_done.sem, k.act_done.at(2 * g + 1))
                    chain(dve.tensor_tensor(t[g % 2], banks(g, 0, 2), s[g % 2], ALU.mult))
                    dve.tensor_tensor(t[g % 2], banks(g, 2, 4), t[g % 2], ALU.mult).then_inc(k.dve_done.sem, 1)
                    dve.wait_ge(k.act_done.sem, k.act_done.at(2 * g + 2))
                    dve.tensor_tensor(u_lo[:, 2 * g:2 * g + 2, :], t[g % 2], u_hi[:, 2 * g:2 * g + 2, :],
                                      ALU.subtract).then_inc(k.dve_done.sem, 1)
                else:
                    dve.wait_ge(k.tile_done.sem, k.tile_done.at(mine[-1] + 1))
                    for m in range(per):
                        c = per * (g - n_up) + m
                        dve.scalar_tensor_tensor(out=k.x[:, c, here], in0=k.ps[:, per * (g % 2) + m, 0:T],
                                                 scalar=k.half[:, j // 2, c, stream:stream + 1], in1=k.x[:, c, here],
                                                 op0=ALU.mult, op1=ALU.add)
    k.tile_done.passed(len(units))
    k.hi_made.passed(len(units) + 1)
    k.lo_made.passed(len(units) + 1)
    k.act_done.passed(2 * n_up)
    k.dve_done.passed(2 * n_up)


def load(k, sp, jobs):
    for dst, src in jobs:
        sp.dma_start(dst, src).then_inc(k.loaded.sem, 16)
    if jobs:
        sp.wait_ge(k.loaded.sem, k.loaded.at(16 * len(jobs)))


def load_constants(k, jobs):
    with k.block() as block:
        @block.sync
        def _(sp):
            load(k, sp, jobs)
    k.loaded.passed(16 * len(jobs))


def fourier(k, u, out, cs, cn, at, jobs):
    mid, end = k.carve(at, 2 * TT, 2 * P)
    with k.block() as block:
        @block.sync
        def _(sp):
            load(k, sp, jobs)

        @block.tensor
        def _(pe):
            for f in range(2):
                for tt in range(TT):
                    pe.matmul(k.ps[:, f * TT + tt, 0:2 * P], u[:, f, tt * P:(tt + 1) * P], cs,
                              start=True, stop=True).then_inc(k.tile_done.sem, 1)
            for f in range(2):
                pe.wait_ge(k.act_done.sem, k.act_done.at((f + 1) * TT))
                for q in range(2 * TT):
                    part, tt = q // TT, q % TT
                    mm = pe.matmul(k.ps[:, 4 + f, 0:T], mid[:, f * TT + tt, part * P:(part + 1) * P],
                                   cn[:, q, :], start=(q == 0), stop=(q == 2 * TT - 1))
                mm.then_inc(k.tile_done.sem, 1)

        @block.scalar
        def _(act):
            for q in range(4):
                act.wait_ge(k.tile_done.sem, k.tile_done.at(q + 1))
                act.activation(mid[:, q, :], k.ps[:, q, 0:2 * P], ACT.Copy).then_inc(k.act_done.sem, 1)
            for f in range(2):
                act.wait_ge(k.tile_done.sem, k.tile_done.at(5 + f))
                act.activation(out[:, f, :], k.ps[:, 4 + f, 0:T], ACT.Copy)
    k.tile_done.passed(6)
    k.act_done.passed(4)
    k.loaded.passed(16 * len(jobs))


def token_shift(k, dve, chain, z, c, tmp, sequences):
    t = tmp[:, c % 2, 0:sequences * T].rearrange("p (s t) -> p s t", s=sequences)
    v = z[:, c, 0:sequences * T].rearrange("p (s t) -> p s t", s=sequences)
    dve.tensor_copy(t[:, :, T - 1:T], v[:, :, T - 2:T - 1])
    dve.tensor_copy(t[:, :, 0:1], v[:, :, 1:2])
    chain(dve.tensor_tensor(t[:, :, 1:T - 1], v[:, :, 0:T - 2], v[:, :, 2:T], ALU.add))
    chain(dve.scalar_tensor_tensor(out=t, in0=t, scalar=0.5, in1=v, op0=ALU.mult, op1=ALU.subtract))
    chain(dve.scalar_tensor_tensor(out=v, in0=t, scalar=column(k, "e_mu_2", c), in1=v, op0=ALU.mult, op1=ALU.add))


def head_norms(k, z):
    tmp, _ = k.carve(k.free, 2, 2 * T)
    with k.block() as block:
        @block.vector
        def _(dve):
            chain = Chain(dve, k.dve_chain)
            for p in range(RC):
                if p >= 2:
                    dve.wait_ge(k.pe_done.sem, k.pe_done.at(p - 1))
                t = tmp[:, p % 2, :]
                chain(dve.tensor_scalar(t, z[:, K0 + p, :], column(k, "e_k_k_2", p), None, ALU.mult))
                dve.tensor_tensor(t, t, t, ALU.mult).then_inc(k.dve_done.sem, 1)
            dve.wait_ge(k.act_done.sem, k.act_done.at(1))
            chain(dve.tensor_scalar(k.rnorm, k.rnorm, 1e-12, None, ALU.max))
            dve.reciprocal(k.rnorm, k.rnorm)

        @block.tensor
        def _(pe):
            for p in range(RC):
                pe.wait_ge(k.dve_done.sem, k.dve_done.at(p + 1))
                pe.matmul(k.ps[0:2 * RC, 0, :], k.pick[:, p, :], tmp[:, p % 2, :], start=(p == 0),
                          stop=(p == RC - 1)).then_inc(k.pe_done.sem, 1)

        @block.scalar
        def _(act):
            act.wait_ge(k.pe_done.sem, k.pe_done.at(RC))
            act.activation(k.rnorm, k.ps[0:2 * RC, 0, :], ACT.Sqrt).then_inc(k.act_done.sem, 1)
    k.dve_done.passed(RC)
    k.pe_done.passed(RC)
    k.act_done.passed(1)


def scan_tile(k, p, z, y, at):
    n = 2 * T
    DIRS = range(2)
    HQ = [(h, q) for h in range(2) for q in range(2)]
    r, kz, v = z[:, R0 + p, :], z[:, K0 + p, :], z[:, V0 + p, :]
    wa = z[:, WA, :]
    kk, end = k.carve(at, n)
    vt, end = k.carve(end, NB, P)
    coef, end = k.carve(end, T)
    AR, BK, At, Bt, Kt, gend, tot, state, RBK, sq = ([None, None] for _ in range(10))
    for d in DIRS:
        AR[d], end = k.carve(end, 2, n)
        BK[d], end = k.carve(end, 2, n)
        At[d], end = k.carve(end, NB, P)
        Bt[d], end = k.carve(end, NB, P)
        Kt[d], end = k.carve(end, NB, P)
        gend[d], end = k.carve(end, NC2)
        tot[d], end = k.carve(end, NC2)
        RBK[d], end = k.carve(end, 2, 2 * T // 2)
        state[d], end = k.carve(end, NC2, HD)
        sq[d] = []
        for _ in range(7):
            s, end = k.carve(end, 2 * NB, HD)
            sq[d].append(s)
    MT, N, TM, TT_, Q = ([sq[d][i] for d in DIRS] for i in range(5))
    off = [[sq[d][5], sq[d][6]] for d in DIRS]
    E = Q
    Z = [off[d][0][:, 0:2 * TT, :] for d in DIRS]
    lw = [flat(sq[d][0]) for d in DIRS]
    cum = [flat(sq[d][1]) for d in DIRS]
    a = [flat(sq[d][2]) for d in DIRS]
    kd = [flat(sq[d][3]) for d in DIRS]
    step = [BK[d][:, 0, :].rearrange("p (c f) -> p c f", c=NC2) for d in DIRS]
    inp = [BK[d][:, 1, :].rearrange("p (c f) -> p c f", c=NC2) for d in DIRS]
    r2 = [AR[d][:, 0, 0:T] for d in DIRS]
    m = k.masks

    def rows(h):
        return slice(h * HD, (h + 1) * HD)

    def bl(b):
        return slice(b * P, (b + 1) * P)

    def ch(c):
        return slice(c * CHUNK, (c + 1) * CHUNK)

    def wide(mask, nb):
        return mask.rearrange("p (o f) -> p o f", o=1).broadcast_to([P, nb, HD])

    def bank(i, a0, nb):
        return k.ps[:, i, a0:a0 + nb * HD].rearrange("p (b f) -> p b f", b=nb)

    with k.block() as block:
        @block.tensor
        def _(pe):
            pe.matmul(k.ps[:, 1, 0:n], k.spread[p], k.rnorm, start=True, stop=True).then_inc(k.pe_done.sem, 1)
            for d in DIRS:
                up = k.up_w[d * RC + p]
                pe.matmul(k.ps[:, 2 + d, 0:n], up[0:HD, :], wa[0:HD, :], start=True, stop=True).then_inc(k.pe_done.sem, 1)
            for d in DIRS:
                up = k.up_w[d * RC + p]
                pe.matmul(k.ps[:, 4 + d, 0:n], up[HD:P, :], wa[HD:P, :], start=True, stop=True).then_inc(k.pe_done.sem, 1)
            for b in range(NB):
                mm = pe.transpose(k.ps[:, 0, bl(b)], v[:, bl(b)], k.ident[:, :])
            mm.then_inc(k.pe_done.sem, 1)

        @block.scalar
        def _(act):
            for d in DIRS:
                act.wait_ge(k.pe_done.sem, k.pe_done.at(2 + d))
                act.activation(lw[d], k.ps[:, 2 + d, 0:n], ACT.Sigmoid, bias=column(k, "e_w0_2", d * RC + p)).then_inc(
                    k.act_done.sem, 1)
            for d in DIRS:
                act.wait_ge(k.pe_done.sem, k.pe_done.at(4 + d))
                act.activation(a[d], k.ps[:, 4 + d, 0:n], ACT.Sigmoid, bias=column(k, "e_a0_2", d * RC + p)).then_inc(
                    k.act_done.sem, 1)
            act.wait_ge(k.pe_done.sem, k.pe_done.at(6))
            act.activation(vt, k.ps[:, 0, :].rearrange("p (b f) -> p b f", b=NB), ACT.Copy)
            for d in DIRS:
                act.wait_ge(k.dve_done.sem, k.dve_done.at(1 + d))
                act.activation(BK[d][:, 0, :], cum[d], ACT.Exp, scale=-1.0)
                act.activation(AR[d][:, 1, 0:T], cum[d][:, 0:T], ACT.Exp)
                act.activation(gend[d], tot[d], ACT.Exp)
                act.activation(AR[d][:, 0, :], lw[d], ACT.Exp).then_inc(k.act_done.sem, 1)

        @block.vector
        def _(dve):
            chain = Chain(dve, k.dve_chain)
            dve.wait_ge(k.pe_done.sem, k.pe_done.at(1))
            chain(dve.scalar_tensor_tensor(out=kk, in0=k.ps[:, 1, 0:n], scalar=column(k, "e_k_k_2", p), in1=kz,
                                           op0=ALU.mult, op1=ALU.mult))
            for d in DIRS:
                dve.wait_ge(k.act_done.sem, k.act_done.at(1 + d))
                chain(dve.tensor_scalar(lw[d], lw[d], -DECAY_SCALE, None, ALU.mult))
                chain(dve.tensor_tensor_scan(cum[d], k.chunk_start, lw[d], 0.0, ALU.mult, ALU.add))
                c3 = cum[d].rearrange("p (c t) -> p c t", c=NC2)
                chain(dve.tensor_copy(tot[d], c3[:, :, CHUNK - 1]))
                if d == 1:
                    chain(dve.tensor_tensor(cum[d], lw[d], cum[d], ALU.subtract))
                    chain(dve.tensor_tensor(c3, c3, tot[d].rearrange("p (c o) -> p c o", o=1).broadcast_to(
                        [P, NC2, CHUNK]), ALU.add))
                dve.tensor_tensor(lw[d], cum[d], lw[d], ALU.subtract).then_inc(k.dve_done.sem, 1)
            for d in DIRS:
                dve.wait_ge(k.act_done.sem, k.act_done.at(3 + d))
                chain(dve.tensor_scalar(kd[d], a[d], 1.0, column(k, "e_k_a_2", p), ALU.subtract, ALU.mult))
                dve.scalar_tensor_tensor(out=kd[d], in0=kd[d], scalar=1.0, in1=kz, op0=ALU.add, op1=ALU.mult)
                chain(dve.tensor_tensor(a[d], a[d], kk, ALU.mult))
            chain(dve.tensor_tensor(coef, kd[0][:, 0:T], kd[1][:, 0:T], ALU.add))
            dve.scalar_tensor_tensor(out=coef, in0=coef, scalar=column(k, "e_r_k_2", p), in1=r[:, 0:T],
                                     op0=ALU.mult, op1=ALU.mult)
            for d in DIRS:
                dve.wait_ge(k.act_done.sem, k.act_done.at(5 + d))
                dve.tensor_tensor(BK[d][:, 1, :], BK[d][:, 0, :], kd[d], ALU.mult)
                dve.tensor_tensor(AR[d][:, 0, :], AR[d][:, 0, :], kk, ALU.mult)
                chain(dve.tensor_tensor(AR[d][:, 1, 0:T], AR[d][:, 1, 0:T], r[:, 0:T], ALU.mult))
                dve.tensor_tensor(BK[d][:, 0, :], BK[d][:, 0, :], a[d], ALU.mult)
    k.pe_done.passed(6)
    k.act_done.passed(6)
    k.dve_done.passed(2)

    with k.block() as block:
        @block.tensor
        def _(pe):
            u = 0
            for d in DIRS:
                for s in (AR[d][:, 0, :], BK[d][:, 0, :], BK[d][:, 1, :]):
                    if u >= BANKS:
                        pe.wait_ge(k.act_done.sem, k.act_done.at(u - BANKS + 1))
                    for b in range(NB):
                        mm = pe.transpose(k.ps[:, u % BANKS, bl(b)], s[:, bl(b)], k.ident[:, :])
                    mm.then_inc(k.tile_done.sem, 1)
                    u += 1
                for h in range(2):
                    if u == 10:
                        pe.wait_ge(k.act_done.sem, k.act_done.at(3))
                    if u > 10:
                        pe.wait_ge(k.dve_done.sem, k.dve_done.at(u - BANKS - 2))
                    for c in range(NC2):
                        mm = pe.matmul(
                            k.ps[rows(c % 2), u % BANKS, :].rearrange("p (a f) -> p a f", a=2)[:, :, ch(c // 2)],
                            AR[d][rows(h), 0, ch(c)], BK[d][rows(h), :, ch(c)], start=True, stop=True)
                    mm.then_inc(k.tile_done.sem, 1)
                    u += 1
                    if u > 10:
                        pe.wait_ge(k.dve_done.sem, k.dve_done.at(u - BANKS - 2))
                    for c in range(NC2):
                        o = k.ps[rows(c % 2), u % BANKS, :]
                        if c < NC2 // 2:
                            pe.matmul(o.rearrange("p (a f) -> p a f", a=2)[:, :, ch(c // 2)],
                                      BK[d][rows(h), 0, ch(c)], AR[d][rows(h), :, ch(c)], start=True, stop=True)
                            pe.matmul(o[:, T + P:T + 2 * P][:, ch(c // 2)], BK[d][rows(h), 1, ch(c)],
                                      AR[d][rows(h), 1, ch(c)], start=True, stop=True)
                        else:
                            mm = pe.matmul(o[:, ch(c // 2)], BK[d][rows(h), 0, ch(c)], AR[d][rows(h), 0, ch(c)],
                                           start=True, stop=True)
                    mm.then_inc(k.tile_done.sem, 1)
                    u += 1

        @block.scalar
        def _(act):
            for d in DIRS:
                for i, dst in enumerate((At[d], Bt[d], Kt[d])):
                    u = 7 * d + i
                    act.wait_ge(k.tile_done.sem, k.tile_done.at(u + 1))
                    act.activation(dst, k.ps[:, u % BANKS, :].rearrange("p (b f) -> p b f", b=NB), ACT.Copy).then_inc(
                        k.act_done.sem, 1)

        @block.vector
        def _(dve):
            chain = Chain(dve, k.dve_chain)
            for d in DIRS:
                for h in range(2):
                    u = 7 * d + 3 + 2 * h
                    hb = slice(NB * h, NB * (h + 1))
                    dve.wait_ge(k.tile_done.sem, k.tile_done.at(u + 1))
                    dve.tensor_tensor(TM[d][:, hb, :], bank(u % BANKS, 0, NB), wide(m[d]["level0"], NB), ALU.mult)
                    dve.tensor_tensor(N[d][:, hb, :], bank(u % BANKS, T, NB), wide(m[d]["strict"], NB), ALU.mult).then_inc(
                        k.dve_done.sem, 1)
                    u += 1
                    dve.wait_ge(k.tile_done.sem, k.tile_done.at(u + 1))
                    dve.tensor_copy(MT[d][:, hb, :], bank(u % BANKS, 0, NB))
                    dve.tensor_tensor(RBK[d][:, h, :].rearrange("p (b f) -> p b f", b=NB), bank(u % BANKS, T, NB),
                                      wide(m[d]["incl_T"], NB), ALU.mult).then_inc(k.dve_done.sem, 1)
                dve.wait_ge(k.dve_done.sem, k.dve_done.at(4 * d + 3))
                dve.tensor_tensor(TM[d], wide(k.ident2, 2 * NB), TM[d], ALU.subtract)

        @block.gpsimd
        def _(pool):
            chain = Chain(pool, k.pool_chain)
            for d in DIRS:
                pool.wait_ge(k.dve_done.sem, k.dve_done.at(4 * d + 4))
                chain(pool.tensor_tensor(off[d][1], MT[d], wide(m[d]["level1_T"], 2 * NB), ALU.mult))
    k.tile_done.passed(14)
    k.act_done.passed(6)
    k.dve_done.passed(8)

    def turned(s):
        return flat(s).rearrange("p (i q f) -> p i q f", q=2, f=HD)

    def two_banks(i):
        return k.ps[:, i:i + 2, 0:NB * HD].rearrange("p b (i f) -> p i b f", f=HD)

    last = LEVELS - 1
    with k.block() as block:
        @block.gpsimd
        def _(pool):
            for l in range(2, LEVELS):
                for d in DIRS:
                    if l > 2:
                        pool.wait_ge(k.tile_done.sem, k.tile_done.at(6 * (l - 3) + 2 * d + 1))
                    pool.tensor_tensor(off[d][l % 2], MT[d], wide(m[d][f"level{l}_T"], 2 * NB), ALU.mult).then_inc(
                        k.pool_done.sem, 1)

        @block.tensor
        def _(pe):
            for l in range(1, LEVELS):
                for d in DIRS:
                    if l > 1:
                        pe.wait_ge(k.pool_done.sem, k.pool_done.at(2 * (l - 2) + d + 1))
                        pe.wait_ge(k.dve_done.sem, k.dve_done.at(4 * (l - 2) + 3 + d))
                    for hb in range(2 * NB):
                        for q in range(2):
                            mm = pe.matmul(k.ps[rows(hb % 2), 2 * d + q, ch(hb // 2)], off[d][l % 2][rows(q), hb, :],
                                           TM[d][rows(q), hb, :], start=True, stop=True)
                    mm.then_inc(k.tile_done.sem, 1)
                    for i in range(NB):
                        mm = pe.transpose(k.ps[:, 4 + 2 * d, bl(i)], flat(TM[d][:, 2 * i:2 * i + 2, :]), k.ident[:, :])
                    mm.then_inc(k.tile_done.sem, 1)
                for d in DIRS:
                    pe.wait_ge(k.act_done.sem, k.act_done.at(2 * (l - 1) + d + 1))
                    pe.wait_ge(k.dve_done.sem, k.dve_done.at(4 * (l - 1) + d + 1))
                    for i in range(NB):
                        for q in range(2):
                            for e in range(2):
                                mm = pe.matmul(k.ps[rows(q), 4 + 2 * d + e, ch(i)], turned(TT_[d])[rows(e), i, q, :],
                                               turned(Q[d])[rows(e), i, q, :], start=True, stop=True)
                    mm.then_inc(k.tile_done.sem, 1)

        @block.scalar
        def _(act):
            for l in range(1, LEVELS):
                for d in DIRS:
                    act.wait_ge(k.tile_done.sem, k.tile_done.at(6 * (l - 1) + 2 * d + 1))
                    act.activation(turned(Q[d]), two_banks(2 * d), ACT.Copy).then_inc(k.act_done.sem, 1)

        @block.vector
        def _(dve):
            for l in range(1, LEVELS):
                for d in DIRS:
                    dve.wait_ge(k.tile_done.sem, k.tile_done.at(6 * (l - 1) + 2 * d + 2))
                    dve.tensor_copy(flat(TT_[d]), k.ps[:, 4 + 2 * d, :]).then_inc(k.dve_done.sem, 1)
                for d in DIRS:
                    dve.wait_ge(k.tile_done.sem, k.tile_done.at(6 * (l - 1) + d + 5))
                    dve.tensor_tensor(turned(TM[d]), turned(TM[d]), two_banks(4 + 2 * d), ALU.subtract).then_inc(
                        k.dve_done.sem, 1)
    k.pool_done.passed(2 * (LEVELS - 2))
    k.tile_done.passed(6 * last)
    k.act_done.passed(2 * last)
    k.dve_done.passed(4 * last)

    with k.block() as block:
        @block.tensor
        def _(pe):
            for d in DIRS:
                for hb in range(2 * NB):
                    h, b = hb // NB, hb % NB
                    for q in range(2):
                        if b < TT:
                            pe.matmul(k.ps[rows(q), 4 * d + 1, ch(2 * h + b)], TM[d][rows(q), hb, :],
                                      RBK[d][rows(q), h, ch(b)], start=True, stop=True)
                        mm = pe.matmul(k.ps[rows(q), 4 * d, ch(hb)], TM[d][rows(q), hb, :], Bt[d][rows(q), b, rows(h)],
                                       start=True, stop=True)
                mm.then_inc(k.tile_done.sem, 1)
            for d in DIRS:
                pe.wait_ge(k.act_done.sem, k.act_done.at(d + 1))
                for hb in range(2 * NB):
                    h, b = hb // NB, hb % NB
                    for q in range(2):
                        if b < TT:
                            pe.matmul(k.ps[rows(q), 4 * d + 3, ch(2 * h + b)], N[d][rows(q), hb, :],
                                      Z[d][rows(q), 2 * h + b, :], start=True, stop=True)
                        mm = pe.matmul(k.ps[rows(q), 4 * d + 2, ch(hb)], N[d][rows(q), hb, :], E[d][rows(q), hb, :],
                                       start=True, stop=True)
                mm.then_inc(k.tile_done.sem, 1)

        @block.scalar
        def _(act):
            for d in DIRS:
                act.wait_ge(k.tile_done.sem, k.tile_done.at(d + 1))
                act.activation(E[d], bank(4 * d, 0, 2 * NB), ACT.Copy)
                act.activation(Z[d], bank(4 * d + 1, 0, 2 * TT), ACT.Copy).then_inc(k.act_done.sem, 1)

        @block.vector
        def _(dve):
            for d in DIRS:
                dve.memset(state[d][:, 0, :], 0.0)
            for d in DIRS:
                dve.wait_ge(k.tile_done.sem, k.tile_done.at(3 + d))
                kt = Kt[d].rearrange("p b (h f) -> p h b f", h=2)
                dve.tensor_tensor(kt, kt, k.ps[:, 4 * d + 2, :].rearrange("p (h b f) -> p h b f", h=2, b=NB), ALU.subtract)
                rk = RBK[d][:, :, P:2 * P]
                dve.tensor_tensor(rk, rk, k.ps[:, 4 * d + 3, 0:2 * P].rearrange("p (h f) -> p h f", h=2), ALU.subtract)
    k.tile_done.passed(4)
    k.act_done.passed(2)

    with k.block() as block:
        @block.tensor
        def _(pe):
            for d in DIRS:
                for b in range(NB):
                    for h, q in HQ:
                        if b < TT:
                            pe.matmul(k.ps[rows(h), 4 * d + 2 + q, ch(b)], At[d][rows(q), b, rows(h)],
                                      Z[d][rows(q), 2 * h + b, :], start=True, stop=True)
                        pe.matmul(k.ps[rows(h), 4 * d + q, ch(b)], At[d][rows(q), b, rows(h)],
                                  E[d][rows(q), NB * h + b, :], start=True, stop=True)
                        mm = pe.matmul(k.ps[rows(h), 4 * d + q, ch(NB + b)], Kt[d][rows(q), b, rows(h)],
                                       vt[rows(q), b, rows(h)], start=True, stop=True)
                mm.then_inc(k.tile_done.sem, 1)

        @block.vector
        def _(dve):
            for d in DIRS:
                dve.wait_ge(k.tile_done.sem, k.tile_done.at(1 + d))
                for q in range(2):
                    dve.tensor_tensor(step[d][:, q:NC2:2, :], wide(k.ident2, NB), bank(4 * d + q, 0, NB), ALU.subtract)
                    dve.tensor_tensor(inp[d][:, q:NC2:2, :], bank(4 * d + q, T, NB),
                                      gend[d][:, q:NC2:2].rearrange("p (c o) -> p c o", o=1).broadcast_to([P, NB, HD]),
                                      ALU.mult)
                    rq = AR[d][:, 1, 0:T].rearrange("p (b q f) -> p b q f", b=TT, q=2)[:, :, q, :]
                    oq = r2[d].rearrange("p (b q f) -> p b q f", b=TT, q=2)[:, :, q, :]
                    dve.tensor_tensor(oq, rq, bank(4 * d + 2 + q, 0, TT), ALU.subtract)
    k.tile_done.passed(2)

    orders = [[4, 5, 6, 7, 0, 1, 2, 3], [7, 6, 5, 4, 3, 2, 1, 0]]
    with k.block() as block:
        @block.tensor
        def _(pe):
            for i in range(NC2):
                for d in DIRS:
                    c = orders[d][i]
                    if i:
                        pe.wait_ge(k.dve_done.sem, k.dve_done.at(2 * (i - 1) + d + 1))
                    if i < NC2 - 1:
                        for h in range(2):
                            mm = pe.matmul(k.ps[rows(h), d, 0:HD], step[d][rows(h), c, :], state[d][rows(h), i, :],
                                           start=True, stop=True)
                        mm.then_inc(k.tile_done.sem, 1)
                    if c < NC2 // 2:
                        for h in range(2):
                            mm = pe.matmul(k.ps[rows(h), 2 + d, ch(c)], state[d][rows(h), i, :], r2[d][rows(h), ch(c)],
                                      start=True, stop=True)
                if i == 0:
                    pe.matmul(k.ps[:, 6, 0:T], k.head_ones[:, :], coef, start=True, stop=True)
                if i < TT:
                    b = i
                    for h, q in HQ:
                        for d in DIRS:
                            pe.matmul(k.ps[rows(h), 4 + q, ch(b)], vt[rows(q), b, rows(h)],
                                      RBK[d][rows(q), h, P + b * HD:P + (b + 1) * HD], start=(d == 0), stop=(d == 1))
            mm.then_inc(k.tile_done.sem, 1)

        @block.vector
        def _(dve):
            chain = Chain(dve, k.dve_chain)
            for i in range(NC2 - 1):
                for d in DIRS:
                    c = orders[d][i]
                    dve.wait_ge(k.tile_done.sem, k.tile_done.at(2 * i + d + 1))
                    dve.scalar_tensor_tensor(out=state[d][:, i + 1, :], in0=k.ps[:, d, 0:HD], scalar=gend[d][:, c:c + 1],
                                             in1=inp[d][:, c, :], op0=ALU.mult, op1=ALU.add).then_inc(k.dve_done.sem, 1)
            dve.wait_ge(k.tile_done.sem, k.tile_done.at(2 * NC2 - 1))
            dve.tensor_tensor(r[:, 0:T], k.ps[:, 6, 0:T], v[:, 0:T], ALU.mult)
            chain(dve.tensor_copy(y, k.ps[:, 2, 0:T]))
            chain(dve.tensor_tensor(y, y, k.ps[:, 3, 0:T], ALU.add))
            for q in range(2):
                yq = y.rearrange("p (b q f) -> p b q f", b=TT, q=2)[:, :, q, :]
                dve.tensor_tensor(yq, yq, bank(4 + q, 0, TT), ALU.add)
    k.tile_done.passed(2 * NC2 - 1)
    k.dve_done.passed(2 * NC2 - 2)


def flat(s):
    return s.rearrange("p a b -> p (a b)")


def scan_outputs(k, z, y, at):
    sqr, end = k.carve(at, RC, T)
    rs, end = k.carve(end, T)
    rs = rs[0:2 * RC, :]
    with k.block() as block:
        @block.tensor
        def _(pe):
            for p in range(RC):
                pe.matmul(k.ps[:, p, 0:T], k.head_ones[:, :], y[:, p, :], start=True, stop=True).then_inc(k.tile_done.sem, 1)
            for p in range(RC):
                pe.wait_ge(k.dve_done.sem, k.dve_done.at(p + 1))
                mm = pe.matmul(k.ps[0:2 * RC, 6, 0:T], k.pick[:, p, :], sqr[:, p, :], start=(p == 0), stop=(p == RC - 1))
            mm.then_inc(k.tile_done.sem, 1)
            pe.wait_ge(k.act_done.sem, k.act_done.at(1))
            for p in range(RC):
                pe.matmul(k.ps[:, p, 0:T], k.spread[p], rs, start=True, stop=True).then_inc(k.tile_done.sem, 1)

        @block.vector
        def _(dve):
            chain = Chain(dve, k.dve_chain)
            for p in range(RC):
                dve.wait_ge(k.tile_done.sem, k.tile_done.at(p + 1))
                chain(dve.scalar_tensor_tensor(out=y[:, p, :], in0=k.ps[:, p, 0:T], scalar=-1.0 / HD, in1=y[:, p, :],
                                               op0=ALU.mult, op1=ALU.add))
                dve.tensor_tensor(sqr[:, p, :], y[:, p, :], y[:, p, :], ALU.mult).then_inc(k.dve_done.sem, 1)
            dve.wait_ge(k.tile_done.sem, k.tile_done.at(RC + 1))
            chain(dve.tensor_scalar(rs, k.ps[0:2 * RC, 6, 0:T], 1.0 / HD, GN_EPS, ALU.mult, ALU.add))
            dve.reciprocal(rs, rs).then_inc(k.dve_done.sem, 1)
            for p in range(RC):
                dve.wait_ge(k.tile_done.sem, k.tile_done.at(RC + 2 + p))
                yp = y[:, p, :]
                chain(dve.scalar_tensor_tensor(out=yp, in0=k.ps[:, p, 0:T], scalar=column(k, "e_gn_w_2", p), in1=yp,
                                               op0=ALU.mult, op1=ALU.mult))
                chain(dve.scalar_tensor_tensor(out=yp, in0=yp, scalar=column(k, "e_gn_b_2", p), in1=z[:, R0 + p, 0:T],
                                               op0=ALU.add, op1=ALU.add))
                dve.tensor_tensor(yp, yp, k.gate[p], ALU.mult)

        @block.scalar
        def _(act):
            act.wait_ge(k.dve_done.sem, k.dve_done.at(RC + 1))
            act.activation(rs, rs, ACT.Sqrt).then_inc(k.act_done.sem, 1)
    k.tile_done.passed(2 * RC + 1)
    k.dve_done.passed(RC + 1)
    k.act_done.passed(1)


def even_mixer(k):
    n = 2 * T
    z, end = k.carve(0, MIX_E, n)
    tmp, end = k.carve(end, 2, n)
    cs, end = k.carve(end, 2 * P)
    cn, end = k.carve(end, 2 * TT, T)
    masks = [k.x[:, b // 4, T + b % 4 * HD:T + (b % 4 + 1) * HD] for b in range(2 * (LEVELS + 2))]
    k.spread = [k.x[0:2 * RC, 4 + c // 2, T + c % 2 * P:T + (c % 2 + 1) * P] for c in range(RC)]
    jobs = [(cs, k.con["dft_channels"]), (cn, k.con["dft_tokens"].rearrange("(a p) t -> p a t", p=P))]
    jobs += [(m, k.con["scan_masks"][:, HD * j:HD * (j + 1)]) for j, m in enumerate(masks)]
    jobs += [(k.spread[c], k.con["spread"][:, P * c:P * (c + 1)]) for c in range(RC)]

    def width(m):
        return n if K0 <= m <= WA else T

    def shift(m):
        return lambda dve, chain: token_shift(k, dve, chain, z, m, tmp, width(m) // T)

    gemm(k, column_groups(MIX_E * P), lambda kt: k.h[:, kt, :], n,
         act=lambda eng, chain, m, ps: eng.activation(z[:, m, 0:width(m)], ps, ACT.Copy),
         aside={m: shift(m) for m in range(FO)}, loads=jobs, width=width)
    y = k.h[:, :, 0:T]
    k.up_w = [k.h[:, b // 2, T + b % 2 * P:T + (b % 2 + 1) * P] for b in range(2 * RC)]
    jobs, i = [], k.inp
    for d in range(2):
        for p in range(RC):
            jobs.append((k.up_w[d * RC + p][0:HD, :], i["e_w_up_2"][0, d, :, p * P:(p + 1) * P]))
            jobs.append((k.up_w[d * RC + p][HD:P, :], i["e_a_up_2"][0, d, :, p * P:(p + 1) * P]))
    fourier(k, z[:, FO:FO + 2, 0:T], y[:, RC:RC + 2, :], cs, cn, end, jobs)
    k.gate = [z[:, R0 + c, T:2 * T] for c in range(RC)]
    end = FO * n
    k.ident2, end = k.carve(end, HD)
    k.chunk_start, end = k.carve(end, n)
    k.rnorm = z[0:2 * RC, GD, :]
    k.pick, end = k.carve(end, RC, 2 * RC)
    k.free = end
    g_up, _ = k.carve(end, D_RWKV)
    jobs = [(k.ident2, k.con["ident2"]),
            (k.chunk_start, k.con["chunk_start"]), (k.pick, k.con["pick"].rearrange("p (a b) -> p a b", a=RC)),
 (g_up, i["e_g_up_2"][0])]
    load_constants(k, jobs)
    fwd, bwd = {}, {}
    fwd["strict"], bwd["strict"] = masks[0], masks[1]
    fwd["incl_T"], bwd["incl_T"] = masks[2], masks[3]
    for l in range(LEVELS):
        a, b = masks[4 + 2 * l], masks[5 + 2 * l]
        fwd[f"level{l}"], fwd[f"level{l}_T"] = a, b
        bwd[f"level{l}"], bwd[f"level{l}_T"] = b, a
    k.masks = [fwd, bwd]
    with k.block() as block:
        @block.scalar
        def _(act):
            act.activation(z[0:HD, WA, :], z[0:HD, WA, :], ACT.Tanh)
            act.activation(z[:, GD, 0:T], z[:, GD, 0:T], ACT.Sigmoid).then_inc(k.act_done.sem, 1)
            for c in range(RC):
                act.wait_ge(k.tile_done.sem, k.tile_done.at(c + 1))
                act.activation(k.gate[c], k.ps[:, c, 0:T], ACT.Copy)

        @block.tensor
        def _(pe):
            pe.wait_ge(k.act_done.sem, k.act_done.at(1))
            for c in range(RC):
                pe.matmul(k.ps[:, c, 0:T], g_up[:, c * P:(c + 1) * P], z[:, GD, 0:T], start=True, stop=True).then_inc(
                    k.tile_done.sem, 1)
    k.act_done.passed(1)
    k.tile_done.passed(RC)
    head_norms(k, z)
    for p in range(RC):
        scan_tile(k, p, z, y[:, p, :], k.free)
    scan_outputs(k, z, y[:, 0:RC, :], k.free)
    gemm(k, column_groups(D), lambda kt: y[:, kt, :], T,
         dve=add_to_x(k, T, lambda m: [(k.mod[:, 5 * DC + m, 0:1], (0, T))]))


def odd_mixer(k):
    z, end = k.carve(0, 14, T)
    pad = CONV_WIDTH // 2
    u, end = k.carve(end, RC, T + 2 * pad)
    c, end = k.carve(end, RC, T)
    cn, end = k.carve(end, RC, T)
    pool, end = k.carve(end, 4 * TT, T)
    pw, end = k.carve(end, 2, P)
    mid, end = k.carve(end, 2 * TT, P)
    y = k.h[:, :, 0:T]

    def place(m):
        if m >= 2 * RC:
            return m
        return m // 4 * 2 + m % 2 + (RC if m % 4 >= 2 else 0)

    def zeros(dve, chain):
        dve.memset(pw, 0.0).then_inc(k.dve_done.sem, 1)
        chain(dve.memset(u, 0.0))

    def convolve(f0, tiles):
        def run(dve, chain):
            for f in range(f0, f0 + tiles):
                ins = dve.tensor_tensor(u[:, f, pad:pad + T], z[:, f, :], z[:, RC + f, :], ALU.mult)
            chain(ins)
            for w in range(CONV_WIDTH):
                for f in range(f0, f0 + tiles):
                    src, tap = u[:, f, w:w + T], k.conv_w[:, f, w:w + 1]
                    if w == 0:
                        ins = dve.tensor_scalar(c[:, f, :], src, tap, column(k, "o_conv_b_2", f), ALU.mult, ALU.add)
                    else:
                        ins = dve.scalar_tensor_tensor(out=c[:, f, :], in0=src, scalar=tap, in1=c[:, f, :],
                                                       op0=ALU.mult, op1=ALU.add)
                chain(ins)
        return run

    jobs = [(pool, k.con["pool"].rearrange("(a p) t -> p a t", p=P))]
    late = []
    for g in range(4):
        r = (g % 2) * HD
        late.append((pw[r:r + HD, g // 2, r:r + HD], k.inp["o_pool_w_2"][0, g]))
    gemm(k, column_groups(14 * P), lambda kt: k.h[:, kt, 0:T], T,
         act=lambda eng, chain, m, ps: eng.activation(z[:, place(m), :], ps,
                                                      ACT.Copy if m >= 2 * RC or m % 4 < 2 else ACT.Sigmoid),
         aside={-1: zeros, 3: convolve(0, 2), 7: convolve(2, 2)}, loads=jobs, late=late)
    k.dve_done.passed(1)
    with k.block() as block:
        @block.vector
        def _(dve):
            convolve(4, 2)(dve, Chain(dve, k.dve_chain))

        @block.tensor
        def _(pe):
            for f in range(2):
                for tt in range(TT):
                    pe.matmul(k.ps[:, 2 * f + tt, 0:P], z[:, 2 * RC + f, tt * P:(tt + 1) * P], pw[:, f, :],
                              start=True, stop=True).then_inc(k.tile_done.sem, 1)
            pe.wait_ge(k.act_done.sem, k.act_done.at(4))
            for g in range(4):
                r = (g % 2) * HD
                for tt in range(TT):
                    mm = pe.matmul(k.ps[r:r + HD, 4 + g // 2, 0:T], mid[:, g // 2 * TT + tt, r:r + HD],
                                   pool[:, g * TT + tt, :], start=(tt == 0), stop=(tt == TT - 1))
            mm.then_inc(k.tile_done.sem, 1)

        @block.scalar
        def _(act):
            for q in range(4):
                act.wait_ge(k.tile_done.sem, k.tile_done.at(q + 1))
                act.activation(mid[:, q, :], k.ps[:, q, 0:P], ACT.Copy).then_inc(k.act_done.sem, 1)
            act.wait_ge(k.tile_done.sem, k.tile_done.at(5))
            for f in range(2):
                act.activation(y[:, RC + f, :], k.ps[:, 4 + f, 0:T], ACT.Copy, scale=column(k, "o_pool_scale_2", f))
    k.tile_done.passed(5)
    k.act_done.passed(4)
    rmsnorm(k, c, cn, RC, T, lambda f: [(column(k, "o_cnorm_g_2", f), (0, T))])
    with k.block() as block:
        @block.scalar
        def _(act):
            for f in range(RC):
                act.activation(c[:, f, :], cn[:, f, :], ACT.Sigmoid).then_inc(k.act_done.sem, 1)

        @block.vector
        def _(dve):
            for f in range(RC):
                dve.wait_ge(k.act_done.sem, k.act_done.at(f + 1))
                dve.tensor_tensor(y[:, f, :], c[:, f, :], cn[:, f, :], ALU.mult)
    k.act_done.passed(RC)
    gemm(k, column_groups(D), lambda kt: y[:, kt, :], T,
         dve=add_to_x(k, T, lambda m: [(k.mod[:, 5 * DC + m, 0:1], (0, T))]))


def second_block(k):
    for i in range(DEPTH):
        both = i == 0
        modulation(k, i, both)
        half_ffn(k, 0, 0)
        if both:
            half_ffn(k, 0, 1)
        modulate(k, 1, 2 * T if both else T)
        if i == 0:
            even_mixer(k)
        else:
            odd_mixer(k)
        half_ffn(k, 2, 0)
    rmsnorm(k, k.x, k.h, DC, T, lambda c: [(column(k, "final_g_2", c), (0, T))])


def more_constants(c):
    import numpy as np
    i = np.arange(P)
    ch, t = np.arange(HD), np.arange(T)
    ang = 2 * np.pi * np.outer(ch, ch) / HD
    both = np.eye(2)
    c["dft_channels"] = np.concatenate([np.kron(both, np.cos(ang)), np.kron(both, -np.sin(ang))], axis=1)
    ang = 2 * np.pi * (np.outer(t, t) % T) / T
    norm = 1.0 / np.sqrt(T * HD)
    c["dft_tokens"] = np.concatenate([np.cos(ang), np.sin(ang)], axis=0) * norm
    i = np.arange(CHUNK)
    lower = i[:, None] > i[None, :]
    incl = lower | np.eye(CHUNK, dtype=bool)
    masks = [lower, lower.T, incl.T, incl]
    for l in range(LEVELS):
        w = 1 << l
        level = ((i[:, None] // (2 * w)) == (i[None, :] // (2 * w))) & ((i[:, None] // w) % 2 == 1) & ((i[None, :] // w) % 2 == 0)
        masks += [level, level.T]
    c["scan_masks"] = np.tile(np.concatenate(masks, axis=1), (2, 1))
    heads = np.arange(P) // HD
    pick = np.zeros((P, RC, 2 * RC))
    for f in range(RC):
        pick[np.arange(P), f, 2 * f + heads] = 1
    c["pick"] = pick.reshape(P, RC * 2 * RC)
    c["spread"] = pick.transpose(2, 1, 0).reshape(2 * RC, RC * P)
    c["ident2"] = np.concatenate([np.eye(HD), np.eye(HD)], axis=0)
    c["chunk_start"] = np.broadcast_to((np.arange(2 * T) % CHUNK != 0)[None, :], (P, 2 * T))
    pools = []
    for w in (2, 4, 8, 16):
        lo = np.maximum(t - w // 2, 0)
        hi = np.minimum(t + (w - 1 - w // 2), T - 1)
        inside = (t[:, None] >= lo[None, :]) & (t[:, None] <= hi[None, :])
        pools.append(inside / (hi - lo + 1)[None, :] - np.eye(T))
    c["pool"] = np.concatenate(pools, axis=0)


def store_output(k, src):
    tok, _ = k.carve(WORK - TT * D, TT, D)
    with k.block() as block:
        @block.tensor
        def _(pe):
            for c in range(DC):
                for tt in range(TT):
                    mm = pe.transpose(k.ps[:, c, tt * P:(tt + 1) * P], src[:, c, tt * P:(tt + 1) * P], k.ident[:, :])
                mm.then_inc(k.tile_done.sem, 1)

        @block.vector
        def _(dve):
            for c in range(DC):
                dve.wait_ge(k.tile_done.sem, k.tile_done.at(c + 1))
                ins = dve.tensor_copy(tok[:, :, c * P:(c + 1) * P], k.ps[:, c, 0:T].rearrange("p (t f) -> p t f", t=TT))
            ins.then_inc(k.dve_done.sem, 1)

        @block.sync
        def _(sp):
            sp.wait_ge(k.dve_done.sem, k.dve_done.at(1))
            sp.dma_start(k.out[0].rearrange("(t p) d -> p t d", p=P), tok).then_inc(k.stored.sem, 16)
            sp.wait_ge(k.stored.sem, 16)


def program(nc, inputs, consts, out):
    with ExitStack() as ctx:
        k = Core(nc, ctx, inputs, consts)
        k.out = out
        for l in range(DEPTH):
            plan_first(k, l)
        if not STOP:
            for i in range(DEPTH):
                plan_second(k, i)
        load_params(k)
        for l in range(DEPTH):
            first_layer(k, l)
        if not STOP:
            second_block(k)
            final = k.h
        else:
            final = k.x
        store_output(k, final)
        k.work_ctx.close()


def constants():
    import numpy as np
    f = np.float32
    i = np.arange(P)
    same = (i[:, None] // HD) == (i[None, :] // HD)
    c = {"ident": np.eye(P), "ones": np.ones((P, P)), "head_ones": same}
    q = np.arange(T).reshape(TT, P).T[:, :, None]
    key = np.arange(T)[None, None, :]
    c["mask_a"] = np.where(key // CHUNK <= q // CHUNK, 0.0, FAR)
    strict = i[:, None] < i[None, :]
    c["mask_strict"] = strict
    diag = np.where(strict, 0.0, FAR)
    c["mask_b"] = np.concatenate([diag, np.zeros((P, P)), diag], axis=1)
    c["neg_tri"] = -(i[:, None] >= i[None, :]).astype(f)
    c["neg_ones"] = -np.ones((P, P))
    c["onehot"] = np.broadcast_to((np.arange(4 * SIDE) == 2 * SIDE)[None, :], (P, 4 * SIDE))
    half = HD // 2
    inv = (f(10000.0) ** (-np.arange(0, HD, 2, dtype=f) / f(HD))).astype(f)
    c["inv_freq"] = np.broadcast_to(inv[None, :], (P, half))
    if not STOP:
        more_constants(c)
    return {n: np.ascontiguousarray(a, dtype=f) for n, a in c.items()}


NAMES = (
    "x p positions attn_norm w_in a_q_norm a_k_norm a_lambda a_subln c_q_norm c_k_norm idx_k_norm w_br_a w_br_b "
    "w_br_c w_out mlp_norm w_up w_down ple_norm w_ple_gate w_ple_proj c_2 ctx_2 c_ctx_2 ada_w_2 ada_b_2 norm_g_2 "
    "ffn1_w_gu_2 ffn1_w_down_2 ffn2_w_gu_2 ffn2_w_down_2 e_w_in_2 e_mu_2 e_w0_2 e_w_up_2 e_a0_2 e_a_up_2 e_g_up_2 "
    "e_k_k_2 e_k_a_2 e_r_k_2 e_gn_w_2 e_gn_b_2 e_w_out_2 o_w_in_2 o_conv_w_2 o_conv_b_2 o_cnorm_g_2 o_pool_w_2 "
    "o_pool_scale_2 o_w_out_2 final_g_2").split()


def kernel(**inputs):
    import numpy as np
    import concourse.bacc as bacc
    from concourse.bass_utils import run_bass_kernel_spmd

    nc = bacc.Bacc("TRN2", target_bir_lowering=False, num_devices=1)
    arrays, aps, consts = {}, {}, {}
    for name in NAMES:
        a = np.ascontiguousarray(inputs[name])
        arrays["in_" + name] = a
        aps[name] = nc.dram_tensor("in_" + name, a.shape, mybir.dt.from_np(a.dtype), kind="ExternalInput").ap()
    for name, a in constants().items():
        arrays["const_" + name] = a
        consts[name] = nc.dram_tensor("const_" + name, a.shape, F32, kind="ExternalInput").ap()
    out = nc.dram_tensor("out_0", (1, T, D), F32, kind="ExternalOutput").ap()
    program(nc, aps, consts, out)
    return run_bass_kernel_spmd(nc, [arrays], core_ids=[0]).results[0]["out_0"]
```
